# Optimizing a Trainium2 kernel written in Bass

```python
import jax
import jax.numpy as jnp
from jax import lax
import numpy as np
import jax, jax.numpy as jnp

D_MODEL = 1024
BATCH = 1
SEQ = 512
DEPTH = 2

HEAD_DIM = 64
N_HEADS = 8
N_KV = 2
HPG = N_HEADS // N_KV
ATTN_W = N_HEADS * HEAD_DIM
KV_W = N_KV * HEAD_DIM
CONV_CH = D_MODEL - ATTN_W
CONV_W = 3
D_MIX = ATTN_W + CONV_CH
CMP_BLOCK = 32
CMP_STRIDE = 16
CMP_HIDDEN = 256
SEL_BLOCK = 64
SEL_TOPN = 16
WINDOW = 512
WIN_QBLOCK = 128
SEL_QCHUNK = 64
D_FF = 2816
N_EXPERTS = 8
TOP_K = 2
D_FF_EXPERT = 1408
N_DENSE = (DEPTH + 1) // 2
N_MOE = DEPTH // 2
ALPHA = (2 * DEPTH) ** 0.25
BETA = (8 * DEPTH) ** -0.25
LN_EPS = 1e-5
NEG = -1e30
FORCE = 1e9
SPLIT_WIDTHS = (ATTN_W, KV_W, KV_W, KV_W, KV_W, KV_W, KV_W, 3 * N_HEADS, CONV_CH, CONV_CH, CONV_CH)
D_IN = sum(SPLIT_WIDTHS)


def layer_norm(x, g, b):
    xf = x.astype(jnp.float32)
    mu = jnp.mean(xf, -1, keepdims=True)
    var = jnp.mean(jnp.square(xf - mu), -1, keepdims=True)
    return ((xf - mu) * lax.rsqrt(var + LN_EPS) * g + b).astype(x.dtype)

def compress(k, pos, w1, b1, w2, b2):
    bsz, g, s, dh = k.shape
    ratio = CMP_BLOCK // CMP_STRIDE
    n_cmp = s // CMP_STRIDE - ratio + 1
    blocks = k.reshape(bsz, g, s // CMP_STRIDE, CMP_STRIDE, dh)
    win = jnp.concatenate([blocks[:, :, r:r + n_cmp] for r in range(ratio)], axis=3)
    win = (win + pos).reshape(bsz, g, n_cmp, CMP_BLOCK * dh)
    return jax.nn.gelu(win @ w1 + b1) @ w2 + b2

def cmp_attention(q, kc, vc):
    s_len = q.shape[3]
    n = kc.shape[2]
    t = jnp.arange(s_len)
    ends = jnp.arange(n) * CMP_STRIDE + CMP_BLOCK - 1
    mask = ends[None, :] <= t[:, None]
    sc = jnp.einsum('bghsd,bgnd->bghsn', q, kc).astype(jnp.float32) * HEAD_DIM ** -0.5
    p = jax.nn.softmax(jnp.where(mask, sc, NEG), axis=-1) * mask
    o = jnp.einsum('bghsn,bgnd->bghsd', p.astype(vc.dtype), vc)
    return o, p

def select_blocks(p_cmp, s_len):
    n = p_cmp.shape[-1]
    n_sel = s_len // SEL_BLOCK
    cs = jnp.arange(n) * CMP_STRIDE
    ss = jnp.arange(n_sel) * SEL_BLOCK
    overlap = ((cs[:, None] < ss[None, :] + SEL_BLOCK) & (cs[:, None] + CMP_BLOCK > ss[None, :])).astype(jnp.float32)
    imp = jnp.einsum('bghsn,nj->bgsj', p_cmp, overlap)
    t = jnp.arange(s_len)[:, None]
    j = jnp.arange(n_sel)[None, :]
    cur = t // SEL_BLOCK
    valid = j * SEL_BLOCK <= t
    forced = (j == 0) | (j == cur) | (j == cur - 1)
    score = jnp.where(forced, FORCE, jnp.where(valid, imp, NEG))
    _, idx = lax.top_k(score, min(SEL_TOPN, n_sel))
    return idx

def sel_attention(q, ks, vs, idx):
    bsz, g, hpg, s_len, dh = q.shape
    n_sel = s_len // SEL_BLOCK
    k_top = idx.shape[-1]
    nc = s_len // SEL_QCHUNK
    kb = ks.reshape(bsz, g, n_sel, SEL_BLOCK, dh)
    vb = vs.reshape(bsz, g, n_sel, SEL_BLOCK, dh)
    qc = q.reshape(bsz, g, hpg, nc, SEL_QCHUNK, dh).transpose(3, 0, 1, 2, 4, 5)
    ic = idx.reshape(bsz, g, nc, SEL_QCHUNK, k_top).transpose(2, 0, 1, 3, 4)
    starts = jnp.arange(nc) * SEL_QCHUNK
    gather = jax.vmap(jax.vmap(lambda blk, ix: blk[ix]))

    def chunk(args):
        qq, ii, start = args
        kg = gather(kb, ii)
        vg = gather(vb, ii)
        sc = jnp.einsum('bghqd,bgqkrd->bghqkr', qq, kg).astype(jnp.float32) * HEAD_DIM ** -0.5
        pos = ii[..., None] * SEL_BLOCK + jnp.arange(SEL_BLOCK)
        tq = start + jnp.arange(SEL_QCHUNK)
        mask = (pos <= tq[None, None, :, None, None])[:, :, None]
        sc = jnp.where(mask, sc, NEG).reshape(bsz, g, hpg, SEL_QCHUNK, k_top * SEL_BLOCK)
        p = jax.nn.softmax(sc, axis=-1).reshape(bsz, g, hpg, SEL_QCHUNK, k_top, SEL_BLOCK)
        return jnp.einsum('bghqkr,bgqkrd->bghqd', p.astype(vg.dtype), vg)

    o = lax.map(chunk, (qc, ic, starts))
    return o.transpose(1, 2, 3, 0, 4, 5).reshape(bsz, g, hpg, s_len, dh)

def win_attention(q, kw, vw):
    bsz, g, hpg, s_len, dh = q.shape
    nb = s_len // WIN_QBLOCK
    span = WINDOW // WIN_QBLOCK
    ksz = (span + 1) * WIN_QBLOCK
    padw = ((0, 0), (0, 0), (WINDOW, 0), (0, 0))
    kp = jnp.pad(kw, padw).reshape(bsz, g, nb + span, WIN_QBLOCK, dh)
    vp = jnp.pad(vw, padw).reshape(bsz, g, nb + span, WIN_QBLOCK, dh)
    kband = jnp.concatenate([kp[:, :, i:i + nb] for i in range(span + 1)], axis=3)
    vband = jnp.concatenate([vp[:, :, i:i + nb] for i in range(span + 1)], axis=3)
    qb = q.reshape(bsz, g, hpg, nb, WIN_QBLOCK, dh)
    sc = jnp.einsum('bghnqd,bgnkd->bghnqk', qb, kband).astype(jnp.float32) * HEAD_DIM ** -0.5
    blk = jnp.arange(nb)[:, None, None] * WIN_QBLOCK
    tq = blk + jnp.arange(WIN_QBLOCK)[None, :, None]
    sk = blk - WINDOW + jnp.arange(ksz)[None, None, :]
    mask = (sk <= tq) & (tq - sk < WINDOW) & (sk >= 0)
    p = jax.nn.softmax(jnp.where(mask, sc, NEG), axis=-1)
    o = jnp.einsum('bghnqk,bgnkd->bghnqd', p.astype(vband.dtype), vband)
    return o.reshape(bsz, g, hpg, s_len, dh)

def short_conv(u, b_gate, c_gate, w):
    s_len = u.shape[1]
    z = jnp.pad(c_gate * u, ((0, 0), (CONV_W - 1, 0), (0, 0)))
    y = z[:, 0:s_len] * w[0]
    for i in range(1, CONV_W):
        y = y + z[:, i:i + s_len] * w[i]
    return b_gate * y

def hybrid_mixer(h, w_in, cmp_pos, cmp_w1, cmp_b1, cmp_w2, cmp_b2, conv_w, w_o):
    bsz, s_len, _ = h.shape
    z = h @ w_in
    offsets = np.cumsum(SPLIT_WIDTHS)[:-1].tolist()
    q, kc, vc, ks, vs, kw, vw, gates, u, bg, cg = jnp.split(z, offsets, axis=-1)
    q = q.reshape(bsz, s_len, N_KV, HPG, HEAD_DIM).transpose(0, 2, 3, 1, 4)

    def kv(t):
        return t.reshape(bsz, s_len, N_KV, HEAD_DIM).transpose(0, 2, 1, 3)

    kc_c = compress(kv(kc), cmp_pos[0], cmp_w1[0], cmp_b1[0], cmp_w2[0], cmp_b2[0])
    vc_c = compress(kv(vc), cmp_pos[1], cmp_w1[1], cmp_b1[1], cmp_w2[1], cmp_b2[1])
    o_cmp, p_cmp = cmp_attention(q, kc_c, vc_c)
    idx = select_blocks(p_cmp, s_len)
    o_sel = sel_attention(q, kv(ks), kv(vs), idx)
    o_win = win_attention(q, kv(kw), kv(vw))
    g = jax.nn.sigmoid(gates).reshape(bsz, s_len, 3, N_KV, HPG).transpose(2, 0, 3, 4, 1)[..., None]
    o_attn = g[0] * o_cmp + g[1] * o_sel + g[2] * o_win
    o_attn = o_attn.transpose(0, 3, 1, 2, 4).reshape(bsz, s_len, ATTN_W)
    o_conv = short_conv(u, bg, cg, conv_w)
    return jnp.concatenate([o_attn, o_conv], axis=-1) @ w_o

def swiglu(h, wg, wu, wd):
    return (jax.nn.silu(h @ wg) * (h @ wu)) @ wd

def moe_swiglu(h, w_router, wg, wu, wd):
    logits = (h @ w_router).astype(jnp.float32)
    top_v, top_i = lax.top_k(logits, TOP_K)
    w_top = jax.nn.softmax(top_v, axis=-1)
    gate = jnp.sum(jax.nn.one_hot(top_i, N_EXPERTS, dtype=jnp.float32) * w_top[..., None], axis=-2)
    out = jnp.zeros_like(h)
    for e in range(N_EXPERTS):
        out = out + gate[..., e:e + 1].astype(h.dtype) * swiglu(h, wg[e], wu[e], wd[e])
    return out

def first_inputs(seed: int = 0) -> dict:
    key = jax.random.key(seed)
    ks = jax.random.split(key, 24)

    def nrm(k, shape, scale):
        return jax.random.normal(k, shape, jnp.float32) * scale

    return {
        'x': nrm(ks[0], (BATCH, SEQ, D_MODEL), 1.0),
        'ln_in_g': 1.0 + nrm(ks[1], (D_MODEL,), 0.02),
        'ln_in_b': nrm(ks[2], (D_MODEL,), 0.02),
        'w_in': nrm(ks[3], (DEPTH, D_MODEL, D_IN), D_MODEL ** -0.5),
        'cmp_pos': nrm(ks[4], (DEPTH, 2, CMP_BLOCK, HEAD_DIM), 0.1),
        'cmp_w1': nrm(ks[5], (DEPTH, 2, CMP_BLOCK * HEAD_DIM, CMP_HIDDEN), (CMP_BLOCK * HEAD_DIM) ** -0.5),
        'cmp_b1': nrm(ks[6], (DEPTH, 2, CMP_HIDDEN), 0.02),
        'cmp_w2': nrm(ks[7], (DEPTH, 2, CMP_HIDDEN, HEAD_DIM), CMP_HIDDEN ** -0.5),
        'cmp_b2': nrm(ks[8], (DEPTH, 2, HEAD_DIM), 0.02),
        'conv_w': nrm(ks[9], (DEPTH, CONV_W, CONV_CH), CONV_W ** -0.5),
        'w_o': nrm(ks[10], (DEPTH, D_MIX, D_MODEL), BETA * D_MIX ** -0.5),
        'ln1_g': 1.0 + nrm(ks[11], (DEPTH, D_MODEL), 0.02),
        'ln1_b': nrm(ks[12], (DEPTH, D_MODEL), 0.02),
        'ln2_g': 1.0 + nrm(ks[13], (DEPTH, D_MODEL), 0.02),
        'ln2_b': nrm(ks[14], (DEPTH, D_MODEL), 0.02),
        'ffn_wg': nrm(ks[15], (N_DENSE, D_MODEL, D_FF), D_MODEL ** -0.5),
        'ffn_wu': nrm(ks[16], (N_DENSE, D_MODEL, D_FF), D_MODEL ** -0.5),
        'ffn_wd': nrm(ks[17], (N_DENSE, D_FF, D_MODEL), BETA * D_FF ** -0.5),
        'moe_router': nrm(ks[18], (N_MOE, D_MODEL, N_EXPERTS), D_MODEL ** -0.5),
        'moe_wg': nrm(ks[19], (N_MOE, N_EXPERTS, D_MODEL, D_FF_EXPERT), D_MODEL ** -0.5),
        'moe_wu': nrm(ks[20], (N_MOE, N_EXPERTS, D_MODEL, D_FF_EXPERT), D_MODEL ** -0.5),
        'moe_wd': nrm(ks[21], (N_MOE, N_EXPERTS, D_FF_EXPERT, D_MODEL), BETA * D_FF_EXPERT ** -0.5),
    }

def first_block(x, ln_in_g, ln_in_b, w_in, cmp_pos, cmp_w1, cmp_b1, cmp_w2, cmp_b2, conv_w, w_o,
              ln1_g, ln1_b, ln2_g, ln2_b, ffn_wg, ffn_wu, ffn_wd,
              moe_router, moe_wg, moe_wu, moe_wd):
    h = layer_norm(x, ln_in_g, ln_in_b)
    for l in range(DEPTH):
        m = hybrid_mixer(h, w_in[l], cmp_pos[l], cmp_w1[l], cmp_b1[l], cmp_w2[l], cmp_b2[l],
                         conv_w[l], w_o[l])
        h = layer_norm(ALPHA * h + m, ln1_g[l], ln1_b[l])
        if l % 2 == 0:
            f = swiglu(h, ffn_wg[l // 2], ffn_wu[l // 2], ffn_wd[l // 2])
        else:
            f = moe_swiglu(h, moe_router[l // 2], moe_wg[l // 2], moe_wu[l // 2], moe_wd[l // 2])
        h = layer_norm(ALPHA * h + f, ln2_g[l], ln2_b[l])
    return h


DEPTH_2 = 1

D_RNN = 1024
RNN_BLOCKS = 8
RNN_BLOCK_W = D_RNN // RNN_BLOCKS
CONV_W_2 = 4
LRU_C = 8.0
HEAD_DIM_2 = 128
D_ATTN = N_HEADS * HEAD_DIM_2
ROT_DIM = HEAD_DIM_2 // 4
ROPE_THETA = 500000.0
DILATED_GROUPS = ((128, 1), (512, 4), (2048, 16))
NEG_INF = -1e30
IN_WIDTHS = (D_RNN, D_RNN, D_ATTN, D_ATTN, D_ATTN, D_ATTN, D_MODEL, D_MODEL)
D_IN_2 = sum(IN_WIDTHS)
IN_SPLITS = [int(s) for s in np.cumsum(IN_WIDTHS)[:-1]]
NORM_EPS = 1e-6


def rms_norm(x, g):
    xf = x.astype(jnp.float32)
    y = xf * lax.rsqrt(jnp.mean(xf * xf, axis=-1, keepdims=True) + NORM_EPS)
    return (y * g.astype(jnp.float32)).astype(x.dtype)

def causal_depthwise_conv(x, w, b):
    y = lax.conv_general_dilated(
        x, w[:, None, :], window_strides=(1,), padding=[(CONV_W_2 - 1, 0)],
        dimension_numbers=("NWC", "WIO", "NWC"), feature_group_count=x.shape[-1])
    return y + b

def rg_lru(x, w_a, b_a, w_x, b_x, lam, positions):
    B, S, _ = x.shape
    xf = x.astype(jnp.float32)
    xh = xf.reshape(B, S, RNN_BLOCKS, RNN_BLOCK_W)
    r = jax.nn.sigmoid(jnp.einsum("bshi,hij->bshj", xh, w_a.astype(jnp.float32)) + b_a.astype(jnp.float32))
    i = jax.nn.sigmoid(jnp.einsum("bshi,hij->bshj", xh, w_x.astype(jnp.float32)) + b_x.astype(jnp.float32))
    r = r.reshape(B, S, D_RNN)
    i = i.reshape(B, S, D_RNN)
    log_a = -LRU_C * r * jax.nn.softplus(-lam.astype(jnp.float32))
    reset = (positions == 0)[..., None]
    a = jnp.where(reset, 0.0, jnp.exp(log_a))
    mult = jnp.where(reset, 1.0, jnp.sqrt(-jnp.expm1(2.0 * log_a)))
    bx = mult * i * xf

    def combine(left, right):
        a1, b1 = left
        a2, b2 = right
        return a1 * a2, a2 * b1 + b2

    _, h = lax.associative_scan(combine, (a, bx), axis=1)
    return h

def apply_partial_rope(t, cos, sin):
    tf = t.astype(jnp.float32)
    half = ROT_DIM // 2
    x1 = tf[..., :half]
    x2 = tf[..., half:ROT_DIM]
    return jnp.concatenate([x1 * cos - x2 * sin, x2 * cos + x1 * sin, tf[..., ROT_DIM:]], axis=-1)

def dilated_window_attention(q, k, v, window, dilation):
    B, S, H, Dh = q.shape
    blk = window // dilation
    span = blk * dilation
    s_pad = -(-S // span) * span
    nb = s_pad // span

    def to_blocks(t):
        t = jnp.pad(t, ((0, 0), (0, s_pad - S), (0, 0), (0, 0)))
        return t.reshape(B, nb, blk, dilation, H, Dh)

    qb, kb, vb = to_blocks(q), to_blocks(k), to_blocks(v)
    pad_prev = ((0, 0), (1, 0), (0, 0), (0, 0), (0, 0), (0, 0))
    kk = jnp.concatenate([jnp.pad(kb[:, :-1], pad_prev), kb], axis=2)
    vv = jnp.concatenate([jnp.pad(vb[:, :-1], pad_prev), vb], axis=2)
    s = jnp.einsum("bnqrhd,bnkrhd->bnrhqk", qb, kk) * (HEAD_DIM_2 ** -0.5)
    qi = jnp.arange(blk)[:, None]
    ki = jnp.arange(2 * blk)[None, :]
    dist = blk + qi - ki
    band = (dist >= 0) & (dist <= blk)
    n_idx = jnp.arange(nb)[:, None, None]
    valid = band[None] & ((n_idx > 0) | (ki[None] >= blk))
    s = jnp.where(valid[None, :, None, None], s, NEG_INF)
    lse = jax.nn.logsumexp(s, axis=-1)
    p = jnp.exp(s - lse[..., None])
    o = jnp.einsum("bnrhqk,bnkrhd->bnqrhd", p, vv)
    o = o.reshape(B, s_pad, H, Dh)[:, :S]
    lse = lse.transpose(0, 1, 4, 2, 3).reshape(B, s_pad, H)[:, :S]
    return o, lse

def dilated_attention_mixture(q, k, v):
    outs, lses = [], []
    for window, dilation in DILATED_GROUPS:
        o, l = dilated_window_attention(q, k, v, window, dilation)
        outs.append(o)
        lses.append(l)
    w = jax.nn.softmax(jnp.stack(lses, axis=0), axis=0)
    return jnp.einsum("gbsh,gbshd->bshd", w, jnp.stack(outs, axis=0))

def second_inputs(seed: int = 0) -> dict:
    key = jax.random.key(seed)
    ks = jax.random.split(key, 20)
    f32 = jnp.float32
    nrm = lambda k, shape, scale: jax.random.normal(k, shape, f32) * scale
    x = jax.random.normal(ks[0], (BATCH, SEQ, D_MODEL), f32)
    c = jax.random.normal(ks[1], (BATCH, D_MODEL), f32)
    positions = jnp.broadcast_to(jnp.arange(SEQ, dtype=jnp.int32)[None, :], (BATCH, SEQ))
    g_norm = 1.0 + nrm(ks[2], (DEPTH_2, D_MODEL), 0.02)
    w_mod = nrm(ks[3], (DEPTH_2, D_MODEL, 3 * D_MODEL), 0.5 * D_MODEL ** -0.5)
    b_mod = nrm(ks[4], (DEPTH_2, 3 * D_MODEL), 0.01)
    w_in = nrm(ks[5], (DEPTH_2, D_MODEL, D_IN_2), D_MODEL ** -0.5)
    b_gate = nrm(ks[6], (DEPTH_2, 2 * D_MODEL), 0.01)
    conv_w = nrm(ks[7], (DEPTH_2, CONV_W_2, D_RNN), CONV_W_2 ** -0.5)
    conv_b = nrm(ks[8], (DEPTH_2, D_RNN), 0.01)
    w_a = nrm(ks[9], (DEPTH_2, RNN_BLOCKS, RNN_BLOCK_W, RNN_BLOCK_W), RNN_BLOCK_W ** -0.5)
    b_a = nrm(ks[10], (DEPTH_2, RNN_BLOCKS, RNN_BLOCK_W), 0.01)
    w_x = nrm(ks[11], (DEPTH_2, RNN_BLOCKS, RNN_BLOCK_W, RNN_BLOCK_W), RNN_BLOCK_W ** -0.5)
    b_x = nrm(ks[12], (DEPTH_2, RNN_BLOCKS, RNN_BLOCK_W), 0.01)
    a0 = jax.random.uniform(ks[13], (DEPTH_2, D_RNN), f32, 0.9, 0.999)
    sig = a0 ** (1.0 / LRU_C)
    lam = jnp.log(sig) - jnp.log1p(-sig)
    w_out_rnn = nrm(ks[14], (DEPTH_2, D_RNN, D_MODEL), D_RNN ** -0.5)
    w_out_attn = nrm(ks[15], (DEPTH_2, D_ATTN, D_MODEL), D_ATTN ** -0.5)
    w_o = nrm(ks[16], (DEPTH_2, D_MODEL, D_MODEL), D_MODEL ** -0.5)
    g_final = 1.0 + nrm(ks[17], (D_MODEL,), 0.02)
    return {"x": x, "c": c, "positions": positions, "g_norm": g_norm, "w_mod": w_mod,
            "b_mod": b_mod, "w_in": w_in, "b_gate": b_gate, "conv_w": conv_w, "conv_b": conv_b,
            "w_a": w_a, "b_a": b_a, "w_x": w_x, "b_x": b_x, "lam": lam, "w_out_rnn": w_out_rnn,
            "w_out_attn": w_out_attn, "w_o": w_o, "g_final": g_final}

def second_block(x, c, positions, g_norm, w_mod, b_mod, w_in, b_gate, conv_w, conv_b,
              w_a, b_a, w_x, b_x, lam, w_out_rnn, w_out_attn, w_o, g_final):
    B, S, _ = x.shape
    dt = x.dtype
    inv_freq = ROPE_THETA ** (-jnp.arange(0, ROT_DIM, 2, dtype=jnp.float32) / ROT_DIM)
    ang = positions.astype(jnp.float32)[..., None] * inv_freq
    cos = jnp.cos(ang)[:, :, None, :]
    sin = jnp.sin(ang)[:, :, None, :]
    c_act = jax.nn.silu(c)
    for l in range(DEPTH_2):
        mod = c_act @ w_mod[l] + b_mod[l]
        shift, scale, gate = jnp.split(mod, 3, axis=-1)
        h = rms_norm(x, g_norm[l]) * (1.0 + scale[:, None, :]) + shift[:, None, :]
        proj = h @ w_in[l]
        x_rnn, z_rnn, q, k, v, z_attn, g_r, g_a = jnp.split(proj, IN_SPLITS, axis=-1)
        xc = causal_depthwise_conv(x_rnn, conv_w[l], conv_b[l])
        hr = rg_lru(xc, w_a[l], b_a[l], w_x[l], b_x[l], lam[l], positions)
        y_rnn = (hr * jax.nn.silu(z_rnn.astype(jnp.float32))).astype(dt) @ w_out_rnn[l]
        qh = apply_partial_rope(q.reshape(B, S, N_HEADS, HEAD_DIM_2), cos, sin)
        kh = apply_partial_rope(k.reshape(B, S, N_HEADS, HEAD_DIM_2), cos, sin)
        vh = v.reshape(B, S, N_HEADS, HEAD_DIM_2).astype(jnp.float32)
        o = dilated_attention_mixture(qh, kh, vh).reshape(B, S, D_ATTN)
        y_attn = (o * jax.nn.silu(z_attn.astype(jnp.float32))).astype(dt) @ w_out_attn[l]
        bg_r, bg_a = jnp.split(b_gate[l], 2, axis=-1)
        merged = jax.nn.sigmoid(g_r + bg_r) * y_rnn + jax.nn.sigmoid(g_a + bg_a) * y_attn
        x = x + gate[:, None, :] * (merged @ w_o[l])
    return rms_norm(x, g_final)


def setup_inputs(seed=0):
    out = dict(first_inputs(seed))
    for name, value in second_inputs(seed + 1).items():
        if name != "x":
            out[name + "_2"] = value
    return out


def reference(
    x, ln_in_g, ln_in_b, w_in, cmp_pos, cmp_w1, cmp_b1, cmp_w2, cmp_b2, conv_w, w_o, ln1_g,
    ln1_b, ln2_g, ln2_b, ffn_wg, ffn_wu, ffn_wd, moe_router, moe_wg, moe_wu, moe_wd, c_2,
    positions_2, g_norm_2, w_mod_2, b_mod_2, w_in_2, b_gate_2, conv_w_2, conv_b_2, w_a_2, b_a_2,
    w_x_2, b_x_2, lam_2, w_out_rnn_2, w_out_attn_2, w_o_2, g_final_2,
):
    x = first_block(
        x, ln_in_g, ln_in_b, w_in, cmp_pos, cmp_w1, cmp_b1, cmp_w2, cmp_b2, conv_w, w_o, ln1_g,
        ln1_b, ln2_g, ln2_b, ffn_wg, ffn_wu, ffn_wd, moe_router, moe_wg, moe_wu, moe_wd,
    )
    return second_block(
        x, c_2, positions_2, g_norm_2, w_mod_2, b_mod_2, w_in_2, b_gate_2, conv_w_2, conv_b_2,
        w_a_2, b_a_2, w_x_2, b_x_2, lam_2, w_out_rnn_2, w_out_attn_2, w_o_2, g_final_2,
    )


_drawn_inputs = setup_inputs


def setup_inputs(seed=0):
    import zlib

    import numpy as np

    out = dict(_drawn_inputs(seed))
    spreads = {}
    factors = {'cmp_pos': 3.45,
     'cmp_b1': 8.0,
     'cmp_b2': 7.091,
     'g_norm_2': 8.0,
     'b_mod_2': 6.474,
     'b_gate_2': 42.957,
     'conv_b_2': 8.0,
     'b_a_2': 64.0,
     'b_x_2': 64.0,
     'g_final_2': 8.01}
    for name, (base, spread) in spreads.items():
        noise = np.random.default_rng([zlib.crc32(name.encode()), seed]).standard_normal(out[name].shape)
        drawn = base * np.exp(spread * noise) if base else spread * noise
        out[name] = jnp.asarray(drawn.astype(out[name].dtype))
    for name, factor in factors.items():
        out[name] = (out[name] * factor).astype(out[name].dtype)
    return out
```

```python
from contextlib import ExitStack, contextmanager

import numpy as np

import concourse.bass as bass
from concourse import mybir

F32 = mybir.dt.float32
F32R = mybir.dt.float32r
I32 = mybir.dt.int32
ALU = mybir.AluOpType
ACT = mybir.ActivationFunctionType
AX = mybir.AxisListType

P = 128
S = 512
D = 1024
KT = D // P
ST = S // P
DEPTH = 2
HEADS = 8
GROUPS = 2
HD = 64
ATTN_W = HEADS * HD
KV_W = GROUPS * HD
CONV_CH = D - ATTN_W
NCMP = S // 16 - 1
CMP_PAIRS = 16
ALPHA = float((2 * DEPTH) ** 0.25)
LN_EPS = 1e-5
RMS_EPS = 1e-6
NEG = -1e30
D_PART = 1408
PT = D_PART // P
DENSE_PARTS = 2
EXPERTS = 8
SCALE1 = HD ** -0.5
HD2 = 128
SCALE2 = HD2 ** -0.5
ROT = 32
RING = 3
PRIMED = 1

C_Q, C_KC, C_VC, C_KS, C_VS, C_KW, C_VW = 0, 512, 640, 768, 896, 1024, 1152
C_GATES = C_VW + KV_W
C_U = C_GATES + 3 * HEADS
C_BG = C_U + CONV_CH
C_CG = C_BG + CONV_CH

K_ID = 0
K_CAUSAL = K_ID + P
K_CMP = K_CAUSAL + P
K_VALID = K_CMP + ST * NCMP
K_DIL = K_VALID + 1
K_ROT = K_DIL + S
K_FREQ = K_ROT + P
K_PAIR = K_FREQ + 1
K_ALL = K_PAIR + EXPERTS * EXPERTS

VECTORS = [("ln_in_g", 8), ("ln_in_b", 8), ("ln1_g", 16), ("ln1_b", 16), ("ln2_g", 16), ("ln2_b", 16),
           ("cmp_b1", 8), ("conv_w", 24), ("b2dup", DEPTH),
           ("g_norm_2", 8), ("b_mod_2", 24), ("b_gate_2", 16), ("conv_w_2", 32),
           ("conv_b_2", 8), ("b_a_2", 8), ("b_x_2", 8), ("lam_2", 8), ("g_final_2", 8), ("c_2", 8),
           ("cmp_pos", 64)]
FIRST_OF = {"g_norm_2": 1, "cmp_pos": 2}


def vector_places():
    where, stage, row = {}, 0, 0
    for name, rows in VECTORS:
        if name in FIRST_OF:
            stage, row = FIRST_OF[name], 0
        where[name] = stage * P + row
        row += rows
        assert row <= P
    return where


def stage_rows():
    used = [0, 0, 0]
    for name, rows in VECTORS:
        used[WHERE[name] // P] = WHERE[name] % P + rows
    return used


def vector_sources(a, name):
    v = a[name]
    if name == "cmp_pos":
        return v.rearrange("l v (t q) d -> (l v t) (q d)", q=2)
    if name in ("b_a_2", "b_x_2"):
        return v.rearrange("l k p -> (l k) p")
    form = {1: "(k p) -> k p", 2: "l (k p) -> (l k) p", 3: "l v (k p) -> (l v k) p"}[len(v.shape)]
    return v.rearrange(form, p=P)


WHERE = vector_places()
STAGE_ROWS = stage_rows()
STAGED = len(VECTORS) - 1 + 2 * DEPTH

N_MOD = 24
N_PROJ = 7 + 4 + 12
N_MIX = N_PROJ + KT
N_PART = 2 * PT + KT
BASE_MIX = [N_MOD, N_MOD + N_MIX + DENSE_PARTS * N_PART]
BASE_FFN = [b + N_MIX for b in BASE_MIX]
PARTS = [DENSE_PARTS, EXPERTS]
BASE_2 = BASE_FFN[1] + EXPERTS * N_PART
B2_X = BASE_2
B2_Z = B2_X + KT
B2_RNN = B2_Z + KT
B2_ZA = B2_RNN + 2 * KT
B2_HEAD = B2_ZA + KT
B2_ATT = B2_HEAD + 3 * HEADS
B2_O = B2_ATT + 2 * KT
N_ALL = B2_O + KT


def constant_table():
    t = np.zeros((P, K_ALL), np.float32)
    p = np.arange(P)[:, None]
    j = np.arange(P)[None, :]
    t[:, K_ID:K_ID + P] = (p == j)
    t[:, K_CAUSAL:K_CAUSAL + P] = np.where(j <= p, 0.0, NEG)
    for i in range(ST):
        ends = np.arange(NCMP)[None, :] * 16 + 31
        t[:, K_CMP + i * NCMP:K_CMP + (i + 1) * NCMP] = np.where(ends <= i * P + p, 0.0, NEG)
    t[:, K_VALID] = (p[:, 0] >= 31)
    dist = p + (S - P) - np.arange(S)[None, :]
    count = ((dist >= 0) & (dist <= 128)).astype(np.float64) + ((dist >= 0) & (dist % 4 == 0)) \
        + ((dist >= 0) & (dist % 16 == 0))
    t[:, K_DIL:K_DIL + S] = np.where(count > 0, np.log(np.maximum(count, 1)) / SCALE2, NEG)
    half = ROT // 2
    for i in range(half):
        t[i + half, K_ROT + i] = -1.0
        t[i, K_ROT + i + half] = 1.0
    freq = np.float32(500000.0) ** (-np.arange(0, ROT, 2, dtype=np.float32) / np.float32(ROT))
    t[:ROT, K_FREQ] = np.concatenate([freq, freq])
    e = np.arange(EXPERTS)
    t[:, K_PAIR:] = (e[None, :] < e[:, None]).astype(np.float32).reshape(1, -1)
    return t


class Lane:

    def __init__(self, eng, sem):
        self.eng, self.sem, self.n, self.turn = eng, sem, 0, 0

    def step(self, ins):
        ins.then_inc(self.sem, 1)
        self.n += 1

    def settle(self):
        self.eng.wait_ge(self.sem, self.turn + self.n)

    @contextmanager
    def loop(self, count, per):
        with self.eng.Fori(0, count) as i:
            before, outer = self.n, self.turn
            self.turn = outer + i * per
            yield i
            assert self.n == before + per, (self.n - before, per)
            self.turn = outer
        self.n = before + per * count


def build(nc, a, out, stop=None):
    with ExitStack() as ctx:
        def sb(name, shape, dt=F32, stack=ctx):
            return stack.enter_context(nc.sbuf_tensor(name, shape, dt))

        def sem(name):
            return ctx.enter_context(nc.semaphore(name))

        bank = [ctx.enter_context(nc.psum_tensor(f"bank{b}", [P, 512], F32)) for b in range(8)]

        raw = [sb(f"raw{r}", [P, PT, P]) for r in range(RING)]
        head = [sb(f"head{r}", [P, PT, P], F32R) for r in range(RING)]
        rest = [sb(f"rest{r}", [P, PT, P], F32R) for r in range(RING)]
        cst = sb("cst", [P, K_ALL])
        par = sb("par", [P, 3 * P])
        H = sb("H", [P, KT, S])
        HH = sb("HH", [P, KT, S], F32R)
        HL = sb("HL", [P, KT, S], F32R)
        mean_w = sb("mean_w", [P, P])
        eps = sb("eps", [P, 2])
        sq = sb("sq", [P, 2, S])
        rstd = sb("rstd", [P, S])
        mod = sb("mod", [P, N_MOD])
        c_act = sb("c_act", [P, KT, 2])
        c_head = sb("c_head", [P, KT, 2], F32R)
        c_rest = sb("c_rest", [P, KT, 2], F32R)
        ident = cst[:, K_ID:K_ID + P]
        causal = cst[:, K_CAUSAL:K_CAUSAL + P]

        with ExitStack() as s:
            x_tok = sb("x_tok", [P, ST, D], stack=s)
            stage = sb("stage", [P, 3, P], stack=s)
        with ExitStack() as s:
            K4 = sb("K4", [P, 4, GROUPS, S], stack=s)
            V = sb("V", [P, 2, ST, P], stack=s)
            GA = sb("GA", [P, ST, 3, HEADS], stack=s)
            KC = sb("KC", [P, GROUPS, NCMP], stack=s)
            VC = sb("VC", [NCMP, GROUPS, HD], stack=s)
            Q = sb("Q", [P, 4, S], stack=s)
            with ExitStack() as s2:
                W1 = sb("W1", [P, 2, CMP_PAIRS, 256], stack=s2)
            with ExitStack() as s2:
                MH = sb("MH", [P, KT, S], F32R, stack=s2)
                ML = sb("ML", [P, KT, S], F32R, stack=s2)
            s.enter_context(nc.sbuf_tensor("mix_place", [P, 2 * KT, S], F32))
            with ExitStack() as s2:
                VT = sb("VT", [P, 2, S], stack=s2)
                GT = sb("GT", [3 * HEADS, S], stack=s2)
                A2 = sb("A2", [P, 2, 3, S // 2], stack=s2)
                W2 = sb("W2", [P, 2, 2, P], stack=s2)
                b2row = sb("b2row", [NCMP, HD], stack=s2)
                bsum = sb("bsum", [P, 4], stack=s2)
                HG = sb("HG", [P, 2, 2, GROUPS * NCMP], stack=s2)
            with ExitStack() as s2:
                t_cg = sb("t_cg", [P, 2, S], stack=s2)
                zpad = sb("zpad", [P, 2, 2 + S], stack=s2)
                cy = sb("cy", [P, 2, S], stack=s2)
            with ExitStack() as s2:
                QC = sb("QC", [P, 2, S], stack=s2)
                Pc = sb("Pc", [P, 2, 32], stack=s2)
                Ps = sb("Ps", [P, 2, S], stack=s2)
                Pw = sb("Pw", [P, 2, S], stack=s2)
                PTs = sb("PTs", [P, ST, P], stack=s2)
                PTw = sb("PTw", [P, ST, P], stack=s2)
                PTc = sb("PTc", [NCMP, P], stack=s2)
                mx = sb("mx", [P, 3], stack=s2)
                nb = sb("nb", [P, 2, 3], stack=s2)
                Z = sb("Z", [P, 2, 3], stack=s2)
                rz = sb("rz", [P, 3], stack=s2)
                fac = sb("fac", [P, 3], stack=s2)
                ot = sb("ot", [P, P], stack=s2)
        with ExitStack() as s:
            UH = sb("UH", [P, PT, S], F32R, stack=s)
            UL = sb("UL", [P, PT, S], F32R, stack=s)
            silu_g = sb("silu_g", [P, 2, S], stack=s)
            gu = sb("gu", [P, 2, S], stack=s)
            GB = sb("GB", [P, EXPERTS, S], stack=s)
            rw = sb("rw", [P, KT, EXPERTS], stack=s)
            lgT = sb("lgT", [EXPERTS, S], stack=s)
            lg = sb("lg", [P, ST, EXPERTS], stack=s)
            gt8 = sb("gt8", [P, ST * EXPERTS, EXPERTS], stack=s)
            eq8 = sb("eq8", [P, ST * EXPERTS, EXPERTS], stack=s)
            sel = sb("sel", [P, ST, EXPERTS], stack=s)
            top = sb("top", [P, ST], stack=s)
            ex = sb("ex", [P, ST, EXPERTS], stack=s)
        with ExitStack() as s:
            with ExitStack() as s2:
                XC = sb("XC", [P, KT, S], stack=s2)
                IX = sb("IX", [P, KT, S], stack=s2)
                R = sb("R", [P, KT, S], stack=s2)
                M = sb("M", [P, KT, S], stack=s2)
            with ExitStack() as s2:
                GH = sb("GH", [P, KT, S], F32R, stack=s2)
                RH = sb("RH", [P, KT, S], F32R, stack=s2)
                RL = sb("RL", [P, KT, S], F32R, stack=s2)
                GL = sb("GL", [P, KT, S], F32R, stack=s2)
            s.enter_context(nc.sbuf_tensor("three_places", [P, 3 * KT, S], F32))
            with ExitStack() as s2:
                with ExitStack() as s3:
                    WA = sb("WA", [P, 2, KT, P], stack=s3)
                    xpad = sb("xpad", [P, 3 + S], stack=s3)
                with ExitStack() as s3:
                    lt = sb("lt", [P, 2, S], stack=s3)
                    la2 = sb("la2", [P, S], stack=s3)
                s2.enter_context(nc.sbuf_tensor("wa_place", [P, 2 * KT * P + S + 4], F32))
                keep = sb("keep", [P, S], stack=s2)
                drop = sb("drop", [P, S], stack=s2)
            s.enter_context(nc.sbuf_tensor("m_place", [P, KT, S], F32))
            modg = sb("modg", [P, KT], stack=s)
            lamc = sb("lamc", [P, 8, KT], stack=s)
            t2 = sb("t2", [P, 2, S], stack=s)
            cosT = sb("cosT", [ROT, S], stack=s)
            sinT = sb("sinT", [ROT, S], stack=s)
            with ExitStack() as s2:
                posi = sb("posi", [P, S], I32, stack=s2)
                ang = sb("ang", [ROT, S], stack=s2)
                turns = sb("turns", [ROT, S], I32, stack=s2)
                turnf = sb("turnf", [ROT, S], stack=s2)
            with ExitStack() as s2:
                qh = sb("qh", [P, S], stack=s2)
                kh = sb("kh", [P, S], stack=s2)
                vh = sb("vh", [P, S], stack=s2)
                V2 = sb("V2", [P, ST, P], stack=s2)
                P2 = sb("P2", [P, 2, S], stack=s2)
                PT2 = sb("PT2", [P, ST, P], stack=s2)
                m2 = sb("m2", [P, 2], stack=s2)
                n2 = sb("n2", [P, 2], stack=s2)
                z2 = sb("z2", [P, 2], stack=s2)
                r2 = sb("r2", [P, 2], stack=s2)
                oz = sb("oz", [P, S], stack=s2)
        with ExitStack() as s:
            y_tok = sb("y_tok", [P, ST, D], stack=s)

        sem_cst = sem("constants_landed")
        sem_stage = sem("vectors_landed")
        sem_x = sem("x_landed")
        raw_landed = [sem(f"raw_landed{r}") for r in range(RING)]
        slab_begun = sem("slab_begun")
        head_done = sem("head_done")
        weights_split = sem("weights_split")
        tile_done = sem("tile_done")
        bank_free = [sem(f"bank_free{b}") for b in range(RING)]
        vec_step = sem("vec_step")
        act_step = sem("act_step")
        setup_done = sem("setup_done")
        par_T = sem("par_transposed")
        par_ready = sem("par_ready")
        c_hi = sem("c_head_ready")
        c_lo = sem("c_rest_ready")
        x_T = sem("x_transposed")
        y_ready = sem("y_ready")
        mean_done = sem("mean_done")
        d_ready = sem("d_ready")
        sq_ready = sem("sq_ready")
        sq_used = sem("sq_used")
        std_ready = sem("std_ready")
        rs_ready = sem("rs_ready")
        xn_ready = sem("xn_ready")
        h_ready = sem("h_ready")
        hh_ready = sem("hh_ready")
        hl_ready = sem("hl_ready")
        w1_landed = sem("w1_landed")
        dup_c = sem("dup_cmp")
        dup_s = sem("dup_sel_win")
        vg_T = sem("vg_transposed")
        vg_ready = sem("vg_ready")
        a2_ready = sem("a2_ready")
        hid_done = sem("hidden_done")
        bsum_ready = sem("bsum_ready")
        gelu_ready = sem("gelu_ready")
        kcvc_done = sem("kcvc_done")
        kcvc_ready = sem("kcvc_ready")
        mixh_ready = sem("mixh_ready")
        mixl_ready = sem("mixl_ready")
        q_ready = sem("q_ready")
        s_done = sem("scores_done")
        max_ready = sem("max_ready")
        exp_ready = sem("exp_ready")
        t_done = sem("probs_transposed")
        pts_ready = sem("pts_ready")
        ptw_ready = sem("ptw_ready")
        pv_done = sem("pv_done")
        comb_ready = sem("combined_ready")
        ot_done = sem("out_transposed")
        oh_ready = sem("att_head_ready")
        ol_ready = sem("att_rest_ready")
        silu_ready = sem("silu_ready")
        uh_ready = sem("uh_ready")
        ul_ready = sem("ul_ready")
        down_taken = sem("down_taken")
        rw_landed = sem("router_landed")
        lg_done = sem("logits_done")
        lg_ready = sem("logits_ready")
        gate_ready = sem("gate_ready")
        b2_landed = sem("block2_landed")
        xc_ready = sem("xc_ready")
        ri_done = sem("ri_done")
        ri_ready = sem("ri_ready")
        ix_ready = sem("ix_ready")
        decay_ready = sem("decay_ready")
        lam_abs = sem("lam_abs_ready")
        lam_exp = sem("lam_exp_ready")
        router_exp = sem("router_exp_ready")
        lru_q = sem("lru_q_ready")
        root_ready = sem("root_ready")
        hr_ready = sem("hr_ready")
        zs_ready = sem("zs_ready")
        u2_ready = sem("u2_ready")
        u2h_ready = sem("u2h_ready")
        u2l_ready = sem("u2l_ready")
        sg_ready = sem("sigmoid_ready")
        ang_ready = sem("angles_ready")
        tab_ready = sem("tables_ready")
        rot_done = sem("rotation_done")
        rope_ready = sem("rope_ready")
        v2_done = sem("v2_done")
        v2_ready = sem("v2_ready")
        s2_done = sem("scores2_done")
        m2_ready = sem("max2_ready")
        e2_ready = sem("exp2_ready")
        p2_ready = sem("p2_ready")
        t2_done = sem("t2_done")
        pt2_ready = sem("pt2_ready")
        pv2_done = sem("pv2_done")
        y_T = sem("y_transposed")
        y_ready2 = sem("y_tok_ready")
        y_out = sem("y_out")

        block = ctx.enter_context(nc.Block())

        def col(name, k):
            c = WHERE[name] + k
            return par[:, c:c + 1]

        def slab(w, c):
            return w[:, c:c + P].rearrange("(k p) n -> p k n", p=P)

        def taken(eng, n):
            eng.wait_ge(bank_free[n % RING], n // RING + 1)

        def take(ins, n):
            ins.then_inc(bank_free[n % RING], 1)

        @block.sync
        def _(sp):
            def load(n, src, kt=KT):
                if not isinstance(n, int) or n >= RING:
                    sp.wait_ge(weights_split, n - (RING - 1))
                sp.dma_start(raw[slot][:, 0:kt, :], src).then_inc(raw_landed[slot], 16)

            sp.dma_start(cst[:, :], a["consts"]).then_inc(sem_cst, 16)
            sp.dma_start(x_tok[:, :, :], a["x"].rearrange("b (t p) d -> p (b t) d", p=P)).then_inc(sem_x, 16)
            for n in range(N_MOD):
                slot = n % RING
                load(n, slab(a["w_mod_2"][0], n * P))
            for l in range(DEPTH):
                w = a["w_in"][l]
                order = [C_KC, C_VC, C_KS, C_KW, C_VS, C_VW, C_GATES] + [C_Q + P * t for t in range(4)]
                for t in range(4):
                    order += [C_CG + P * t, C_U + P * t, C_BG + P * t]
                for k, c in enumerate(order):
                    slot = (BASE_MIX[l] + k) % RING
                    load(BASE_MIX[l] + k, slab(w, c))
                for k in range(KT):
                    n = BASE_MIX[l] + N_PROJ + k
                    slot = n % RING
                    load(n, slab(a["w_o"][l], k * P))
                with sp.Fori(0, PARTS[l]) as e:
                    for j in range(N_PART):
                        n = BASE_FFN[l] + e * N_PART + j
                        slot = (BASE_FFN[l] + j) % RING
                        if j < 2 * PT:
                            m = j // 2
                            if l == 0:
                                w = a["ffn_wg" if j % 2 == 0 else "ffn_wu"]
                                src = w[0].rearrange("(k p) n -> p k n", p=P)[:, :, bass.ds(e * D_PART + m * P, P)]
                            else:
                                w = a["moe_wg" if j % 2 == 0 else "moe_wu"]
                                src = w[0, bass.ds(e, 1), :, m * P:(m + 1) * P] \
                                    .rearrange("o (k p) n -> p (o k) n", p=P)
                            load(n, src)
                        else:
                            m = j - 2 * PT
                            if l == 0:
                                src = a["ffn_wd"][0].rearrange("(e k p) n -> e p k n", p=P, k=PT)[
                                    bass.ds(e, 1), :, :, m * P:(m + 1) * P].rearrange("o p k n -> (o p) k n")
                            else:
                                src = a["moe_wd"][0, bass.ds(e, 1), :, m * P:(m + 1) * P] \
                                    .rearrange("o (k p) n -> p (o k) n", p=P)
                            load(n, src, PT)
            w2 = a["w_in_2"][0]
            order = [(w2, k * P) for k in range(2 * KT)]
            for k in range(KT):
                order += [(w2, 6 * D + k * P), (a["w_out_rnn_2"][0], k * P)]
            order += [(w2, 5 * D + k * P) for k in range(KT)]
            for h in range(HEADS):
                order += [(w2, 2 * D + h * P), (w2, 3 * D + h * P), (w2, 4 * D + h * P)]
            for k in range(KT):
                order += [(w2, 7 * D + k * P), (a["w_out_attn_2"][0], k * P)]
            order += [(a["w_o_2"][0], k * P) for k in range(KT)]
            assert len(order) == N_ALL - BASE_2
            for k, (w, c) in enumerate(order):
                slot = (BASE_2 + k) % RING
                load(BASE_2 + k, slab(w, c))
            for t in range(ST):
                sp.wait_ge(y_ready2, 2 * (t + 1))
                sp.dma_start(out[0, t * P:(t + 1) * P, :], y_tok[:, t, :]).then_inc(y_out, 16)
            sp.wait_ge(y_out, 16 * ST)

        @block.gpsimd
        def _(pool):
            def split(n, slot, kt):
                pool.wait_ge(raw_landed[slot], ((n - slot) // RING + 1) * 16 if isinstance(n, int) else n[1])
                v = n if isinstance(n, int) else n[0]
                if not isinstance(n, int) or n >= RING:
                    pool.wait_ge(tile_done, v - (RING - 1))
                pool.sem_inc(slab_begun, 1)
                pool.tensor_copy(head[slot][:, 0:kt, :], raw[slot][:, 0:kt, :]).then_inc(head_done, 1)
                pool.wait_ge(head_done, v + 1)
                pool.tensor_tensor(rest[slot][:, 0:kt, :], raw[slot][:, 0:kt, :], head[slot][:, 0:kt, :],
                                   ALU.subtract).then_inc(weights_split, 1)

            def run(n0, count, kt=KT):
                turns_, left = count // RING, count % RING
                first = 0
                if n0 == 0:
                    for j in range(RING):
                        split(j, j, kt)
                    first = RING
                    turns_ -= 1
                if turns_ > 0:
                    with pool.Fori(0, turns_) as i:
                        for j in range(RING):
                            n = n0 + first + j
                            slot = n % RING
                            split((i * RING + n, i * 16 + ((n - slot) // RING + 1) * 16), slot, kt)
                for j in range(left):
                    n = n0 + first + turns_ * RING + j
                    split(n, n % RING, kt)

            run(0, BASE_FFN[0])
            for l in range(DEPTH):
                with pool.Fori(0, PARTS[l]) as e:
                    for j in range(N_PART):
                        n = BASE_FFN[l] + j
                        slot = n % RING
                        split((e * N_PART + n, e * (16 * N_PART // RING) + ((n - slot) // RING + 1) * 16), slot,
                              KT if j < 2 * PT else PT)
                if l == 0:
                    run(BASE_MIX[1], N_MIX)
            run(BASE_2, N_ALL - BASE_2)

        @block.tensor
        def _(pe):
            def tile(n, hi, lo, kt=KT, cols=S, use=None, ready=None):
                static = n if isinstance(n, int) else use[0]
                slot = static % RING
                pe.wait_ge(weights_split, n + 1)
                if static >= RING:
                    pe.wait_ge(bank_free[slot], static // RING if isinstance(n, int) else use[1])
                last = None
                for k in range(kt):
                    if ready:
                        ready(k)
                    for w, act, first, final in ((head, hi, True, False), (head, lo, False, False),
                                                 (rest, hi, False, True)):
                        last = pe.matmul(bank[slot][:, 0:cols], w[slot][:, k, :], act[:, k, 0:cols],
                                         start=(k == 0 and first), stop=(k == kt - 1 and final))
                last.then_inc(tile_done, 1)

            def tiles(n0, count, hi, lo):
                turns_ = count // RING
                if turns_ > 1:
                    with pe.Fori(0, turns_) as i:
                        for j in range(RING):
                            n = n0 + j
                            tile(i * RING + n, hi, lo, use=(n, i + n // RING))
                    done = turns_ * RING
                else:
                    done = 0
                for j in range(done, count):
                    tile(n0 + j, hi, lo)

            def mean(L, ready):
                for k in range(KT):
                    ready(k)
                    last = pe.matmul(bank[3][:, :], mean_w[:, :], H[:, k, :], start=(k == 0), stop=(k == KT - 1))
                last.then_inc(mean_done, 1)

            def var(L):
                for k in range(KT):
                    pe.wait_ge(sq_ready, KT * L + k + 1)
                    pe.matmul(bank[4][:, :], mean_w[:, :], sq[:, k % 2, :], start=(k == 0),
                              stop=(k == KT - 1)).then_inc(sq_used, 1)

            def mod_tiles(lo, hi):
                for n in range(lo, hi):
                    tile(n, c_head, c_rest, cols=2)

            for primed in (s_done, pv_done, pv2_done):
                pe.sem_inc(primed, PRIMED)
            pe.wait_ge(sem_cst, 16)
            pe.wait_ge(sem_stage, 16 * STAGED)
            pe.wait_ge(setup_done, 3)
            for r, rows in enumerate(STAGE_ROWS):
                last = pe.transpose(bank[7][:, r * P:r * P + rows], stage[0:rows, r, :], cst[0:rows, K_ID:K_ID + rows])
            last.then_inc(par_T, 1)
            pe.wait_ge(sem_x, 16)
            for k in range(KT):
                if k >= 2:
                    pe.wait_ge(y_ready, k - 1)
                for t in range(ST):
                    last = pe.transpose(bank[5 + k % 2][:, t * P:(t + 1) * P], x_tok[:, t, k * P:(k + 1) * P], ident)
                last.then_inc(x_T, 1)
            mean(0, lambda k: pe.wait_ge(y_ready, k + 1))
            pe.wait_ge(c_lo, 1)
            mod_tiles(0, 9)
            var(0)
            mod_tiles(9, N_MOD)

            def mixer(l):
                n0 = BASE_MIX[l]
                pe.wait_ge(hl_ready, KT * (2 * l + 1))
                tiles(n0, 11, HH, HL)
                for b in range(2):
                    taken(pe, n0 + 4 + b)
                    for t in range(ST):
                        last = pe.transpose(bank[5 + b][:, t * P:(t + 1) * P], VT[:, b, t * P:(t + 1) * P], ident)
                    last.then_inc(vg_T, 1)
                taken(pe, n0 + 6)
                for t in range(ST):
                    last = pe.transpose(bank[7][:, t * 24:(t + 1) * 24], GT[:, t * P:(t + 1) * P],
                                        cst[0:24, K_ID:K_ID + 24])
                last.then_inc(vg_T, 1)
                pe.wait_ge(w1_landed, 16 * 7 * (l + 1))
                pe.wait_ge(a2_ready, l + 1)
                pe.wait_ge(vg_ready, 3 * l + 3)
                for kv in range(2):
                    for m in range(2):
                        b = bank[3 + 2 * kv + m]
                        for tp in range(CMP_PAIRS):
                            last = pe.matmul(b[:, 0:3 * NCMP].rearrange("p (g n) -> p g n", g=3),
                                             W1[:, kv, tp, m * P:(m + 1) * P],
                                             A2[:, kv, :, tp:tp + 8 * (NCMP - 1) + 1:8],
                                             start=(tp == 0), stop=(tp == CMP_PAIRS - 1))
                        last.then_inc(hid_done, 1)
                pe.wait_ge(gelu_ready, 4 * (l + 1))
                for m in range(2):
                    pe.matmul(bank[7][:, 0:2 * NCMP], W2[:, 0, m, :], HG[:, 0, m, :], start=(m == 0), stop=(m == 1))
                for g in range(GROUPS):
                    for m in range(2):
                        last = pe.matmul(bank[7][0:NCMP, 64 + g * HD:64 + (g + 1) * HD],
                                         HG[:, 1, m, g * NCMP:(g + 1) * NCMP], W2[:, 1, m, 0:HD],
                                         start=(m == 0), stop=(m == 1))
                last.then_inc(kcvc_done, 1)
                tiles(n0 + 11, 12, HH, HL)
                attention(l)
                pe.wait_ge(mixl_ready, 4 * (l + 1))
                pe.wait_ge(ol_ready, PRIMED + 16 * (l + 1))
                tiles(n0 + N_PROJ, KT, MH, ML)
                mean(2 * l + 1, lambda k: taken(pe, n0 + N_PROJ + k))
                var(2 * l + 1)

            def attention(l):
                pe.wait_ge(kcvc_ready, 2 * (l + 1))
                pe.wait_ge(dup_s, 64 * (l + 1))
                n_last = BASE_MIX[l] + N_PROJ - 1
                for b in range(RING):
                    taken(pe, n_last - b)

                with pe.Fori(0, 4) as t:
                    g = t // 2
                    u0 = 8 * t + 32 * l

                    def scores(v):
                        i, par_ = v // 2, v % 2
                        w = (i + 1) * P
                        if v == 0:
                            pe.wait_ge(q_ready, t + 4 * l + 1)
                            pe.wait_ge(exp_ready, PRIMED + 3 * u0)
                        else:
                            pe.wait_ge(exp_ready, PRIMED + 3 * (u0 + v))
                        lhs = QC[:, par_, i * P:(i + 1) * P]
                        pe.matmul(bank[7][:, 0:NCMP], lhs, KC[:, bass.ds(g, 1), :].rearrange("p o n -> p (o n)"),
                                  start=True, stop=False)
                        pe.matmul(bank[7][:, 0:NCMP], ident, cst[:, K_CMP + i * NCMP:K_CMP + (i + 1) * NCMP],
                                  start=False, stop=True)
                        for b, kind in ((3, 2), (5, 3)):
                            o = bank[b + v % 2]
                            pe.matmul(o[:, 0:w], lhs, K4[:, kind, bass.ds(g, 1), 0:w].rearrange("p o n -> p (o n)"),
                                      start=True, stop=False)
                            last = pe.matmul(o[:, i * P:w], ident, causal, start=False, stop=True)
                        last.then_inc(s_done, 1)

                    def turn(v):
                        i = v // 2
                        pe.wait_ge(exp_ready, PRIMED + 3 * (u0 + v + 1))
                        pe.wait_ge(comb_ready, PRIMED + u0 + v)
                        pe.wait_ge(pts_ready, PRIMED + u0 + v)
                        if v % 2 == 0:
                            pe.wait_ge(ol_ready, PRIMED + 4 * t + 16 * l + i)
                        pe.transpose(bank[2][0:NCMP, 0:P], Pc[:, v % 2, 0:NCMP], ident)
                        for k in range(i + 1):
                            pe.transpose(bank[0][:, k * P:(k + 1) * P], Ps[:, v % 2, k * P:(k + 1) * P], ident)
                        for k in range(i + 1):
                            last = pe.transpose(bank[1][:, k * P:(k + 1) * P], Pw[:, v % 2, k * P:(k + 1) * P], ident)
                        last.then_inc(t_done, 1)

                    def values(v):
                        i = v // 2
                        pe.wait_ge(ptw_ready, 2 * (u0 + v + 1))
                        pe.wait_ge(pts_ready, PRIMED + u0 + v + 1)
                        for b, src in ((0, PTs), (1, PTw)):
                            for k in range(i + 1):
                                pe.matmul(bank[2][:, (1 + b) * HD:(2 + b) * HD], src[:, k, :],
                                                 V[:, b, k, bass.ds(g * HD, HD)], start=(k == 0), stop=(k == i))
                        pe.matmul(bank[2][:, 0:HD], PTc[:, :], VC[:, bass.ds(g, 1), :].rearrange("p o n -> p (o n)"),
                                  start=True, stop=True).then_inc(pv_done, 1)

                    def out_turn(v):
                        pe.wait_ge(comb_ready, PRIMED + u0 + v + 1)
                        pe.transpose(bank[2][:, 0:P], ot[:, :], ident).then_inc(ot_done, 1)

                    scores(0)
                    for v in range(8):
                        if v < 7:
                            scores(v + 1)
                        if v % 2 == 0 and v > 0:
                            out_turn(v - 1)
                        turn(v)
                        values(v)
                    out_turn(7)

            def ffn(l):
                n0 = BASE_FFN[l]
                L = 2 * l + 1
                pe.wait_ge(hl_ready, KT * (L + 1))
                if l == 1:
                    router()
                with pe.Fori(0, PARTS[l]) as e:
                    for j in range(2 * PT):
                        tile(e * N_PART + n0 + j, HH, HL, use=(n0 + j, e * (N_PART // RING) + (n0 + j) // RING))
                    for j in range(KT):
                        n = n0 + 2 * PT + j

                        def ready(k, j=j):
                            if j == 0:
                                pe.wait_ge(ul_ready, PT * e + PT * l * DENSE_PARTS + k + 1)
                        tile(e * N_PART + n, UH, UL, kt=PT, use=(n, e * (N_PART // RING) + n // RING), ready=ready)
                if l == 0:
                    mean(L + 1, lambda k: taken(pe, BASE_MIX[1] - KT + k))
                else:
                    mean(L + 1, lambda k: pe.wait_ge(down_taken, PRIMED + KT * (EXPERTS - 1) + k + 1))
                var(L + 1)

            def router():
                pe.wait_ge(rw_landed, 16)
                for k in range(KT):
                    last = pe.matmul(bank[5][0:EXPERTS, :], rw[:, k, :], H[:, k, :], start=(k == 0), stop=(k == KT - 1))
                last.then_inc(lg_done, 1)
                pe.wait_ge(lg_ready, 1)
                for t in range(ST):
                    last = pe.transpose(bank[6][:, t * EXPERTS:(t + 1) * EXPERTS], lgT[:, t * P:(t + 1) * P],
                                        cst[0:EXPERTS, 0:EXPERTS])
                last.then_inc(lg_done, 1)
                pe.wait_ge(lg_ready, 3)
                for t in range(ST):
                    last = pe.transpose(bank[5][0:EXPERTS, t * P:(t + 1) * P], ex[:, t, :], ident)
                last.then_inc(lg_done, 1)
                pe.wait_ge(lg_ready, 4)
                for e in range(EXPERTS):
                    if e >= 2:
                        pe.wait_ge(gate_ready, e - 1)
                    pe.matmul(bank[6 + e % 2][:, :], cst[0:EXPERTS, e:e + 1].broadcast_to((EXPERTS, P)), lgT[:, :],
                              start=True, stop=True).then_inc(lg_done, 1)

            for l in range(DEPTH):
                mixer(l)
                ffn(l)

            var(5)
            pe.wait_ge(hl_ready, 5 * KT)
            pe.wait_ge(b2_landed, 48)

            def lru_gates(k):
                pe.wait_ge(xc_ready, k + 1)
                for b in range(2):
                    if k >= 1:
                        pe.wait_ge(ri_ready, 2 * (k - 1) + b + 1)
                    pe.matmul(bank[5 + b][:, :], WA[:, b, k, :], XC[:, k, :], start=True, stop=True) \
                      .then_inc(ri_done, 1)

            for k in range(KT):
                tile(B2_X + k, HH, HL)
                if k >= 1:
                    lru_gates(k - 1)
            lru_gates(KT - 1)
            tiles(B2_Z, KT, HH, HL)
            for k in range(KT):
                tile(B2_RNN + 2 * k, HH, HL)
                pe.wait_ge(u2l_ready, KT)
                tile(B2_RNN + 2 * k + 1, RH, RL)
            tiles(B2_ZA, KT, HH, HL)
            with pe.Fori(0, HEADS) as h:
                for j in range(3):
                    n = B2_HEAD + j
                    tile(h * 3 + n, HH, HL, use=(n, h + n // RING))
                for j, src in ((0, qh), (1, kh)):
                    pe.wait_ge(bank_free[(B2_HEAD + j) % RING], h + (B2_HEAD + j) // RING + 1)
                    if j == 1:
                        pe.wait_ge(u2_ready, KT + h)
                    pe.matmul(bank[3 + j][:, :], cst[:, K_ROT:K_ROT + P], src[:, :], start=True,
                              stop=True).then_inc(rot_done, 1)
                pe.wait_ge(bank_free[(B2_HEAD + 2) % RING], h + (B2_HEAD + 2) // RING + 1)
                for t in range(ST):
                    last = pe.transpose(bank[5][:, t * P:(t + 1) * P], vh[:, t * P:(t + 1) * P], ident)
                last.then_inc(v2_done, 1)
                pe.wait_ge(rope_ready, 2 * h + 2)

                def scores2(i):
                    w = (i + 1) * P
                    if i >= 2:
                        pe.wait_ge(e2_ready, 4 * h + i - 1)
                    pe.matmul(bank[6 + i % 2][:, 0:w], qh[:, i * P:w], kh[:, 0:w], start=True, stop=False)
                    pe.matmul(bank[6 + i % 2][:, 0:w], ident, cst[:, K_DIL + (3 - i) * P:K_DIL + S], start=False,
                              stop=True).then_inc(s2_done, 1)

                scores2(0)
                pe.wait_ge(v2_ready, h + 1)
                for i in range(ST):
                    if i < ST - 1:
                        scores2(i + 1)
                    pe.wait_ge(p2_ready, 4 * h + i + 1)
                    if i >= 1:
                        pe.wait_ge(pt2_ready, 4 * h + i)
                    for k in range(i + 1):
                        last = pe.transpose(bank[5][:, k * P:(k + 1) * P], P2[:, i % 2, k * P:(k + 1) * P], ident)
                    last.then_inc(t2_done, 1)
                    pe.wait_ge(pt2_ready, 4 * h + i + 1)
                    for k in range(i + 1):
                        last = pe.matmul(bank[4][:, i * P:(i + 1) * P], V2[:, k, :], PT2[:, k, :],
                                         start=(k == 0), stop=(k == i))
                    last.then_inc(pv2_done, 1)
            for k in range(KT):
                tile(B2_ATT + 2 * k, HH, HL)
                pe.wait_ge(u2l_ready, 2 * KT)
                tile(B2_ATT + 2 * k + 1, RH, RL)
            pe.wait_ge(u2l_ready, 3 * KT)
            tiles(B2_O, KT, GH, GL)
            var(6)
            for t in range(ST):
                for b in range(2):
                    q = 2 * t + b
                    pe.wait_ge(xn_ready, 7 * KT)
                    if q >= 2:
                        pe.wait_ge(y_ready2, q - 1)
                    for k in range(4):
                        last = pe.transpose(bank[5 + b][:, k * P:(k + 1) * P],
                                            H[:, 4 * b + k, t * P:(t + 1) * P], ident)
                    last.then_inc(y_T, 1)

        @block.scalar
        def _(act):
            lane = Lane(act, act_step)
            for primed in (exp_ready, pts_ready):
                act.sem_inc(primed, PRIMED)
            for name, rows in VECTORS:
                st, row = WHERE[name] // P, WHERE[name] % P
                if name == "b2dup":
                    for l in range(DEPTH):
                        for d in range(2):
                            act.dma_start(stage[row + l:row + l + 1, st, d * HD:(d + 1) * HD],
                                          a["cmp_b2"][l, 0:1, :]).then_inc(sem_stage, 16)
                else:
                    act.dma_start(stage[row:row + rows, st, :], vector_sources(a, name)).then_inc(sem_stage, 16)

            def compression_weights(l):
                for kv in range(2):
                    act.dma_start(W1[:, kv, :, :], a["cmp_w1"][l, kv].rearrange("(k p) n -> p k n", p=P)) \
                       .then_inc(w1_landed, 16)
                    for d in range(2):
                        act.dma_start(W2[:, kv, :, d * HD:(d + 1) * HD],
                                      a["cmp_w2"][l, kv].rearrange("(k p) n -> p k n", p=P)).then_inc(w1_landed, 16)
                act.dma_start(b2row[:, :], a["cmp_b2"][l, 1:2, :].broadcast_to((NCMP, HD))).then_inc(w1_landed, 16)

            def squares(L, ready):
                for k in range(KT):
                    ready(k)
                    if KT * L + k >= 2:
                        act.wait_ge(sq_used, KT * L + k - 1)
                    act.activation(sq[:, k % 2, :], H[:, k, :], ACT.Square).then_inc(sq_ready, 1)

            def root(L, e):
                act.wait_ge(sq_used, KT * (L + 1))
                act.activation(rstd[:, :], bank[4][:, :], ACT.Sqrt, bias=eps[:, e:e + 1]).then_inc(std_ready, 1)

            def layer_norm(L, g, b, row, split_=True):
                squares(L, lambda k: act.wait_ge(d_ready, KT * L + k + 1))
                root(L, 0)
                for k in range(KT):
                    act.wait_ge(xn_ready, KT * L + k + 1)
                    act.activation(H[:, k, :], H[:, k, :], ACT.Identity, bias=col(b, row + k),
                                   scale=col(g, row + k)).then_inc(h_ready, 1)
                    if split_:
                        act.wait_ge(h_ready, KT * L + k + 1)
                        act.activation(HH[:, k, :], H[:, k, :], ACT.Copy).then_inc(hh_ready, 1)

            act.wait_ge(par_ready, 3)
            act.wait_ge(setup_done, 3)
            for d in range(2):
                lane.step(act.activation(c_act[:, :, d], par[:, WHERE["c_2"]:WHERE["c_2"] + KT], ACT.Silu))
            lane.settle()
            act.activation(c_head[:, :, :], c_act[:, :, :], ACT.Copy).then_inc(c_hi, 1)
            layer_norm(0, "ln_in_g", "ln_in_b", 0)
            for l in range(DEPTH):
                n0 = BASE_MIX[l]
                if l == 1:
                    act.wait_ge(tile_done, BASE_MIX[1])
                compression_weights(l)
                for kind in range(4):
                    n = n0 + kind
                    act.wait_ge(tile_done, n + 1)
                    lane.step(act.activation(K4[0:64, kind, 0, :], bank[n % RING][0:64, :], ACT.Copy))
                    take(act.activation(K4[64:128, kind, 1, :], bank[n % RING][64:128, :], ACT.Copy), n)
                    lane.settle()
                    taken(act, n)
                    for g in range(GROUPS):
                        rows, other = slice(64 * g, 64 * g + 64), slice(64 - 64 * g, 128 - 64 * g)
                        act.dma_start(K4[other, kind, g, :], K4[rows, kind, g, :]) \
                           .then_inc(dup_c if kind < 2 else dup_s, 16)
                for b in range(2):
                    n = n0 + 4 + b
                    act.wait_ge(tile_done, n + 1)
                    take(act.activation(VT[:, b, :], bank[n % RING][:, :], ACT.Copy), n)
                n = n0 + 6
                act.wait_ge(tile_done, n + 1)
                take(act.activation(GT[:, :], bank[n % RING][0:3 * HEADS, :], ACT.Sigmoid), n)
                for kv in range(2):
                    for m in range(2):
                        j = 2 * kv + m
                        act.wait_ge(bsum_ready, 4 * l + j + 1)
                        act.activation(HG[:, kv, m, :], bank[3 + j][:, 0:2 * NCMP], ACT.Gelu_apprx_tanh,
                                       bias=bsum[:, j:j + 1]).then_inc(gelu_ready, 1)
                for c in range(4):
                    n = n0 + 11 + 3 * c
                    act.wait_ge(tile_done, n + 1)
                    if c >= 2:
                        taken(act, n + 1 - 6)
                    take(act.activation(t_cg[:, c % 2, :], bank[n % RING][:, :], ACT.Copy), n)
                    taken(act, n + 2)
                    act.activation(MH[:, 4 + c, :], cy[:, c % 2, :], ACT.Copy).then_inc(mixh_ready, 1)
                with act.Fori(0, 4) as t:
                    u0 = 8 * t + 32 * l

                    def exps(v):
                        w = (v // 2 + 1) * P
                        act.wait_ge(max_ready, u0 + v + 1)
                        if v >= 2:
                            act.wait_ge(t_done, u0 + v - 1)
                        for j, (o, src) in enumerate(((Pc[:, v % 2, 0:NCMP], bank[7][:, 0:NCMP]),
                                                      (Ps[:, v % 2, 0:w], bank[3 + v % 2][:, 0:w]),
                                                      (Pw[:, v % 2, 0:w], bank[5 + v % 2][:, 0:w]))):
                            act.activation(o, src, ACT.Exp, bias=nb[:, v % 2, j:j + 1], scale=SCALE1,
                                           accum_out=Z[:, v % 2, j:j + 1]).then_inc(exp_ready, 1)

                    def head_out(i):
                        act.wait_ge(ot_done, 4 * t + 16 * l + i + 1)
                        act.activation(MH[:, bass.ds(t, 1), i * P:(i + 1) * P].rearrange("p o n -> p (o n)"),
                                       bank[2][:, 0:P], ACT.Copy).then_inc(oh_ready, 1)

                    exps(0)
                    for v in range(8):
                        i = v // 2
                        if v < 7:
                            exps(v + 1)
                        if v % 2 == 0 and v > 0:
                            head_out(i - 1)
                        act.wait_ge(t_done, u0 + v + 1)
                        act.wait_ge(pv_done, PRIMED + u0 + v)
                        act.activation(PTs[:, 0:i + 1, :], bank[0][:, 0:(i + 1) * P]
                                       .rearrange("p (k q) -> p k q", q=P), ACT.Copy).then_inc(pts_ready, 1)
                    head_out(3)
                layer_norm(2 * l + 1, "ln1_g", "ln1_b", KT * l)
                if l == 1:
                    act.dma_start(rw[:, :, :], a["moe_router"][0].rearrange("(k p) e -> p k e", p=P)) \
                       .then_inc(rw_landed, 16)
                    act.wait_ge(lg_ready, 2)
                    act.activation(ex[:, :, :], lg[:, :, :], ACT.Exp).then_inc(router_exp, 1)
                n0 = BASE_FFN[l]
                with act.Fori(0, PARTS[l]) as e:
                    for j in range(PT):
                        n = n0 + 2 * j
                        act.wait_ge(tile_done, e * N_PART + n + 1)
                        take(act.activation(silu_g[:, j % 2, :], bank[n % RING][:, :], ACT.Silu), n)
                        act.wait_ge(bank_free[(n + 1) % RING], e * (N_PART // RING) + (n + 1) // RING + 1)
                        act.activation(UH[:, j, :], gu[:, j % 2, :], ACT.Copy).then_inc(uh_ready, 1)
                layer_norm(2 * l + 2, "ln2_g", "ln2_b", KT * l, split_=(l == 0))

            squares(5, lambda k: act.wait_ge(h_ready, KT * 4 + k + 1))
            act.dma_start(WA[:, 0, :, :], a["w_a_2"][0].rearrange("k p n -> p k n")).then_inc(b2_landed, 16)
            act.dma_start(WA[:, 1, :, :], a["w_x_2"][0].rearrange("k p n -> p k n")).then_inc(b2_landed, 16)
            act.dma_start(posi[:, :], a["positions_2"].broadcast_to((P, S))).then_inc(b2_landed, 16)
            root(5, 1)
            for k in range(KT):
                act.wait_ge(xn_ready, 5 * KT + k + 1)
                act.activation(HH[:, k, :], t2[:, k % 2, :], ACT.Identity, bias=mod[:, k:k + 1],
                               scale=modg[:, k:k + 1]).then_inc(hh_ready, 1)
            act.wait_ge(lam_abs, 1)
            act.activation(lamc[:, 1, :], lamc[:, 0, :], ACT.Exp, scale=-1.0).then_inc(lam_exp, 1)
            for j, o in enumerate((sinT, cosT)):
                act.wait_ge(ang_ready, j + 1)
                act.activation(o[:, :], o[:, :], ACT.Sin).then_inc(tab_ready, 1)

            def conv_in(k):
                n = B2_X + k
                act.wait_ge(tile_done, n + 1)
                if k >= 1:
                    act.wait_ge(xc_ready, k)
                take(act.activation(xpad[:, 3:3 + S], bank[n % RING][:, :], ACT.Copy), n)

            conv_in(0)
            for k in range(KT):
                if k + 1 < KT:
                    conv_in(k + 1)
                for b, (o, bias) in enumerate(((R, "b_a_2"), (IX, "b_x_2"))):
                    act.wait_ge(ri_done, 2 * k + b + 1)
                    act.activation(o[:, k, :], bank[5 + b][:, :], ACT.Sigmoid, bias=col(bias, k)) \
                       .then_inc(ri_ready, 1)
            for k in range(KT):
                act.wait_ge(ix_ready, k + 1)
                act.activation(XC[:, k, :], R[:, k, :], ACT.Exp, scale=lamc[:, 6, k:k + 1]).then_inc(decay_ready, 1)
                if k >= 2:
                    act.wait_ge(lru_q, k - 1)
                act.activation(lt[:, k % 2, :], R[:, k, :], ACT.Tanh, scale=lamc[:, 7, k:k + 1]) \
                   .then_inc(decay_ready, 1)
            for k in range(KT):
                act.wait_ge(lru_q, k + 1)
                act.activation(R[:, k, :], R[:, k, :], ACT.Sqrt).then_inc(root_ready, 1)
            for k in range(KT):
                n = B2_Z + k
                act.wait_ge(tile_done, n + 1)
                act.wait_ge(hr_ready, k + 1)
                take(act.activation(XC[:, k, :], bank[n % RING][:, :], ACT.Silu), n)
                act.wait_ge(u2_ready, k + 1)
                act.activation(RH[:, k, :], t2[:, k % 2, :], ACT.Copy).then_inc(u2h_ready, 1)
            act.wait_ge(u2l_ready, KT)
            for k in range(KT):
                n = B2_RNN + 2 * k
                act.wait_ge(tile_done, n + 1)
                if k >= 2:
                    taken(act, n + 1 - 4)
                take(act.activation(t2[:, k % 2, :], bank[n % RING][:, :], ACT.Sigmoid, bias=col("b_gate_2", k)), n)
            for k in range(KT):
                n = B2_ZA + k
                act.wait_ge(tile_done, n + 1)
                take(act.activation(XC[:, k, :], bank[n % RING][:, :], ACT.Silu), n)
            with act.Fori(0, HEADS) as h:
                for j, o in enumerate((qh, kh, vh)):
                    n = B2_HEAD + j
                    act.wait_ge(tile_done, h * 3 + n + 1)
                    take(act.activation(o[:, :], bank[n % RING][:, :], ACT.Copy), n)

                def turned(i):
                    act.wait_ge(t2_done, 4 * h + i + 1)
                    act.wait_ge(pv2_done, PRIMED + 4 * h + i)
                    act.activation(PT2[:, 0:i + 1, :], bank[5][:, 0:(i + 1) * P].rearrange("p (k q) -> p k q", q=P),
                                   ACT.Copy).then_inc(pt2_ready, 1)

                for i in range(ST):
                    w = (i + 1) * P
                    act.wait_ge(m2_ready, 4 * h + i + 1)
                    if i >= 2:
                        act.wait_ge(t2_done, 4 * h + i - 1)
                    act.activation(P2[:, i % 2, 0:w], bank[6 + i % 2][:, 0:w], ACT.Exp, bias=n2[:, i % 2:i % 2 + 1],
                                   scale=SCALE2, accum_out=z2[:, i % 2:i % 2 + 1]).then_inc(e2_ready, 1)
                    if i >= 1:
                        turned(i - 1)
                turned(ST - 1)
                act.wait_ge(u2_ready, h + KT + 1)
                act.activation(RH[:, bass.ds(h, 1), :].rearrange("p o n -> p (o n)"), oz[:, :], ACT.Copy) \
                   .then_inc(u2h_ready, 1)
            for k in range(KT):
                n = B2_ATT + 2 * k
                act.wait_ge(tile_done, n + 1)
                if k >= 2:
                    taken(act, n + 1 - 4)
                take(act.activation(t2[:, k % 2, :], bank[n % RING][:, :], ACT.Sigmoid, bias=col("b_gate_2", KT + k)),
                     n)
                act.wait_ge(u2_ready, 2 * KT + k + 1)
                act.activation(GH[:, k, :], P2[:, k % 2, :], ACT.Copy).then_inc(u2h_ready, 1)
            squares(6, lambda k: taken(act, B2_O + k))
            root(6, 1)
            for q in range(2 * ST):
                t, b = q // 2, q % 2
                act.wait_ge(y_T, q + 1)
                act.activation(y_tok[:, t, b * S:(b + 1) * S], bank[5 + b][:, :], ACT.Copy).then_inc(y_ready2, 1)

        @block.vector
        def _(dve):
            lane = Lane(dve, vec_step)

            def step(ins):
                lane.step(ins)
                lane.settle()

            for primed in (comb_ready, ol_ready, down_taken):
                dve.sem_inc(primed, PRIMED)
            dve.memset(mean_w[:, :], 1.0 / D).then_inc(setup_done, 1)
            dve.memset(eps[:, 0:1], LN_EPS).then_inc(setup_done, 1)
            dve.memset(eps[:, 1:2], RMS_EPS).then_inc(setup_done, 1)
            dve.wait_ge(par_T, 1)
            for r, rows in enumerate(STAGE_ROWS):
                dve.tensor_copy(par[:, r * P:r * P + rows], bank[7][:, r * P:r * P + rows]).then_inc(par_ready, 1)
            dve.wait_ge(c_hi, 1)
            dve.tensor_tensor(c_rest[:, :, :], c_act[:, :, :], c_head[:, :, :], ALU.subtract).then_inc(c_lo, 1)
            for k in range(KT):
                dve.wait_ge(x_T, k + 1)
                dve.tensor_copy(H[:, k, :], bank[5 + k % 2][:, :]).then_inc(y_ready, 1)

            def mod_taken(lo, hi):
                for n in range(lo, hi):
                    dve.wait_ge(tile_done, n + 1)
                    take(dve.tensor_tensor(mod[:, n:n + 1], bank[n % RING][:, 0:1], col("b_mod_2", n), ALU.add), n)

            def centre(L):
                dve.wait_ge(mean_done, L + 1)
                for k in range(KT):
                    dve.tensor_tensor(H[:, k, :], H[:, k, :], bank[3][:, :], ALU.subtract).then_inc(d_ready, 1)

            def invert(L):
                dve.wait_ge(std_ready, L + 1)
                dve.reciprocal(rstd[:, :], rstd[:, :]).then_inc(rs_ready, 1)
                dve.wait_ge(rs_ready, L + 1)

            def layer_norm(L, split_=True, between=None):
                centre(L)
                if between:
                    between()
                invert(L)
                for k in range(KT):
                    dve.tensor_tensor(H[:, k, :], H[:, k, :], rstd[:, :], ALU.mult).then_inc(xn_ready, 1)
                if split_:
                    for k in range(KT):
                        dve.wait_ge(hh_ready, KT * L + k + 1)
                        dve.tensor_tensor(HL[:, k, :], H[:, k, :], HH[:, k, :], ALU.subtract).then_inc(hl_ready, 1)

            layer_norm(0, between=lambda: mod_taken(0, 9))
            mod_taken(9, N_MOD)

            def mixer(l):
                n0 = BASE_MIX[l]
                if l == 1:
                    dve.wait_ge(tile_done, BASE_MIX[1])
                step(dve.memset(A2[:, :, 2, :], 0.0))
                for kv in range(2):
                    c = WHERE["cmp_pos"] + (2 * l + kv) * CMP_PAIRS
                    step(dve.tensor_copy(A2[:, kv, 2, 0:CMP_PAIRS], par[:, c:c + CMP_PAIRS]))
                for t in range(4):
                    n = n0 + 7 + t
                    dve.wait_ge(tile_done, n + 1)
                    take(dve.tensor_copy(Q[:, t, :], bank[n % RING][:, :]), n)
                for b in range(2):
                    dve.wait_ge(vg_T, 3 * l + b + 1)
                    dve.tensor_copy(V[:, b, :, :], bank[5 + b][:, :].rearrange("p (t n) -> p t n", n=P)) \
                       .then_inc(vg_ready, 1)
                dve.wait_ge(vg_T, 3 * l + 3)
                dve.tensor_copy(GA[:, :, :, :], bank[7][:, 0:ST * 24].rearrange("p (t b h) -> p t b h", b=3, h=HEADS)) \
                   .then_inc(vg_ready, 1)
                dve.wait_ge(vg_ready, 3 * l + 3)
                step(dve.tensor_scalar(GA[:, 0, 0, :], GA[:, 0, 0, :], cst[:, K_VALID:K_VALID + 1], None, ALU.mult))
                dve.wait_ge(dup_c, 64 * (l + 1))
                for kv in range(2):
                    for q in range(2):
                        rows = slice(64 * q, 64 * q + 64)
                        ins = dve.tensor_copy(A2[rows, kv, 0:2, :], K4[rows, kv, :, q:S:2])
                        if kv == 1 and q == 1:
                            ins.then_inc(a2_ready, 1)
                        else:
                            step(ins)
                for j in range(4):
                    dve.wait_ge(hid_done, 4 * l + j + 1)
                    dve.tensor_tensor(bsum[:, j:j + 1], bank[3 + j][:, 2 * NCMP:2 * NCMP + 1],
                                      col("cmp_b1", 4 * l + j), ALU.add).then_inc(bsum_ready, 1)
                dve.wait_ge(kcvc_done, l + 1)
                dve.tensor_scalar(KC[:, :, :], bank[7][:, 0:2 * NCMP].rearrange("p (g n) -> p g n", g=2),
                                  col("b2dup", l), None, ALU.add).then_inc(kcvc_ready, 1)
                dve.tensor_tensor(VC[:, :, :], bank[7][0:NCMP, 64:64 + 2 * HD].rearrange("p (g d) -> p g d", g=2),
                                  b2row[:, :].unsqueeze(1).broadcast_to((NCMP, 2, HD)), ALU.add) \
                   .then_inc(kcvc_ready, 1)
                dve.wait_ge(gelu_ready, 4 * (l + 1))
                dve.wait_ge(kcvc_ready, 2 * (l + 1))
                step(dve.memset(zpad[:, :, 0:2], 0.0))
                for c in range(4):
                    n = n0 + 11 + 3 * c
                    r = c % 2
                    taken(dve, n)
                    dve.wait_ge(tile_done, n + 2)
                    take(dve.tensor_tensor(zpad[:, r, 2:2 + S], t_cg[:, r, :], bank[(n + 1) % RING][:, :], ALU.mult),
                         n + 1)
                    taken(dve, n + 1)
                    w = [col("conv_w", 12 * l + 4 * i + c) for i in range(3)]
                    step(dve.tensor_scalar(cy[:, r, :], zpad[:, r, 0:S], w[0], None, ALU.mult))
                    for i in (1, 2):
                        step(dve.scalar_tensor_tensor(out=cy[:, r, :], in0=zpad[:, r, i:i + S], scalar=w[i],
                                                      in1=cy[:, r, :], op0=ALU.mult, op1=ALU.add))
                    dve.wait_ge(tile_done, n + 3)
                    take(dve.tensor_tensor(cy[:, r, :], cy[:, r, :], bank[(n + 2) % RING][:, :], ALU.mult), n + 2)
                    dve.wait_ge(mixh_ready, 4 * l + c + 1)
                    dve.tensor_tensor(ML[:, 4 + c, :], cy[:, r, :], MH[:, 4 + c, :], ALU.subtract) \
                       .then_inc(mixl_ready, 1)
                dve.wait_ge(mixl_ready, 4 * (l + 1))
                attention(l)
                for k in range(KT):
                    n = n0 + N_PROJ + k
                    dve.wait_ge(tile_done, n + 1)
                    take(dve.scalar_tensor_tensor(out=H[:, k, :], in0=H[:, k, :], scalar=ALPHA,
                                                  in1=bank[n % RING][:, :], op0=ALU.mult, op1=ALU.add), n)

            def attention(l):
                step(dve.memset(QC[64:128, 0, :], 0.0))
                step(dve.memset(QC[0:64, 1, :], 0.0))
                with lane.loop(4, 1 + 7 * 8) as t:
                    u0 = 8 * t + 32 * l
                    dve.wait_ge(s_done, PRIMED + u0)
                    lane.step(dve.tensor_copy(QC[0:64, 0, :], Q[0:64, bass.ds(t, 1), :].rearrange("p o n -> p (o n)")))
                    dve.tensor_copy(QC[64:128, 1, :], Q[64:128, bass.ds(t, 1), :].rearrange("p o n -> p (o n)")) \
                       .then_inc(q_ready, 1)

                    def maxima(v):
                        w = (v // 2 + 1) * P
                        dve.wait_ge(s_done, PRIMED + u0 + v + 1)
                        for j, src in enumerate((bank[7][:, 0:NCMP], bank[3 + v % 2][:, 0:w],
                                                 bank[5 + v % 2][:, 0:w])):
                            lane.step(dve.tensor_reduce(mx[:, j:j + 1], src, AX.X, ALU.max))
                        lane.settle()
                        dve.tensor_scalar(nb[:, v % 2, :], mx[:, :], -SCALE1, None, ALU.mult).then_inc(max_ready, 1)

                    def rest_out(i):
                        dve.wait_ge(oh_ready, 4 * t + 16 * l + i + 1)
                        dve.tensor_tensor(ML[:, bass.ds(t, 1), i * P:(i + 1) * P].rearrange("p o n -> p (o n)"),
                                          bank[2][:, 0:P],
                                          MH[:, bass.ds(t, 1), i * P:(i + 1) * P].rearrange("p o n -> p (o n)"),
                                          ALU.subtract).then_inc(ol_ready, 1)

                    maxima(0)
                    for v in range(8):
                        i, r = v // 2, v % 2
                        if v < 7:
                            dve.wait_ge(max_ready, u0 + v + 1)
                            maxima(v + 1)
                        if r == 0 and v > 0:
                            rest_out(i - 1)
                        dve.wait_ge(exp_ready, PRIMED + 3 * (u0 + v + 1))
                        step(dve.reciprocal(rz[:, :], Z[:, r, :]))
                        lane.step(dve.tensor_tensor(fac[:, :], rz[:, :],
                                                    GA[:, i, :, bass.ds(2 * t + r, 1)].rearrange("p b o -> p (b o)"),
                                                    ALU.mult))
                        dve.wait_ge(t_done, u0 + v + 1)
                        dve.tensor_copy(PTc[:, :], bank[2][0:NCMP, 0:P]).then_inc(ptw_ready, 1)
                        dve.tensor_copy(PTw[:, 0:i + 1, :], bank[1][:, 0:(i + 1) * P]
                                        .rearrange("p (k q) -> p k q", q=P)).then_inc(ptw_ready, 1)
                        lane.settle()
                        dve.wait_ge(pv_done, PRIMED + u0 + v + 1)
                        o = ot[:, r * HD:(r + 1) * HD]
                        step(dve.tensor_scalar(o, bank[2][:, 0:HD], fac[:, 0:1], None, ALU.mult))
                        step(dve.scalar_tensor_tensor(out=o, in0=bank[2][:, HD:2 * HD], scalar=fac[:, 1:2],
                                                      in1=o, op0=ALU.mult, op1=ALU.add))
                        dve.scalar_tensor_tensor(out=o, in0=bank[2][:, 2 * HD:3 * HD], scalar=fac[:, 2:3],
                                                 in1=o, op0=ALU.mult, op1=ALU.add).then_inc(comb_ready, 1)
                    rest_out(3)

            def router():
                dve.wait_ge(lg_done, 1)
                dve.tensor_copy(lgT[:, :], bank[5][0:EXPERTS, :]).then_inc(lg_ready, 1)
                dve.wait_ge(lg_done, 2)
                step(dve.tensor_copy(lg[:, :, :], bank[6][:, 0:ST * EXPERTS].rearrange("p (t e) -> p t e", e=EXPERTS)))
                step(dve.tensor_reduce(top[:, :], lg[:, :, :], AX.X, ALU.max))
                flat = lg[:, :, :].rearrange("p t e -> p (t e)")
                for t in range(ST):
                    rows = slice(t * EXPERTS, (t + 1) * EXPERTS)
                    other = lg[:, t, :].unsqueeze(1).broadcast_to((P, EXPERTS, EXPERTS))
                    own = lg[:, t, :].unsqueeze(2).broadcast_to((P, EXPERTS, EXPERTS))
                    step(dve.tensor_tensor(gt8[:, rows, :], other, own, ALU.is_gt))
                    step(dve.tensor_tensor(eq8[:, rows, :], other, own, ALU.is_equal))
                    step(dve.tensor_tensor(eq8[:, rows, :], eq8[:, rows, :],
                                           cst[:, K_PAIR:K_ALL].rearrange("p (e j) -> p e j", j=EXPERTS), ALU.mult))
                step(dve.tensor_tensor(gt8[:, :, :], gt8[:, :, :], eq8[:, :, :], ALU.add))
                step(dve.tensor_reduce(sel[:, :, :].rearrange("p t e -> p (t e)"), gt8[:, :, :], AX.X, ALU.add))
                step(dve.tensor_scalar(sel[:, :, :], sel[:, :, :], 2.0, None, ALU.is_lt))
                dve.tensor_tensor(lg[:, :, :], lg[:, :, :], top[:, :].unsqueeze(2).broadcast_to((P, ST, EXPERTS)),
                                  ALU.subtract).then_inc(lg_ready, 1)
                dve.wait_ge(router_exp, 1)
                step(dve.tensor_tensor(ex[:, :, :], ex[:, :, :], sel[:, :, :], ALU.mult))
                step(dve.tensor_reduce(top[:, :], ex[:, :, :], AX.X, ALU.add))
                step(dve.reciprocal(top[:, :], top[:, :]))
                dve.tensor_tensor(ex[:, :, :], ex[:, :, :], top[:, :].unsqueeze(2).broadcast_to((P, ST, EXPERTS)),
                                  ALU.mult).then_inc(lg_ready, 1)
                dve.wait_ge(lg_done, 3)
                dve.tensor_copy(lgT[:, :], bank[5][0:EXPERTS, :]).then_inc(lg_ready, 1)
                for e in range(EXPERTS):
                    dve.wait_ge(lg_done, 4 + e)
                    dve.tensor_copy(GB[:, e, :], bank[6 + e % 2][:, :]).then_inc(gate_ready, 1)

            def ffn(l):
                n0 = BASE_FFN[l]
                if l == 1:
                    router()
                dve.wait_ge(hl_ready, KT * (2 * l + 2))
                for k in range(KT):
                    lane.step(dve.tensor_scalar(H[:, k, :], H[:, k, :], ALPHA, None, ALU.mult))
                lane.settle()
                if l == 1:
                    dve.wait_ge(gate_ready, EXPERTS)
                with dve.Fori(0, PARTS[l]) as e:
                    turn = e * (N_PART // RING)

                    def taken_here(n):
                        dve.wait_ge(bank_free[n % RING], turn + n // RING + 1)

                    for j in range(PT):
                        n = n0 + 2 * j
                        q = PT * e + PT * DENSE_PARTS * l
                        taken_here(n)
                        dve.wait_ge(tile_done, e * N_PART + n + 2)
                        if j >= 2:
                            dve.wait_ge(ul_ready, q + j - 1)
                        take(dve.tensor_tensor(gu[:, j % 2, :], silu_g[:, j % 2, :], bank[(n + 1) % RING][:, :],
                                               ALU.mult), n + 1)
                        dve.wait_ge(uh_ready, q + j + 1)
                        dve.tensor_tensor(UL[:, j, :], gu[:, j % 2, :], UH[:, j, :], ALU.subtract) \
                           .then_inc(ul_ready, 1)
                    for k in range(KT):
                        n = n0 + 2 * PT + k
                        dve.wait_ge(tile_done, e * N_PART + n + 1)
                        if l == 0:
                            take(dve.tensor_tensor(H[:, k, :], H[:, k, :], bank[n % RING][:, :], ALU.add), n)
                        else:
                            if k < 2:
                                dve.wait_ge(ul_ready, q + PT)
                            dve.wait_ge(down_taken, PRIMED + e * KT + max(k - 1, 0))
                            take(dve.tensor_tensor(gu[:, k % 2, :], bank[n % RING][:, :],
                                                   GB[:, bass.ds(e, 1), :].rearrange("p o n -> p (o n)"), ALU.mult), n)
                            taken_here(n)
                            dve.tensor_tensor(H[:, k, :], H[:, k, :], gu[:, k % 2, :], ALU.add) \
                               .then_inc(down_taken, 1)

            for l in range(DEPTH):
                mixer(l)
                layer_norm(2 * l + 1)
                ffn(l)
                layer_norm(2 * l + 2, split_=(l == 0))

            dve.wait_ge(h_ready, 5 * KT)
            step(dve.scalar_tensor_tensor(out=modg[:, :], in0=mod[:, KT:2 * KT], scalar=1.0,
                                          in1=par[:, WHERE["g_norm_2"]:WHERE["g_norm_2"] + KT],
                                          op0=ALU.add, op1=ALU.mult))
            lam = par[:, WHERE["lam_2"]:WHERE["lam_2"] + KT]
            L8 = [lamc[:, j, :] for j in range(8)]
            step(dve.tensor_scalar(L8[2], lam, -1.0, None, ALU.mult))
            dve.tensor_tensor(L8[0], lam, L8[2], ALU.max).then_inc(lam_abs, 1)
            invert(5)
            for k in range(KT):
                if k >= 2:
                    dve.wait_ge(hh_ready, 4 * KT + k - 1)
                dve.tensor_tensor(t2[:, k % 2, :], H[:, k, :], rstd[:, :], ALU.mult).then_inc(xn_ready, 1)
                dve.wait_ge(xn_ready, 5 * KT + k + 1)
                step(dve.tensor_scalar(IX[:, k, :], t2[:, k % 2, :], modg[:, k:k + 1], mod[:, k:k + 1],
                                       ALU.mult, ALU.add))
                dve.wait_ge(hh_ready, 4 * KT + k + 1)
                dve.tensor_tensor(HL[:, k, :], IX[:, k, :], HH[:, k, :], ALU.subtract).then_inc(hl_ready, 1)
            dve.wait_ge(lam_exp, 1)
            step(dve.tensor_scalar(L8[3], L8[1], 2.0, None, ALU.add))
            step(dve.reciprocal(L8[3], L8[3]))
            step(dve.tensor_tensor(L8[4], L8[1], L8[3], ALU.mult))
            step(dve.tensor_tensor(L8[5], L8[4], L8[4], ALU.mult))
            step(dve.tensor_scalar(L8[6], L8[5], 1.0 / 17, None, ALU.mult))
            for odd in (15, 13, 11, 9, 7, 5, 3):
                step(dve.scalar_tensor_tensor(out=L8[6], in0=L8[6], scalar=1.0 / odd, in1=L8[5],
                                              op0=ALU.add, op1=ALU.mult))
            step(dve.scalar_tensor_tensor(out=L8[6], in0=L8[6], scalar=1.0, in1=L8[4], op0=ALU.add, op1=ALU.mult))
            step(dve.tensor_scalar(L8[2], L8[2], 0.0, None, ALU.max))
            step(dve.scalar_tensor_tensor(out=L8[7], in0=L8[6], scalar=2.0, in1=L8[2], op0=ALU.mult, op1=ALU.add))
            step(dve.tensor_scalar(L8[6], L8[7], -8.0, None, ALU.mult))
            step(dve.tensor_scalar(L8[7], L8[7], 8.0, None, ALU.mult))
            dve.wait_ge(b2_landed, 48)
            step(dve.tensor_scalar(keep[:, :], posi[:, :], 0, None, ALU.not_equal))
            step(dve.tensor_scalar(drop[:, :], posi[:, :], 0, None, ALU.is_equal))
            step(dve.tensor_scalar(ang[:, :], posi[0:ROT, :], cst[0:ROT, K_FREQ:K_FREQ + 1], None, ALU.mult))
            two_pi = [6.28125, 0.0019350051879882812, 2 * np.pi - 6.28125 - 0.0019350051879882812]
            for o, quarter in ((sinT, 0.0), (cosT, np.pi / 2)):
                step(dve.tensor_scalar(turns[:, :], ang[:, :], quarter, 1 / (2 * np.pi), ALU.add, ALU.mult))
                step(dve.tensor_copy(turnf[:, :], turns[:, :]))
                step(dve.scalar_tensor_tensor(out=o[:, :], in0=turnf[:, :], scalar=-two_pi[0], in1=ang[:, :],
                                              op0=ALU.mult, op1=ALU.add))
                for part in two_pi[1:]:
                    step(dve.scalar_tensor_tensor(out=o[:, :], in0=turnf[:, :], scalar=-part, in1=o[:, :],
                                                  op0=ALU.mult, op1=ALU.add))
                step(dve.tensor_scalar(o[:, :], o[:, :], quarter, None, ALU.add))
                dve.tensor_scalar(o[:, :], o[:, :], 3.1415925, -3.1415925, ALU.min, ALU.max).then_inc(ang_ready, 1)

            step(dve.memset(xpad[:, 0:3], 0.0))

            def gated(k):
                dve.wait_ge(ri_ready, 2 * k + 2)
                dve.tensor_tensor(IX[:, k, :], IX[:, k, :], XC[:, k, :], ALU.mult).then_inc(ix_ready, 1)

            for k in range(KT):
                taken(dve, B2_X + k)
                w = [col("conv_w_2", KT * i + k) for i in range(4)]
                step(dve.tensor_scalar(XC[:, k, :], xpad[:, 0:S], w[0], col("conv_b_2", k), ALU.mult, ALU.add))
                for i in (1, 2, 3):
                    ins = dve.scalar_tensor_tensor(out=XC[:, k, :], in0=xpad[:, i:i + S], scalar=w[i],
                                                   in1=XC[:, k, :], op0=ALU.mult, op1=ALU.add)
                    if i < 3:
                        step(ins)
                ins.then_inc(xc_ready, 1)
                if k >= 1:
                    gated(k - 1)
            gated(KT - 1)
            for k in range(KT):
                dve.wait_ge(decay_ready, 2 * k + 2)
                step(dve.tensor_tensor(la2[:, :], XC[:, k, :], XC[:, k, :], ALU.mult))
                dve.scalar_tensor_tensor(out=R[:, k, :], in0=la2[:, :], scalar=1.0, in1=lt[:, k % 2, :],
                                         op0=ALU.add, op1=ALU.mult).then_inc(lru_q, 1)
                dve.wait_ge(lru_q, k + 1)
                step(dve.tensor_tensor(XC[:, k, :], XC[:, k, :], keep[:, :], ALU.mult))

            def gated_state(k):
                taken(dve, B2_Z + k)
                if k >= 2:
                    dve.wait_ge(u2l_ready, k - 1)
                dve.tensor_tensor(t2[:, k % 2, :], R[:, k, :], XC[:, k, :], ALU.mult).then_inc(u2_ready, 1)
                dve.wait_ge(u2h_ready, k + 1)
                dve.tensor_tensor(RL[:, k, :], t2[:, k % 2, :], RH[:, k, :], ALU.subtract).then_inc(u2l_ready, 1)

            for k in range(KT):
                dve.wait_ge(root_ready, k + 1)
                step(dve.tensor_tensor(R[:, k, :], R[:, k, :], keep[:, :], ALU.mult))
                step(dve.tensor_tensor(R[:, k, :], R[:, k, :], drop[:, :], ALU.add))
                step(dve.tensor_tensor(IX[:, k, :], IX[:, k, :], R[:, k, :], ALU.mult))
                dve.tensor_tensor_scan(out=R[:, k, :], data0=XC[:, k, :], data1=IX[:, k, :], initial=0.0,
                                       op0=ALU.mult, op1=ALU.add).then_inc(hr_ready, 1)
                dve.wait_ge(hr_ready, k + 1)
                if k >= 1:
                    gated_state(k - 1)
            gated_state(KT - 1)
            for k in range(KT):
                n = B2_RNN + 2 * k
                taken(dve, n)
                dve.wait_ge(tile_done, n + 2)
                take(dve.tensor_tensor(M[:, k, :], t2[:, k % 2, :], bank[(n + 1) % RING][:, :], ALU.mult), n + 1)
            taken(dve, B2_RNN + 2 * KT - 1)
            with lane.loop(HEADS, 2 * 2 + 2 * ST) as h:
                for j, x in enumerate((qh, kh)):
                    dve.wait_ge(rot_done, 2 * h + j + 1)
                    lane.step(dve.tensor_tensor(t2[0:ROT, 0, :], bank[3 + j][0:ROT, :], sinT[:, :], ALU.mult))
                    lane.step(dve.tensor_tensor(t2[0:ROT, 1, :], x[0:ROT, :], cosT[:, :], ALU.mult))
                    lane.settle()
                    dve.tensor_tensor(x[0:ROT, :], t2[0:ROT, 0, :], t2[0:ROT, 1, :], ALU.add).then_inc(rope_ready, 1)
                    dve.wait_ge(rope_ready, 2 * h + j + 1)
                dve.wait_ge(v2_done, h + 1)
                dve.tensor_copy(V2[:, :, :], bank[5][:, :].rearrange("p (t n) -> p t n", n=P)).then_inc(v2_ready, 1)

                def maxima2(i):
                    w = (i + 1) * P
                    dve.wait_ge(s2_done, 4 * h + i + 1)
                    step(dve.tensor_reduce(m2[:, i % 2:i % 2 + 1], bank[6 + i % 2][:, 0:w], AX.X, ALU.max))
                    dve.tensor_scalar(n2[:, i % 2:i % 2 + 1], m2[:, i % 2:i % 2 + 1], -SCALE2, None, ALU.mult) \
                       .then_inc(m2_ready, 1)

                maxima2(0)
                for i in range(ST):
                    w = (i + 1) * P
                    if i < ST - 1:
                        maxima2(i + 1)
                    dve.wait_ge(e2_ready, 4 * h + i + 1)
                    step(dve.reciprocal(r2[:, i % 2:i % 2 + 1], z2[:, i % 2:i % 2 + 1]))
                    dve.tensor_scalar(P2[:, i % 2, 0:w], P2[:, i % 2, 0:w], r2[:, i % 2:i % 2 + 1], None, ALU.mult) \
                       .then_inc(p2_ready, 1)
                dve.wait_ge(pv2_done, PRIMED + 4 * h + ST)
                dve.wait_ge(u2l_ready, h + KT)
                dve.tensor_tensor(oz[:, :], bank[4][:, :], XC[:, bass.ds(h, 1), :].rearrange("p o n -> p (o n)"),
                                  ALU.mult).then_inc(u2_ready, 1)
                dve.wait_ge(u2h_ready, h + KT + 1)
                dve.tensor_tensor(RL[:, bass.ds(h, 1), :].rearrange("p o n -> p (o n)"), oz[:, :],
                                  RH[:, bass.ds(h, 1), :].rearrange("p o n -> p (o n)"), ALU.subtract) \
                   .then_inc(u2l_ready, 1)
            for k in range(KT):
                n = B2_ATT + 2 * k
                taken(dve, n)
                dve.wait_ge(tile_done, n + 2)
                if k >= 2:
                    dve.wait_ge(u2l_ready, 2 * KT + k - 1)
                take(dve.tensor_tensor(P2[:, k % 2, :], t2[:, k % 2, :], bank[(n + 1) % RING][:, :], ALU.mult), n + 1)
                taken(dve, n + 1)
                dve.tensor_tensor(P2[:, k % 2, :], P2[:, k % 2, :], M[:, k, :], ALU.add).then_inc(u2_ready, 1)
                dve.wait_ge(u2h_ready, 2 * KT + k + 1)
                dve.tensor_tensor(GL[:, k, :], P2[:, k % 2, :], GH[:, k, :], ALU.subtract).then_inc(u2l_ready, 1)
            for k in range(KT):
                n = B2_O + k
                dve.wait_ge(tile_done, n + 1)
                take(dve.scalar_tensor_tensor(out=H[:, k, :], in0=bank[n % RING][:, :],
                                              scalar=mod[:, 2 * KT + k:2 * KT + k + 1], in1=H[:, k, :],
                                              op0=ALU.mult, op1=ALU.add), n)
            invert(6)
            for k in range(KT):
                dve.scalar_tensor_tensor(out=H[:, k, :], in0=H[:, k, :], scalar=col("g_final_2", k), in1=rstd[:, :],
                                         op0=ALU.mult, op1=ALU.mult).then_inc(xn_ready, 1)


_INS = ["x", "ln_in_g", "ln_in_b", "w_in", "cmp_pos", "cmp_w1", "cmp_b1", "cmp_w2", "cmp_b2", "conv_w", "w_o",
        "ln1_g", "ln1_b", "ln2_g", "ln2_b", "ffn_wg", "ffn_wu", "ffn_wd", "moe_router", "moe_wg", "moe_wu",
        "moe_wd", "c_2", "positions_2", "g_norm_2", "w_mod_2", "b_mod_2", "w_in_2", "b_gate_2", "conv_w_2",
        "conv_b_2", "w_a_2", "b_a_2", "w_x_2", "b_x_2", "lam_2", "w_out_rnn_2", "w_out_attn_2", "w_o_2",
        "g_final_2"]


def kernel(**inputs):
    import concourse.bacc as _bacc
    from concourse.bass_utils import run_bass_kernel_spmd as _run

    nc = _bacc.Bacc("TRN2", target_bir_lowering=False, num_devices=1)
    arrays, args = {}, {}
    for name in _INS + ["consts"]:
        v = constant_table() if name == "consts" else np.ascontiguousarray(inputs[name])
        arrays[f"in_{name}_dram"] = v
        args[name] = nc.dram_tensor(f"in_{name}_dram", v.shape, mybir.dt.from_np(v.dtype),
                                    kind="ExternalInput").ap()
    out = nc.dram_tensor("out_0_dram", (1, S, D), F32, kind="ExternalOutput").ap()
    build(nc, args, out)
    r = _run(nc, [arrays], core_ids=[0])
    return r.results[0]["out_0_dram"]
```

```python
from contextlib import ExitStack, contextmanager

import numpy as np

import concourse.bass as bass
from concourse import mybir

F32 = mybir.dt.float32
F32R = mybir.dt.float32r
I32 = mybir.dt.int32
ALU = mybir.AluOpType
ACT = mybir.ActivationFunctionType
AX = mybir.AxisListType

P = 128
S = 512
D = 1024
KT = D // P
ST = S // P
DEPTH = 2
HEADS = 8
GROUPS = 2
HD = 64
ATTN_W = HEADS * HD
KV_W = GROUPS * HD
CONV_CH = D - ATTN_W
NCMP = S // 16 - 1
CMP_PAIRS = 16
ALPHA = float((2 * DEPTH) ** 0.25)
LN_EPS = 1e-5
RMS_EPS = 1e-6
NEG = -1e30
D_PART = 1408
PT = D_PART // P
DENSE_PARTS = 2
EXPERTS = 8
SCALE1 = HD ** -0.5
HD2 = 128
SCALE2 = HD2 ** -0.5
ROT = 32
RING = 3
PRIMED = 1

C_Q, C_KC, C_VC, C_KS, C_VS, C_KW, C_VW = 0, 512, 640, 768, 896, 1024, 1152
C_GATES = C_VW + KV_W
C_U = C_GATES + 3 * HEADS
C_BG = C_U + CONV_CH
C_CG = C_BG + CONV_CH

K_ID = 0
K_CAUSAL = K_ID + P
K_CMP = K_CAUSAL + P
K_VALID = K_CMP + ST * NCMP
K_DIL = K_VALID + 1
K_ROT = K_DIL + S
K_FREQ = K_ROT + P
K_PAIR = K_FREQ + 1
K_ALL = K_PAIR + EXPERTS * EXPERTS

VECTORS = [("ln_in_g", 8), ("ln_in_b", 8), ("ln1_g", 16), ("ln1_b", 16), ("ln2_g", 16), ("ln2_b", 16),
           ("cmp_b1", 8), ("conv_w", 24), ("b2dup", DEPTH),
           ("g_norm_2", 8), ("b_mod_2", 24), ("b_gate_2", 16), ("conv_w_2", 32),
           ("conv_b_2", 8), ("b_a_2", 8), ("b_x_2", 8), ("lam_2", 8), ("g_final_2", 8), ("c_2", 8),
           ("cmp_pos", 64)]
FIRST_OF = {"g_norm_2": 1, "cmp_pos": 2}


def vector_places():
    where, stage, row = {}, 0, 0
    for name, rows in VECTORS:
        if name in FIRST_OF:
            stage, row = FIRST_OF[name], 0
        where[name] = stage * P + row
        row += rows
        assert row <= P
    return where


def stage_rows():
    used = [0, 0, 0]
    for name, rows in VECTORS:
        used[WHERE[name] // P] = WHERE[name] % P + rows
    return used


def vector_sources(a, name):
    v = a[name]
    if name == "cmp_pos":
        return v.rearrange("l v (t q) d -> (l v t) (q d)", q=2)
    if name in ("b_a_2", "b_x_2"):
        return v.rearrange("l k p -> (l k) p")
    form = {1: "(k p) -> k p", 2: "l (k p) -> (l k) p", 3: "l v (k p) -> (l v k) p"}[len(v.shape)]
    return v.rearrange(form, p=P)


WHERE = vector_places()
STAGE_ROWS = stage_rows()
STAGED = len(VECTORS) - 1 + 2 * DEPTH

N_MOD = 24
N_PROJ = 7 + 4 + 12
N_MIX = N_PROJ + KT
N_PART = 2 * PT + KT
BASE_MIX = [N_MOD, N_MOD + N_MIX + DENSE_PARTS * N_PART]
BASE_FFN = [b + N_MIX for b in BASE_MIX]
PARTS = [DENSE_PARTS, EXPERTS]
BASE_2 = BASE_FFN[1] + EXPERTS * N_PART
B2_X = BASE_2
B2_Z = B2_X + KT
B2_RNN = B2_Z + KT
B2_ZA = B2_RNN + 2 * KT
B2_HEAD = B2_ZA + KT
B2_ATT = B2_HEAD + 3 * HEADS
B2_O = B2_ATT + 2 * KT
N_ALL = B2_O + KT


def constant_table():
    t = np.zeros((P, K_ALL), np.float32)
    p = np.arange(P)[:, None]
    j = np.arange(P)[None, :]
    t[:, K_ID:K_ID + P] = (p == j)
    t[:, K_CAUSAL:K_CAUSAL + P] = np.where(j <= p, 0.0, NEG)
    for i in range(ST):
        ends = np.arange(NCMP)[None, :] * 16 + 31
        t[:, K_CMP + i * NCMP:K_CMP + (i + 1) * NCMP] = np.where(ends <= i * P + p, 0.0, NEG)
    t[:, K_VALID] = (p[:, 0] >= 31)
    dist = p + (S - P) - np.arange(S)[None, :]
    count = ((dist >= 0) & (dist <= 128)).astype(np.float64) + ((dist >= 0) & (dist % 4 == 0)) \
        + ((dist >= 0) & (dist % 16 == 0))
    t[:, K_DIL:K_DIL + S] = np.where(count > 0, np.log(np.maximum(count, 1)) / SCALE2, NEG)
    half = ROT // 2
    for i in range(half):
        t[i + half, K_ROT + i] = -1.0
        t[i, K_ROT + i + half] = 1.0
    freq = np.float32(500000.0) ** (-np.arange(0, ROT, 2, dtype=np.float32) / np.float32(ROT))
    t[:ROT, K_FREQ] = np.concatenate([freq, freq])
    e = np.arange(EXPERTS)
    t[:, K_PAIR:] = (e[None, :] < e[:, None]).astype(np.float32).reshape(1, -1)
    return t


class Lane:

    def __init__(self, eng, sem):
        self.eng, self.sem, self.n, self.turn = eng, sem, 0, 0

    def step(self, ins):
        ins.then_inc(self.sem, 1)
        self.n += 1

    def settle(self):
        self.eng.wait_ge(self.sem, self.turn + self.n)

    @contextmanager
    def loop(self, count, per):
        with self.eng.Fori(0, count) as i:
            before, outer = self.n, self.turn
            self.turn = outer + i * per
            yield i
            assert self.n == before + per, (self.n - before, per)
            self.turn = outer
        self.n = before + per * count


def build(nc, a, out, stop=None):
    with ExitStack() as ctx:
        def sb(name, shape, dt=F32, stack=ctx):
            return stack.enter_context(nc.sbuf_tensor(name, shape, dt))

        def sem(name):
            return ctx.enter_context(nc.semaphore(name))

        bank = [ctx.enter_context(nc.psum_tensor(f"bank{b}", [P, 512], F32)) for b in range(8)]

        raw = [sb(f"raw{r}", [P, PT, P]) for r in range(RING)]
        head = [sb(f"head{r}", [P, PT, P], F32R) for r in range(RING)]
        rest = [sb(f"rest{r}", [P, PT, P], F32R) for r in range(RING)]
        cst = sb("cst", [P, K_ALL])
        par = sb("par", [P, 3 * P])
        H = sb("H", [P, KT, S])
        HH = sb("HH", [P, KT, S], F32R)
        HL = sb("HL", [P, KT, S], F32R)
        mean_w = sb("mean_w", [P, P])
        eps = sb("eps", [P, 2])
        sq = sb("sq", [P, 2, S])
        rstd = sb("rstd", [P, S])
        mod = sb("mod", [P, N_MOD])
        c_act = sb("c_act", [P, KT, 2])
        c_head = sb("c_head", [P, KT, 2], F32R)
        c_rest = sb("c_rest", [P, KT, 2], F32R)
        ident = cst[:, K_ID:K_ID + P]
        causal = cst[:, K_CAUSAL:K_CAUSAL + P]

        with ExitStack() as s:
            x_tok = sb("x_tok", [P, ST, D], stack=s)
            stage = sb("stage", [P, 3, P], stack=s)
        with ExitStack() as s:
            K4 = sb("K4", [P, 4, GROUPS, S], stack=s)
            V = sb("V", [P, 2, ST, P], stack=s)
            GA = sb("GA", [P, ST, 3, HEADS], stack=s)
            KC = sb("KC", [P, GROUPS, NCMP], stack=s)
            VC = sb("VC", [NCMP, GROUPS, HD], stack=s)
            Q = sb("Q", [P, 4, S], stack=s)
            with ExitStack() as s2:
                W1 = sb("W1", [P, 2, CMP_PAIRS, 256], stack=s2)
            with ExitStack() as s2:
                MH = sb("MH", [P, KT, S], F32R, stack=s2)
                ML = sb("ML", [P, KT, S], F32R, stack=s2)
            s.enter_context(nc.sbuf_tensor("mix_place", [P, 2 * KT, S], F32))
            with ExitStack() as s2:
                VT = sb("VT", [P, 2, S], stack=s2)
                GT = sb("GT", [3 * HEADS, S], stack=s2)
                A2 = sb("A2", [P, 2, 3, S // 2], stack=s2)
                W2 = sb("W2", [P, 2, 2, P], stack=s2)
                b2row = sb("b2row", [NCMP, HD], stack=s2)
                bsum = sb("bsum", [P, 4], stack=s2)
                HG = sb("HG", [P, 2, 2, GROUPS * NCMP], stack=s2)
            with ExitStack() as s2:
                QC = sb("QC", [P, 2, S], stack=s2)
                Cc = sb("Cc", [P, 2, ST, NCMP], stack=s2)
                Psw = sb("Psw", [P, 2, 2, S], stack=s2)
                PTsw = sb("PTsw", [P, 2, 2, ST, P], stack=s2)
                mxc = sb("mxc", [P, HEADS, ST], stack=s2)
                mx = sb("mx", [P, 2], stack=s2)
                nb = sb("nb", [P, 2, 2], stack=s2)
                Z = sb("Z", [P, 2, 2], stack=s2)
                rz = sb("rz", [P, 2], stack=s2)
                fac = sb("fac", [P, 2], stack=s2)
                ot = sb("ot", [P, P], stack=s2)
                t_cg = sb("t_cg", [P, S], stack=s2)
                zpad = sb("zpad", [P, 2 + S], stack=s2)
                cy = sb("cy", [P, S], stack=s2)
            Pcm = K4[:, 0, :, :].rearrange("p g n -> p (g n)")[:, 0:HEADS * ST * NCMP] \
                .rearrange("p (h i n) -> p h i n", h=HEADS, n=NCMP)
            PTc = K4[0:NCMP, 1, :, :].rearrange("p g (a q) -> p (g a) q", q=P)
        with ExitStack() as s:
            UH = sb("UH", [P, PT, S], F32R, stack=s)
            UL = sb("UL", [P, PT, S], F32R, stack=s)
            silu_g = sb("silu_g", [P, 2, S], stack=s)
            gu = sb("gu", [P, 2, S], stack=s)
            GB = sb("GB", [P, EXPERTS, S], stack=s)
            rw = sb("rw", [P, KT, EXPERTS], stack=s)
            lgT = sb("lgT", [EXPERTS, S], stack=s)
            lg = sb("lg", [P, ST, EXPERTS], stack=s)
            gt8 = sb("gt8", [P, ST * EXPERTS, EXPERTS], stack=s)
            eq8 = sb("eq8", [P, ST * EXPERTS, EXPERTS], stack=s)
            sel = sb("sel", [P, ST, EXPERTS], stack=s)
            top = sb("top", [P, ST], stack=s)
            ex = sb("ex", [P, ST, EXPERTS], stack=s)
        with ExitStack() as s:
            with ExitStack() as s2:
                XC = sb("XC", [P, KT, S], stack=s2)
                IX = sb("IX", [P, KT, S], stack=s2)
                R = sb("R", [P, KT, S], stack=s2)
                M = sb("M", [P, KT, S], stack=s2)
            with ExitStack() as s2:
                GH = sb("GH", [P, KT, S], F32R, stack=s2)
                RH = sb("RH", [P, KT, S], F32R, stack=s2)
                RL = sb("RL", [P, KT, S], F32R, stack=s2)
                GL = sb("GL", [P, KT, S], F32R, stack=s2)
            s.enter_context(nc.sbuf_tensor("three_places", [P, 3 * KT, S], F32))
            with ExitStack() as s2:
                with ExitStack() as s3:
                    WA = sb("WA", [P, 2, KT, P], stack=s3)
                    xpad = sb("xpad", [P, 3 + S], stack=s3)
                with ExitStack() as s3:
                    lt = sb("lt", [P, 2, S], stack=s3)
                    la2 = sb("la2", [P, S], stack=s3)
                s2.enter_context(nc.sbuf_tensor("wa_place", [P, 2 * KT * P + S + 4], F32))
                keep = sb("keep", [P, S], stack=s2)
                drop = sb("drop", [P, S], stack=s2)
            s.enter_context(nc.sbuf_tensor("m_place", [P, KT, S], F32))
            modg = sb("modg", [P, KT], stack=s)
            lamc = sb("lamc", [P, 8, KT], stack=s)
            t2 = sb("t2", [P, 2, S], stack=s)
            cosT = sb("cosT", [ROT, S], stack=s)
            sinT = sb("sinT", [ROT, S], stack=s)
            with ExitStack() as s2:
                posi = sb("posi", [P, S], I32, stack=s2)
                ang = sb("ang", [ROT, S], stack=s2)
                turns = sb("turns", [ROT, S], I32, stack=s2)
                turnf = sb("turnf", [ROT, S], stack=s2)
            with ExitStack() as s2:
                qh = sb("qh", [P, S], stack=s2)
                kh = sb("kh", [P, S], stack=s2)
                vh = sb("vh", [P, S], stack=s2)
                V2 = sb("V2", [P, ST, P], stack=s2)
                P2 = sb("P2", [P, 2, S], stack=s2)
                PT2 = sb("PT2", [P, ST, P], stack=s2)
                m2 = sb("m2", [P, 2], stack=s2)
                n2 = sb("n2", [P, 2], stack=s2)
                z2 = sb("z2", [P, 2], stack=s2)
                r2 = sb("r2", [P, 2], stack=s2)
                oz = sb("oz", [P, S], stack=s2)
        with ExitStack() as s:
            y_tok = sb("y_tok", [P, ST, D], stack=s)

        sem_cst = sem("constants_landed")
        sem_stage = sem("vectors_landed")
        sem_x = sem("x_landed")
        raw_landed = [sem(f"raw_landed{r}") for r in range(RING)]
        head_done = sem("head_done")
        weights_split = sem("weights_split")
        tile_done = sem("tile_done")
        bank_free = [sem(f"bank_free{b}") for b in range(RING)]
        vec_step = sem("vec_step")
        act_step = sem("act_step")
        setup_done = sem("setup_done")
        par_T = sem("par_transposed")
        par_ready = sem("par_ready")
        c_hi = sem("c_head_ready")
        c_lo = sem("c_rest_ready")
        x_T = sem("x_transposed")
        y_ready = sem("y_ready")
        mean_done = sem("mean_done")
        d_ready = sem("d_ready")
        sq_ready = sem("sq_ready")
        sq_used = sem("sq_used")
        std_ready = sem("std_ready")
        rs_ready = sem("rs_ready")
        xn_ready = sem("xn_ready")
        h_ready = sem("h_ready")
        hh_ready = sem("hh_ready")
        hl_ready = sem("hl_ready")
        w1_landed = sem("w1_landed")
        dup_c = sem("dup_cmp")
        dup_s = sem("dup_sel_win")
        vg_T = sem("vg_transposed")
        vg_ready = sem("vg_ready")
        a2_ready = sem("a2_ready")
        hid_done = sem("hidden_done")
        bsum_ready = sem("bsum_ready")
        gelu_ready = sem("gelu_ready")
        kcvc_done = sem("kcvc_done")
        kcvc_ready = sem("kcvc_ready")
        mixh_ready = sem("mixh_ready")
        mixl_ready = sem("mixl_ready")
        q_ready = sem("q_ready")
        s_done = sem("scores_done")
        max_ready = sem("max_ready")
        exp_ready = sem("exp_ready")
        t_done = sem("probs_transposed")
        cs_done = sem("cmp_scores_done")
        cx_ready = sem("cmp_shifted_ready")
        ce_ready = sem("cmp_exp_ready")
        cp_ready = sem("cmp_probs_ready")
        tc_done = sem("cmp_transposed")
        tc_ready = sem("cmp_transposed_taken")
        ps_ready = sem("probs_scaled")
        pts_ready = sem("pts_ready")
        ptw_ready = sem("ptw_ready")
        pv_done = sem("pv_done")
        comb_ready = sem("combined_ready")
        ot_done = sem("out_transposed")
        oh_ready = sem("att_head_ready")
        ol_ready = sem("att_rest_ready")
        silu_ready = sem("silu_ready")
        uh_ready = sem("uh_ready")
        ul_ready = sem("ul_ready")
        down_taken = sem("down_taken")
        rw_landed = sem("router_landed")
        lg_done = sem("logits_done")
        lg_ready = sem("logits_ready")
        gate_ready = sem("gate_ready")
        b2_landed = sem("block2_landed")
        xc_ready = sem("xc_ready")
        ri_done = sem("ri_done")
        ri_ready = sem("ri_ready")
        ix_ready = sem("ix_ready")
        decay_ready = sem("decay_ready")
        lam_abs = sem("lam_abs_ready")
        lam_exp = sem("lam_exp_ready")
        router_exp = sem("router_exp_ready")
        lru_q = sem("lru_q_ready")
        root_ready = sem("root_ready")
        hr_ready = sem("hr_ready")
        zs_ready = sem("zs_ready")
        u2_ready = sem("u2_ready")
        u2h_ready = sem("u2h_ready")
        u2l_ready = sem("u2l_ready")
        sg_ready = sem("sigmoid_ready")
        ang_ready = sem("angles_ready")
        tab_ready = sem("tables_ready")
        rot_done = sem("rotation_done")
        rope_ready = sem("rope_ready")
        v2_done = sem("v2_done")
        v2_ready = sem("v2_ready")
        s2_done = sem("scores2_done")
        m2_ready = sem("max2_ready")
        e2_ready = sem("exp2_ready")
        p2_ready = sem("p2_ready")
        t2_done = sem("t2_done")
        pt2_ready = sem("pt2_ready")
        pv2_done = sem("pv2_done")
        y_T = sem("y_transposed")
        y_ready2 = sem("y_tok_ready")
        y_out = sem("y_out")

        block = ctx.enter_context(nc.Block())

        def col(name, k):
            c = WHERE[name] + k
            return par[:, c:c + 1]

        def slab(w, c):
            return w[:, c:c + P].rearrange("(k p) n -> p k n", p=P)

        def taken(eng, n):
            eng.wait_ge(bank_free[n % RING], n // RING + 1)

        def take(ins, n):
            ins.then_inc(bank_free[n % RING], 1)

        @block.sync
        def _(sp):
            def load(n, src, kt=KT):
                if not isinstance(n, int) or n >= RING:
                    sp.wait_ge(weights_split, n - (RING - 1))
                sp.dma_start(raw[slot][:, 0:kt, :], src).then_inc(raw_landed[slot], 16)

            sp.dma_start(cst[:, :], a["consts"]).then_inc(sem_cst, 16)
            sp.dma_start(x_tok[:, :, :], a["x"].rearrange("b (t p) d -> p (b t) d", p=P)).then_inc(sem_x, 16)
            for n in range(N_MOD):
                slot = n % RING
                load(n, slab(a["w_mod_2"][0], n * P))
            for l in range(DEPTH):
                w = a["w_in"][l]
                order = [C_KC, C_VC, C_KS, C_KW, C_VS, C_VW, C_GATES] + [C_Q + P * t for t in range(4)]
                for t in range(4):
                    order += [C_CG + P * t, C_U + P * t, C_BG + P * t]
                for k, c in enumerate(order):
                    slot = (BASE_MIX[l] + k) % RING
                    load(BASE_MIX[l] + k, slab(w, c))
                for k in range(KT):
                    n = BASE_MIX[l] + N_PROJ + k
                    slot = n % RING
                    load(n, slab(a["w_o"][l], k * P))
                with sp.Fori(0, PARTS[l]) as e:
                    for j in range(N_PART):
                        n = BASE_FFN[l] + e * N_PART + j
                        slot = (BASE_FFN[l] + j) % RING
                        if j < 2 * PT:
                            m = j // 2
                            if l == 0:
                                w = a["ffn_wg" if j % 2 == 0 else "ffn_wu"]
                                src = w[0].rearrange("(k p) n -> p k n", p=P)[:, :, bass.ds(e * D_PART + m * P, P)]
                            else:
                                w = a["moe_wg" if j % 2 == 0 else "moe_wu"]
                                src = w[0, bass.ds(e, 1), :, m * P:(m + 1) * P] \
                                    .rearrange("o (k p) n -> p (o k) n", p=P)
                            load(n, src)
                        else:
                            m = j - 2 * PT
                            if l == 0:
                                src = a["ffn_wd"][0].rearrange("(e k p) n -> e p k n", p=P, k=PT)[
                                    bass.ds(e, 1), :, :, m * P:(m + 1) * P].rearrange("o p k n -> (o p) k n")
                            else:
                                src = a["moe_wd"][0, bass.ds(e, 1), :, m * P:(m + 1) * P] \
                                    .rearrange("o (k p) n -> p (o k) n", p=P)
                            load(n, src, PT)
            w2 = a["w_in_2"][0]
            order = [(w2, k * P) for k in range(2 * KT)]
            for k in range(KT):
                order += [(w2, 6 * D + k * P), (a["w_out_rnn_2"][0], k * P)]
            order += [(w2, 5 * D + k * P) for k in range(KT)]
            for h in range(HEADS):
                order += [(w2, 2 * D + h * P), (w2, 3 * D + h * P), (w2, 4 * D + h * P)]
            for k in range(KT):
                order += [(w2, 7 * D + k * P), (a["w_out_attn_2"][0], k * P)]
            order += [(a["w_o_2"][0], k * P) for k in range(KT)]
            assert len(order) == N_ALL - BASE_2
            for k, (w, c) in enumerate(order):
                slot = (BASE_2 + k) % RING
                load(BASE_2 + k, slab(w, c))
            for t in range(ST):
                sp.wait_ge(y_ready2, 2 * (t + 1))
                sp.dma_start(out[0, t * P:(t + 1) * P, :], y_tok[:, t, :]).then_inc(y_out, 16)
            sp.wait_ge(y_out, 16 * ST)

        @block.gpsimd
        def _(pool):
            def split(n, slot, kt):
                pool.wait_ge(head_done, n + 1)
                pool.tensor_tensor(rest[slot][:, 0:kt, :], raw[slot][:, 0:kt, :], head[slot][:, 0:kt, :],
                                   ALU.subtract).then_inc(weights_split, 1)

            def run(n0, count, kt=KT):
                turns_, left = count // RING, count % RING
                first = 0
                if n0 == 0:
                    for j in range(RING):
                        split(j, j, kt)
                    first = RING
                    turns_ -= 1
                if turns_ > 0:
                    with pool.Fori(0, turns_) as i:
                        for j in range(RING):
                            n = n0 + first + j
                            slot = n % RING
                            split(i * RING + n, slot, kt)
                for j in range(left):
                    n = n0 + first + turns_ * RING + j
                    split(n, n % RING, kt)

            run(0, BASE_FFN[0])
            for l in range(DEPTH):
                with pool.Fori(0, PARTS[l]) as e:
                    for j in range(N_PART):
                        n = BASE_FFN[l] + j
                        slot = n % RING
                        split(e * N_PART + n, slot, KT if j < 2 * PT else PT)
                if l == 0:
                    run(BASE_MIX[1], N_MIX)
            run(BASE_2, N_ALL - BASE_2)

        @block.tensor
        def _(pe):
            def tile(n, hi, lo, kt=KT, cols=S, use=None, ready=None):
                static = n if isinstance(n, int) else use[0]
                slot = static % RING
                pe.wait_ge(weights_split, n + 1)
                if static >= RING:
                    pe.wait_ge(bank_free[slot], static // RING if isinstance(n, int) else use[1])
                last = None
                for k in range(kt):
                    if ready:
                        ready(k)
                    for w, act, first, final in ((head, hi, True, False), (head, lo, False, False),
                                                 (rest, hi, False, True)):
                        last = pe.matmul(bank[slot][:, 0:cols], w[slot][:, k, :], act[:, k, 0:cols],
                                         start=(k == 0 and first), stop=(k == kt - 1 and final))
                last.then_inc(tile_done, 1)

            def tiles(n0, count, hi, lo, ready=None):
                done = 0
                if ready:
                    tile(n0, hi, lo, ready=ready)
                    done = 1
                turns_ = (count - done) // RING
                if turns_ > 1:
                    with pe.Fori(0, turns_) as i:
                        for j in range(RING):
                            n = n0 + done + j
                            tile(i * RING + n, hi, lo, use=(n, i + n // RING))
                    done += turns_ * RING
                for j in range(done, count):
                    tile(n0 + j, hi, lo)

            def mean(L, ready):
                for k in range(KT):
                    ready(k)
                    last = pe.matmul(bank[3][:, :], mean_w[:, :], H[:, k, :], start=(k == 0), stop=(k == KT - 1))
                last.then_inc(mean_done, 1)

            def var(L):
                for k in range(KT):
                    pe.wait_ge(sq_ready, KT * L + k + 1)
                    pe.matmul(bank[4][:, :], mean_w[:, :], sq[:, k % 2, :], start=(k == 0),
                              stop=(k == KT - 1)).then_inc(sq_used, 1)

            def mod_tiles(lo, hi):
                for n in range(lo, hi):
                    tile(n, c_head, c_rest, cols=2)

            for primed in (s_done, pv_done, pv2_done):
                pe.sem_inc(primed, PRIMED)
            pe.wait_ge(sem_cst, 16)
            pe.wait_ge(sem_stage, 16 * STAGED)
            pe.wait_ge(setup_done, 3)
            for r, rows in enumerate(STAGE_ROWS):
                last = pe.transpose(bank[7][:, r * P:r * P + rows], stage[0:rows, r, :], cst[0:rows, K_ID:K_ID + rows])
            last.then_inc(par_T, 1)
            pe.wait_ge(sem_x, 16)
            for k in range(KT):
                if k >= 2:
                    pe.wait_ge(y_ready, k - 1)
                for t in range(ST):
                    last = pe.transpose(bank[5 + k % 2][:, t * P:(t + 1) * P], x_tok[:, t, k * P:(k + 1) * P], ident)
                last.then_inc(x_T, 1)
            mean(0, lambda k: pe.wait_ge(y_ready, k + 1))
            pe.wait_ge(c_lo, 1)
            mod_tiles(0, 9)
            var(0)
            mod_tiles(9, N_MOD)

            def mixer(l):
                n0 = BASE_MIX[l]
                tiles(n0, 11, HH, HL, ready=lambda k: pe.wait_ge(hl_ready, KT * 2 * l + k + 1))
                for b in range(2):
                    taken(pe, n0 + 4 + b)
                    for t in range(ST):
                        last = pe.transpose(bank[5 + b][:, t * P:(t + 1) * P], VT[:, b, t * P:(t + 1) * P], ident)
                    last.then_inc(vg_T, 1)
                taken(pe, n0 + 6)
                for t in range(ST):
                    last = pe.transpose(bank[7][:, t * 24:(t + 1) * 24], GT[:, t * P:(t + 1) * P],
                                        cst[0:24, K_ID:K_ID + 24])
                last.then_inc(vg_T, 1)
                pe.wait_ge(w1_landed, 16 * 7 * (l + 1))
                pe.wait_ge(a2_ready, l + 1)
                pe.wait_ge(vg_ready, 3 * l + 3)
                for kv in range(2):
                    for m in range(2):
                        b = bank[3 + 2 * kv + m]
                        for tp in range(CMP_PAIRS):
                            last = pe.matmul(b[:, 0:3 * NCMP].rearrange("p (g n) -> p g n", g=3),
                                             W1[:, kv, tp, m * P:(m + 1) * P],
                                             A2[:, kv, :, tp:tp + 8 * (NCMP - 1) + 1:8],
                                             start=(tp == 0), stop=(tp == CMP_PAIRS - 1))
                        last.then_inc(hid_done, 1)
                pe.wait_ge(gelu_ready, 4 * (l + 1))
                for m in range(2):
                    pe.matmul(bank[7][:, 0:2 * NCMP], W2[:, 0, m, :], HG[:, 0, m, :], start=(m == 0), stop=(m == 1))
                for g in range(GROUPS):
                    for m in range(2):
                        last = pe.matmul(bank[7][0:NCMP, 64 + g * HD:64 + (g + 1) * HD],
                                         HG[:, 1, m, g * NCMP:(g + 1) * NCMP], W2[:, 1, m, 0:HD],
                                         start=(m == 0), stop=(m == 1))
                last.then_inc(kcvc_done, 1)
                attention(l)
                pe.wait_ge(mixl_ready, 4 * (l + 1))
                pe.wait_ge(ol_ready, PRIMED + 16 * (l + 1))
                tiles(n0 + N_PROJ, KT, MH, ML)
                mean(2 * l + 1, lambda k: taken(pe, n0 + N_PROJ + k))
                var(2 * l + 1)

            def attention(l):
                n0 = BASE_MIX[l] + 11
                pe.wait_ge(kcvc_ready, 2 * (l + 1))
                for t in range(4):
                    taken(pe, n0 - 4 + t)
                for h in [0, 2, 4, 6, 1, 3, 5, 7]:
                    rows = slice(HD * (h % 2), HD * (h % 2) + HD)
                    for i in range(ST):
                        c = ((h // 2) * ST + i) * NCMP
                        last = pe.matmul(bank[3 + h % 2][:, c:c + NCMP], Q[rows, h // 2, i * P:(i + 1) * P],
                                         KC[rows, h // 4, :], start=True, stop=True)
                last.then_inc(cs_done, 1)
                pe.wait_ge(cx_ready, 2 * (l + 1))
                pe.wait_ge(dup_s, 64 * (l + 1))

                with pe.Fori(0, 4) as t:
                    g = t // 2
                    u0 = 8 * t + 32 * l

                    def scores(v):
                        i = v // 2
                        w = (i + 1) * P
                        if v == 0:
                            pe.wait_ge(q_ready, t + 4 * l + 1)
                        pe.wait_ge(exp_ready, PRIMED + 2 * (u0 + v))
                        lhs = QC[:, v % 2, i * P:(i + 1) * P]
                        for b, kind in ((3, 2), (4, 3)):
                            pe.matmul(bank[b][:, 0:w], lhs,
                                      K4[:, kind, bass.ds(g, 1), 0:w].rearrange("p o n -> p (o n)"),
                                      start=True, stop=False)
                            last = pe.matmul(bank[b][:, i * P:w], ident, causal, start=False, stop=True)
                        last.then_inc(s_done, 1)

                    def compressed_turn():
                        for r in range(2):
                            for i in range(ST):
                                last = pe.transpose(bank[5 + r][0:NCMP, i * P:(i + 1) * P], Cc[:, r, i, :], ident)
                        last.then_inc(tc_done, 1)

                    def piece(v):
                        for z in range(3 * v, 3 * v + 3):
                            j, k = z // KT, z % KT
                            slot = (n0 + j) % RING
                            if k == 0:
                                pe.wait_ge(weights_split, 3 * t + n0 + j + 1)
                                pe.wait_ge(bank_free[slot], t + (n0 + j) // RING)
                            for w, x in ((head, HH), (head, HL), (rest, HH)):
                                last = pe.matmul(bank[slot][:, :], w[slot][:, k, :], x[:, k, :],
                                                 start=(k == 0 and w is head and x is HH),
                                                 stop=(k == KT - 1 and w is rest))
                            if k == KT - 1:
                                last.then_inc(tile_done, 1)

                    def turn(v):
                        i = v // 2
                        pe.wait_ge(ps_ready, u0 + v + 1)
                        if v == 0:
                            pe.wait_ge(tc_ready, t + 4 * l + 1)
                        else:
                            pe.wait_ge(pts_ready, PRIMED + u0 + v)
                            pe.wait_ge(ptw_ready, u0 + v)
                        for b in range(2):
                            for k in range(i + 1):
                                last = pe.transpose(bank[5 + b][:, k * P:(k + 1) * P],
                                                    Psw[:, v % 2, b, k * P:(k + 1) * P], ident)
                        last.then_inc(t_done, 1)

                    def values(v):
                        i, r = v // 2, v % 2
                        pe.wait_ge(ptw_ready, u0 + v + 1)
                        pe.wait_ge(pts_ready, PRIMED + u0 + v + 1)
                        if v == 0:
                            pe.wait_ge(tc_ready, t + 4 * l + 1)
                        if r == 0:
                            pe.wait_ge(ol_ready, PRIMED + 4 * t + 16 * l + i)
                        o = bank[7][:, r * HD:(r + 1) * HD]
                        for b in range(2):
                            for k in range(i + 1):
                                pe.matmul(o, PTsw[:, v % 2, b, k, :], V[:, b, k, bass.ds(g * HD, HD)],
                                          start=(b == 0 and k == 0), stop=False)
                        pe.matmul(o, PTc[:, ST * r + i, :], VC[:, bass.ds(g, 1), :].rearrange("p o n -> p (o n)"),
                                  start=False, stop=True).then_inc(pv_done, 1)

                    def out_turn(i):
                        pe.wait_ge(comb_ready, 4 * t + 16 * l + i + 1)
                        pe.transpose(bank[7][:, P:2 * P], ot[:, :], ident).then_inc(ot_done, 1)

                    scores(0)
                    compressed_turn()
                    for v in range(8):
                        if v < 7:
                            scores(v + 1)
                        if v >= 3 and v % 2 == 1:
                            out_turn((v - 3) // 2)
                        piece(v)
                        turn(v)
                        if v > 0:
                            values(v - 1)
                    values(7)
                    out_turn(3)

            def ffn(l):
                n0 = BASE_FFN[l]
                L = 2 * l + 1
                pe.wait_ge(hl_ready, KT * (L + 1))
                if l == 1:
                    router()
                with pe.Fori(0, PARTS[l]) as e:
                    for j in range(2 * PT):
                        tile(e * N_PART + n0 + j, HH, HL, use=(n0 + j, e * (N_PART // RING) + (n0 + j) // RING))
                    for j in range(KT):
                        n = n0 + 2 * PT + j

                        def ready(k, j=j):
                            if j == 0:
                                pe.wait_ge(ul_ready, PT * e + PT * l * DENSE_PARTS + k + 1)
                        tile(e * N_PART + n, UH, UL, kt=PT, use=(n, e * (N_PART // RING) + n // RING), ready=ready)
                if l == 0:
                    mean(L + 1, lambda k: taken(pe, BASE_MIX[1] - KT + k))
                else:
                    mean(L + 1, lambda k: pe.wait_ge(down_taken, PRIMED + KT * (EXPERTS - 1) + k + 1))
                var(L + 1)

            def router():
                pe.wait_ge(rw_landed, 16)
                for k in range(KT):
                    last = pe.matmul(bank[5][0:EXPERTS, :], rw[:, k, :], H[:, k, :], start=(k == 0), stop=(k == KT - 1))
                last.then_inc(lg_done, 1)
                pe.wait_ge(lg_ready, 1)
                for t in range(ST):
                    last = pe.transpose(bank[6][:, t * EXPERTS:(t + 1) * EXPERTS], lgT[:, t * P:(t + 1) * P],
                                        cst[0:EXPERTS, 0:EXPERTS])
                last.then_inc(lg_done, 1)
                pe.wait_ge(lg_ready, 3)
                for t in range(ST):
                    last = pe.transpose(bank[5][0:EXPERTS, t * P:(t + 1) * P], ex[:, t, :], ident)
                last.then_inc(lg_done, 1)
                pe.wait_ge(lg_ready, 4)
                for e in range(EXPERTS):
                    if e >= 2:
                        pe.wait_ge(gate_ready, e - 1)
                    pe.matmul(bank[6 + e % 2][:, :], cst[0:EXPERTS, e:e + 1].broadcast_to((EXPERTS, P)), lgT[:, :],
                              start=True, stop=True).then_inc(lg_done, 1)

            for l in range(DEPTH):
                mixer(l)
                ffn(l)

            var(5)
            pe.wait_ge(b2_landed, 48)

            def lru_gates(k):
                pe.wait_ge(xc_ready, k + 1)
                for b in range(2):
                    if k >= 1:
                        pe.wait_ge(ri_ready, 2 * (k - 1) + b + 1)
                    pe.matmul(bank[5 + b][:, :], WA[:, b, k, :], XC[:, k, :], start=True, stop=True) \
                      .then_inc(ri_done, 1)

            for k in range(KT):
                tile(B2_X + k, HH, HL,
                     ready=(lambda j: pe.wait_ge(hl_ready, 4 * KT + j + 1)) if k == 0 else None)
                if k >= 1:
                    lru_gates(k - 1)
            lru_gates(KT - 1)
            tiles(B2_Z, KT, HH, HL)
            for k in range(KT):
                tile(B2_RNN + 2 * k, HH, HL)
                pe.wait_ge(u2l_ready, KT)
                tile(B2_RNN + 2 * k + 1, RH, RL)
            tiles(B2_ZA, KT, HH, HL)
            with pe.Fori(0, HEADS) as h:
                for j in range(3):
                    n = B2_HEAD + j
                    tile(h * 3 + n, HH, HL, use=(n, h + n // RING))
                for j, src in ((0, qh), (1, kh)):
                    pe.wait_ge(bank_free[(B2_HEAD + j) % RING], h + (B2_HEAD + j) // RING + 1)
                    if j == 1:
                        pe.wait_ge(u2_ready, KT + h)
                    pe.matmul(bank[3 + j][:, :], cst[:, K_ROT:K_ROT + P], src[:, :], start=True,
                              stop=True).then_inc(rot_done, 1)
                pe.wait_ge(bank_free[(B2_HEAD + 2) % RING], h + (B2_HEAD + 2) // RING + 1)
                for t in range(ST):
                    last = pe.transpose(bank[5][:, t * P:(t + 1) * P], vh[:, t * P:(t + 1) * P], ident)
                last.then_inc(v2_done, 1)
                pe.wait_ge(rope_ready, 2 * h + 2)

                def scores2(i):
                    w = (i + 1) * P
                    if i >= 2:
                        pe.wait_ge(e2_ready, 4 * h + i - 1)
                    pe.matmul(bank[6 + i % 2][:, 0:w], qh[:, i * P:w], kh[:, 0:w], start=True, stop=False)
                    pe.matmul(bank[6 + i % 2][:, 0:w], ident, cst[:, K_DIL + (3 - i) * P:K_DIL + S], start=False,
                              stop=True).then_inc(s2_done, 1)

                scores2(0)
                pe.wait_ge(v2_ready, h + 1)
                for i in range(ST):
                    if i < ST - 1:
                        scores2(i + 1)
                    pe.wait_ge(p2_ready, 4 * h + i + 1)
                    if i >= 1:
                        pe.wait_ge(pt2_ready, 4 * h + i)
                    for k in range(i + 1):
                        last = pe.transpose(bank[5][:, k * P:(k + 1) * P], P2[:, i % 2, k * P:(k + 1) * P], ident)
                    last.then_inc(t2_done, 1)
                    pe.wait_ge(pt2_ready, 4 * h + i + 1)
                    for k in range(i + 1):
                        last = pe.matmul(bank[4][:, i * P:(i + 1) * P], V2[:, k, :], PT2[:, k, :],
                                         start=(k == 0), stop=(k == i))
                    last.then_inc(pv2_done, 1)
            for k in range(KT):
                tile(B2_ATT + 2 * k, HH, HL)
                pe.wait_ge(u2l_ready, 2 * KT)
                tile(B2_ATT + 2 * k + 1, RH, RL)
            pe.wait_ge(u2l_ready, 3 * KT)
            tiles(B2_O, KT, GH, GL)
            var(6)
            for t in range(ST):
                for b in range(2):
                    q = 2 * t + b
                    pe.wait_ge(xn_ready, 7 * KT)
                    if q >= 2:
                        pe.wait_ge(y_ready2, q - 1)
                    for k in range(4):
                        last = pe.transpose(bank[5 + b][:, k * P:(k + 1) * P],
                                            H[:, 4 * b + k, t * P:(t + 1) * P], ident)
                    last.then_inc(y_T, 1)

        @block.scalar
        def _(act):
            lane = Lane(act, act_step)
            for primed in (exp_ready, pts_ready):
                act.sem_inc(primed, PRIMED)
            for name, rows in VECTORS:
                st, row = WHERE[name] // P, WHERE[name] % P
                if name == "b2dup":
                    for l in range(DEPTH):
                        for d in range(2):
                            act.dma_start(stage[row + l:row + l + 1, st, d * HD:(d + 1) * HD],
                                          a["cmp_b2"][l, 0:1, :]).then_inc(sem_stage, 16)
                else:
                    act.dma_start(stage[row:row + rows, st, :], vector_sources(a, name)).then_inc(sem_stage, 16)

            def compression_weights(l):
                for kv in range(2):
                    act.dma_start(W1[:, kv, :, :], a["cmp_w1"][l, kv].rearrange("(k p) n -> p k n", p=P)) \
                       .then_inc(w1_landed, 16)
                    for d in range(2):
                        act.dma_start(W2[:, kv, :, d * HD:(d + 1) * HD],
                                      a["cmp_w2"][l, kv].rearrange("(k p) n -> p k n", p=P)).then_inc(w1_landed, 16)
                act.dma_start(b2row[:, :], a["cmp_b2"][l, 1:2, :].broadcast_to((NCMP, HD))).then_inc(w1_landed, 16)

            def make_head(n, kt=KT, use=None):
                static = n if use is None else use[0]
                slot = static % RING
                landed = 16 * (static // RING + 1) if use is None else use[1]
                act.wait_ge(raw_landed[slot], landed)
                if static >= RING:
                    act.wait_ge(tile_done, n - (RING - 1))
                act.activation(head[slot][:, 0:kt, :], raw[slot][:, 0:kt, :], ACT.Copy).then_inc(head_done, 1)

            def heads_ahead(first, count):
                for n in range(first + 2, first + count + 2):
                    if n < N_ALL:
                        make_head(n)

            def squares(L, ready):
                for k in range(KT):
                    ready(k)
                    if KT * L + k >= 2:
                        act.wait_ge(sq_used, KT * L + k - 1)
                    act.activation(sq[:, k % 2, :], H[:, k, :], ACT.Square).then_inc(sq_ready, 1)

            def root(L, e):
                act.wait_ge(sq_used, KT * (L + 1))
                act.activation(rstd[:, :], bank[4][:, :], ACT.Sqrt, bias=eps[:, e:e + 1]).then_inc(std_ready, 1)

            def layer_norm(L, g, b, row, split_=True, after_centre=None):
                if after_centre:
                    after_centre()
                squares(L, lambda k: act.wait_ge(d_ready, KT * L + k + 1))
                root(L, 0)
                for k in range(KT):
                    act.wait_ge(xn_ready, KT * L + k + 1)
                    act.activation(H[:, k, :], H[:, k, :], ACT.Identity, bias=col(b, row + k),
                                   scale=col(g, row + k)).then_inc(h_ready, 1)
                    if split_:
                        act.wait_ge(h_ready, KT * L + k + 1)
                        act.activation(HH[:, k, :], H[:, k, :], ACT.Copy).then_inc(hh_ready, 1)

            make_head(0)
            make_head(1)
            act.wait_ge(par_ready, 3)
            act.wait_ge(setup_done, 3)
            for d in range(2):
                lane.step(act.activation(c_act[:, :, d], par[:, WHERE["c_2"]:WHERE["c_2"] + KT], ACT.Silu))
            lane.settle()
            act.activation(c_head[:, :, :], c_act[:, :, :], ACT.Copy).then_inc(c_hi, 1)
            layer_norm(0, "ln_in_g", "ln_in_b", 0, after_centre=lambda: heads_ahead(0, 9))
            heads_ahead(9, N_MOD - 9)
            for l in range(DEPTH):
                n0 = BASE_MIX[l]
                if l == 1:
                    act.wait_ge(tile_done, BASE_MIX[1])
                compression_weights(l)
                for kind in range(4):
                    n = n0 + kind
                    heads_ahead(n, 1)
                    act.wait_ge(tile_done, n + 1)
                    lane.step(act.activation(K4[0:64, kind, 0, :], bank[n % RING][0:64, :], ACT.Copy))
                    take(act.activation(K4[64:128, kind, 1, :], bank[n % RING][64:128, :], ACT.Copy), n)
                    lane.settle()
                    taken(act, n)
                    for g in range(GROUPS):
                        rows, other = slice(64 * g, 64 * g + 64), slice(64 - 64 * g, 128 - 64 * g)
                        act.dma_start(K4[other, kind, g, :], K4[rows, kind, g, :]) \
                           .then_inc(dup_c if kind < 2 else dup_s, 16)
                for b in range(2):
                    n = n0 + 4 + b
                    heads_ahead(n, 1)
                    act.wait_ge(tile_done, n + 1)
                    take(act.activation(VT[:, b, :], bank[n % RING][:, :], ACT.Copy), n)
                n = n0 + 6
                heads_ahead(n, 1)
                act.wait_ge(tile_done, n + 1)
                take(act.activation(GT[:, :], bank[n % RING][0:3 * HEADS, :], ACT.Sigmoid), n)
                heads_ahead(n0 + 7, 4)
                for kv in range(2):
                    for m in range(2):
                        j = 2 * kv + m
                        act.wait_ge(bsum_ready, 4 * l + j + 1)
                        act.activation(HG[:, kv, m, :], bank[3 + j][:, 0:2 * NCMP], ACT.Gelu_apprx_tanh,
                                       bias=bsum[:, j:j + 1]).then_inc(gelu_ready, 1)
                for b in range(2):
                    act.wait_ge(cx_ready, 2 * l + 2)
                    x = Pcm[:, 4 * b:4 * b + 4, :, :].rearrange("p h i n -> p (h i n)")
                    act.activation(x, x, ACT.Exp, scale=SCALE1).then_inc(ce_ready, 1)
                n0 = BASE_MIX[l] + 11
                with act.Fori(0, 4) as t:
                    u0 = 8 * t + 32 * l

                    def exps(v):
                        w = (v // 2 + 1) * P
                        act.wait_ge(max_ready, u0 + v + 1)
                        if v >= 2:
                            act.wait_ge(t_done, u0 + v - 1)
                        for b in range(2):
                            act.activation(Psw[:, v % 2, b, 0:w], bank[3 + b][:, 0:w], ACT.Exp,
                                           bias=nb[:, v % 2, b:b + 1], scale=SCALE1,
                                           accum_out=Z[:, v % 2, b:b + 1]).then_inc(exp_ready, 1)

                    def head_out(i):
                        act.wait_ge(ot_done, 4 * t + 16 * l + i + 1)
                        act.activation(MH[:, bass.ds(t, 1), i * P:(i + 1) * P].rearrange("p o n -> p (o n)"),
                                       bank[7][:, P:2 * P], ACT.Copy).then_inc(oh_ready, 1)

                    def head_of(j):
                        m = n0 + 2 + j
                        make_head(3 * t + m, use=(m, 16 * t + 16 * (m // RING + 1)))

                    exps(0)
                    for v in range(8):
                        i = v // 2
                        if v < 7:
                            exps(v + 1)
                        if v in (0, 3, 6):
                            head_of(v // 3)
                        if v == 3:
                            act.wait_ge(tile_done, 3 * t + n0 + 1)
                            take(act.activation(t_cg[:, :], bank[n0 % RING][:, :], ACT.Copy), n0)
                        if v >= 3 and v % 2 == 1:
                            head_out((v - 3) // 2)
                        act.wait_ge(t_done, u0 + v + 1)
                        act.wait_ge(pv_done, u0 + v - 1 + PRIMED)
                        act.activation(PTsw[:, v % 2, 0, 0:i + 1, :], bank[5][:, 0:(i + 1) * P]
                                       .rearrange("p (k q) -> p k q", q=P), ACT.Copy).then_inc(pts_ready, 1)
                    head_out(3)
                    act.wait_ge(bank_free[(n0 + 2) % RING], t + (n0 + 2) // RING + 1)
                    act.activation(MH[:, bass.ds(t + 4, 1), :].rearrange("p o n -> p (o n)"), cy[:, :],
                                   ACT.Copy).then_inc(mixh_ready, 1)
                heads_ahead(BASE_MIX[l] + N_PROJ, KT)
                layer_norm(2 * l + 1, "ln1_g", "ln1_b", KT * l)
                if l == 1:
                    act.dma_start(rw[:, :, :], a["moe_router"][0].rearrange("(k p) e -> p k e", p=P)) \
                       .then_inc(rw_landed, 16)
                    act.wait_ge(lg_ready, 2)
                    act.activation(ex[:, :, :], lg[:, :, :], ACT.Exp).then_inc(router_exp, 1)
                n0 = BASE_FFN[l]
                with act.Fori(0, PARTS[l]) as e:
                    def ahead(j):
                        m = n0 + j + 2
                        make_head(e * N_PART + m, PT if 2 * PT <= j + 2 < N_PART else KT,
                                  use=(m, 16 * (N_PART // RING) * e + 16 * (m // RING + 1)))

                    for j in range(PT):
                        n = n0 + 2 * j
                        ahead(2 * j)
                        act.wait_ge(tile_done, e * N_PART + n + 1)
                        take(act.activation(silu_g[:, j % 2, :], bank[n % RING][:, :], ACT.Silu), n)
                        ahead(2 * j + 1)
                        act.wait_ge(bank_free[(n + 1) % RING], e * (N_PART // RING) + (n + 1) // RING + 1)
                        act.activation(UH[:, j, :], gu[:, j % 2, :], ACT.Copy).then_inc(uh_ready, 1)
                    for j in range(2 * PT, N_PART):
                        ahead(j)
                layer_norm(2 * l + 2, "ln2_g", "ln2_b", KT * l, split_=(l == 0))

            squares(5, lambda k: act.wait_ge(h_ready, KT * 4 + k + 1))
            act.dma_start(WA[:, 0, :, :], a["w_a_2"][0].rearrange("k p n -> p k n")).then_inc(b2_landed, 16)
            act.dma_start(WA[:, 1, :, :], a["w_x_2"][0].rearrange("k p n -> p k n")).then_inc(b2_landed, 16)
            act.dma_start(posi[:, :], a["positions_2"].broadcast_to((P, S))).then_inc(b2_landed, 16)
            root(5, 1)
            for k in range(KT):
                act.wait_ge(xn_ready, 5 * KT + k + 1)
                act.activation(HH[:, k, :], t2[:, k % 2, :], ACT.Identity, bias=mod[:, k:k + 1],
                               scale=modg[:, k:k + 1]).then_inc(hh_ready, 1)
            act.wait_ge(lam_abs, 1)
            act.activation(lamc[:, 1, :], lamc[:, 0, :], ACT.Exp, scale=-1.0).then_inc(lam_exp, 1)
            for j, o in enumerate((sinT, cosT)):
                act.wait_ge(ang_ready, j + 1)
                act.activation(o[:, :], o[:, :], ACT.Sin).then_inc(tab_ready, 1)

            def conv_in(k):
                n = B2_X + k
                heads_ahead(n, 1)
                act.wait_ge(tile_done, n + 1)
                if k >= 1:
                    act.wait_ge(xc_ready, k)
                take(act.activation(xpad[:, 3:3 + S], bank[n % RING][:, :], ACT.Copy), n)

            conv_in(0)
            for k in range(KT):
                if k + 1 < KT:
                    conv_in(k + 1)
                for b, (o, bias) in enumerate(((R, "b_a_2"), (IX, "b_x_2"))):
                    act.wait_ge(ri_done, 2 * k + b + 1)
                    act.activation(o[:, k, :], bank[5 + b][:, :], ACT.Sigmoid, bias=col(bias, k)) \
                       .then_inc(ri_ready, 1)
            for k in range(KT):
                act.wait_ge(ix_ready, k + 1)
                act.activation(XC[:, k, :], R[:, k, :], ACT.Exp, scale=lamc[:, 6, k:k + 1]).then_inc(decay_ready, 1)
                if k >= 2:
                    act.wait_ge(lru_q, k - 1)
                act.activation(lt[:, k % 2, :], R[:, k, :], ACT.Tanh, scale=lamc[:, 7, k:k + 1]) \
                   .then_inc(decay_ready, 1)
            for k in range(KT):
                act.wait_ge(lru_q, k + 1)
                act.activation(R[:, k, :], R[:, k, :], ACT.Sqrt).then_inc(root_ready, 1)
            for k in range(KT):
                n = B2_Z + k
                heads_ahead(n, 1)
                act.wait_ge(tile_done, n + 1)
                act.wait_ge(hr_ready, k + 1)
                take(act.activation(XC[:, k, :], bank[n % RING][:, :], ACT.Silu), n)
                act.wait_ge(u2_ready, k + 1)
                act.activation(RH[:, k, :], t2[:, k % 2, :], ACT.Copy).then_inc(u2h_ready, 1)
            act.wait_ge(u2l_ready, KT)
            for k in range(KT):
                n = B2_RNN + 2 * k
                heads_ahead(n, 1)
                act.wait_ge(tile_done, n + 1)
                if k >= 2:
                    taken(act, n + 1 - 4)
                take(act.activation(t2[:, k % 2, :], bank[n % RING][:, :], ACT.Sigmoid, bias=col("b_gate_2", k)), n)
                heads_ahead(n + 1, 1)
            for k in range(KT):
                n = B2_ZA + k
                heads_ahead(n, 1)
                act.wait_ge(tile_done, n + 1)
                take(act.activation(XC[:, k, :], bank[n % RING][:, :], ACT.Silu), n)
            with act.Fori(0, HEADS) as h:
                for j, o in enumerate((qh, kh, vh)):
                    n = B2_HEAD + j
                    make_head(h * 3 + n + 2, use=(n + 2, 16 * h + 16 * ((n + 2) // RING + 1)))
                    act.wait_ge(tile_done, h * 3 + n + 1)
                    take(act.activation(o[:, :], bank[n % RING][:, :], ACT.Copy), n)

                def turned(i):
                    act.wait_ge(t2_done, 4 * h + i + 1)
                    act.wait_ge(pv2_done, PRIMED + 4 * h + i)
                    act.activation(PT2[:, 0:i + 1, :], bank[5][:, 0:(i + 1) * P].rearrange("p (k q) -> p k q", q=P),
                                   ACT.Copy).then_inc(pt2_ready, 1)

                for i in range(ST):
                    w = (i + 1) * P
                    act.wait_ge(m2_ready, 4 * h + i + 1)
                    if i >= 2:
                        act.wait_ge(t2_done, 4 * h + i - 1)
                    act.activation(P2[:, i % 2, 0:w], bank[6 + i % 2][:, 0:w], ACT.Exp, bias=n2[:, i % 2:i % 2 + 1],
                                   scale=SCALE2, accum_out=z2[:, i % 2:i % 2 + 1]).then_inc(e2_ready, 1)
                    if i >= 1:
                        turned(i - 1)
                turned(ST - 1)
                act.wait_ge(u2_ready, h + KT + 1)
                act.activation(RH[:, bass.ds(h, 1), :].rearrange("p o n -> p (o n)"), oz[:, :], ACT.Copy) \
                   .then_inc(u2h_ready, 1)
            for k in range(KT):
                n = B2_ATT + 2 * k
                heads_ahead(n, 1)
                act.wait_ge(tile_done, n + 1)
                if k >= 2:
                    taken(act, n + 1 - 4)
                take(act.activation(t2[:, k % 2, :], bank[n % RING][:, :], ACT.Sigmoid, bias=col("b_gate_2", KT + k)),
                     n)
                heads_ahead(n + 1, 1)
                act.wait_ge(u2_ready, 2 * KT + k + 1)
                act.activation(GH[:, k, :], P2[:, k % 2, :], ACT.Copy).then_inc(u2h_ready, 1)
            heads_ahead(B2_O, KT)
            squares(6, lambda k: taken(act, B2_O + k))
            root(6, 1)
            for q in range(2 * ST):
                t, b = q // 2, q % 2
                act.wait_ge(y_T, q + 1)
                act.activation(y_tok[:, t, b * S:(b + 1) * S], bank[5 + b][:, :], ACT.Copy).then_inc(y_ready2, 1)

        @block.vector
        def _(dve):
            lane = Lane(dve, vec_step)

            def step(ins):
                lane.step(ins)
                lane.settle()

            for primed in (ol_ready, down_taken):
                dve.sem_inc(primed, PRIMED)
            dve.memset(mean_w[:, :], 1.0 / D).then_inc(setup_done, 1)
            dve.memset(eps[:, 0:1], LN_EPS).then_inc(setup_done, 1)
            dve.memset(eps[:, 1:2], RMS_EPS).then_inc(setup_done, 1)
            dve.wait_ge(par_T, 1)
            for r, rows in enumerate(STAGE_ROWS):
                dve.tensor_copy(par[:, r * P:r * P + rows], bank[7][:, r * P:r * P + rows]).then_inc(par_ready, 1)
            dve.wait_ge(c_hi, 1)
            dve.tensor_tensor(c_rest[:, :, :], c_act[:, :, :], c_head[:, :, :], ALU.subtract).then_inc(c_lo, 1)
            for k in range(KT):
                dve.wait_ge(x_T, k + 1)
                dve.tensor_copy(H[:, k, :], bank[5 + k % 2][:, :]).then_inc(y_ready, 1)

            def mod_taken(lo, hi):
                for n in range(lo, hi):
                    dve.wait_ge(tile_done, n + 1)
                    take(dve.tensor_tensor(mod[:, n:n + 1], bank[n % RING][:, 0:1], col("b_mod_2", n), ALU.add), n)

            def centre(L):
                dve.wait_ge(mean_done, L + 1)
                for k in range(KT):
                    dve.tensor_tensor(H[:, k, :], H[:, k, :], bank[3][:, :], ALU.subtract).then_inc(d_ready, 1)

            def invert(L):
                dve.wait_ge(std_ready, L + 1)
                dve.reciprocal(rstd[:, :], rstd[:, :]).then_inc(rs_ready, 1)
                dve.wait_ge(rs_ready, L + 1)

            def layer_norm(L, split_=True, between=None):
                centre(L)
                if between:
                    between()
                invert(L)
                for k in range(KT + 2):
                    if k < KT:
                        dve.tensor_tensor(H[:, k, :], H[:, k, :], rstd[:, :], ALU.mult).then_inc(xn_ready, 1)
                    if split_ and k >= 2:
                        dve.wait_ge(hh_ready, KT * L + k - 1)
                        dve.tensor_tensor(HL[:, k - 2, :], H[:, k - 2, :], HH[:, k - 2, :], ALU.subtract) \
                           .then_inc(hl_ready, 1)

            layer_norm(0, between=lambda: mod_taken(0, 9))
            mod_taken(9, N_MOD)

            def mixer(l):
                n0 = BASE_MIX[l]
                if l == 1:
                    dve.wait_ge(tile_done, BASE_MIX[1])
                step(dve.memset(A2[:, :, 2, :], 0.0))
                for kv in range(2):
                    c = WHERE["cmp_pos"] + (2 * l + kv) * CMP_PAIRS
                    step(dve.tensor_copy(A2[:, kv, 2, 0:CMP_PAIRS], par[:, c:c + CMP_PAIRS]))
                for t in range(4):
                    n = n0 + 7 + t
                    dve.wait_ge(tile_done, n + 1)
                    take(dve.tensor_copy(Q[:, t, :], bank[n % RING][:, :]), n)
                for b in range(2):
                    dve.wait_ge(vg_T, 3 * l + b + 1)
                    dve.tensor_copy(V[:, b, :, :], bank[5 + b][:, :].rearrange("p (t n) -> p t n", n=P)) \
                       .then_inc(vg_ready, 1)
                dve.wait_ge(vg_T, 3 * l + 3)
                dve.tensor_copy(GA[:, :, :, :], bank[7][:, 0:ST * 24].rearrange("p (t b h) -> p t b h", b=3, h=HEADS)) \
                   .then_inc(vg_ready, 1)
                dve.wait_ge(vg_ready, 3 * l + 3)
                step(dve.tensor_scalar(GA[:, 0, 0, :], GA[:, 0, 0, :], cst[:, K_VALID:K_VALID + 1], None, ALU.mult))
                dve.wait_ge(dup_c, 64 * (l + 1))
                for kv in range(2):
                    for q in range(2):
                        rows = slice(64 * q, 64 * q + 64)
                        ins = dve.tensor_copy(A2[rows, kv, 0:2, :], K4[rows, kv, :, q:S:2])
                        if kv == 1 and q == 1:
                            ins.then_inc(a2_ready, 1)
                        else:
                            step(ins)
                for j in range(4):
                    dve.wait_ge(hid_done, 4 * l + j + 1)
                    dve.tensor_tensor(bsum[:, j:j + 1], bank[3 + j][:, 2 * NCMP:2 * NCMP + 1],
                                      col("cmp_b1", 4 * l + j), ALU.add).then_inc(bsum_ready, 1)
                dve.wait_ge(kcvc_done, l + 1)
                dve.tensor_scalar(KC[:, :, :], bank[7][:, 0:2 * NCMP].rearrange("p (g n) -> p g n", g=2),
                                  col("b2dup", l), None, ALU.add).then_inc(kcvc_ready, 1)
                dve.tensor_tensor(VC[:, :, :], bank[7][0:NCMP, 64:64 + 2 * HD].rearrange("p (g d) -> p g d", g=2),
                                  b2row[:, :].unsqueeze(1).broadcast_to((NCMP, 2, HD)), ALU.add) \
                   .then_inc(kcvc_ready, 1)
                dve.wait_ge(gelu_ready, 4 * (l + 1))
                dve.wait_ge(kcvc_ready, 2 * (l + 1))
                attention(l)
                for k in range(KT):
                    n = n0 + N_PROJ + k
                    dve.wait_ge(tile_done, n + 1)
                    take(dve.scalar_tensor_tensor(out=H[:, k, :], in0=H[:, k, :], scalar=ALPHA,
                                                  in1=bank[n % RING][:, :], op0=ALU.mult, op1=ALU.add), n)

            def attention(l):
                n0 = BASE_MIX[l] + 11
                dve.wait_ge(cs_done, l + 1)
                mask = cst[:, K_CMP:K_CMP + ST * NCMP].rearrange("p (i n) -> p i n", n=NCMP)
                for b in range(2):
                    hs = slice(b, HEADS, 2)
                    step(dve.tensor_tensor(Pcm[:, hs, :, :], bank[3 + b][:, 0:4 * ST * NCMP]
                                           .rearrange("p (h i n) -> p h i n", h=4, n=NCMP),
                                           mask.unsqueeze(1).broadcast_to((P, 4, ST, NCMP)), ALU.add))
                    step(dve.tensor_reduce(mxc[:, hs, :], Pcm[:, hs, :, :], AX.X, ALU.max))
                    dve.tensor_tensor(Pcm[:, hs, :, :], Pcm[:, hs, :, :],
                                      mxc[:, hs, :].unsqueeze(3).broadcast_to((P, 4, ST, NCMP)), ALU.subtract) \
                       .then_inc(cx_ready, 1)
                for b in range(2):
                    hs = slice(4 * b, 4 * b + 4)
                    dve.wait_ge(ce_ready, 2 * l + b + 1)
                    step(dve.tensor_reduce(mxc[:, hs, :], Pcm[:, hs, :, :], AX.X, ALU.add))
                    step(dve.reciprocal(mxc[:, hs, :], mxc[:, hs, :]))
                    step(dve.tensor_tensor(mxc[:, hs, :], mxc[:, hs, :],
                                           GA[:, :, 0, hs].rearrange("p i h -> p h i"), ALU.mult))
                    step(dve.tensor_tensor(Pcm[:, hs, :, :], Pcm[:, hs, :, :],
                                           mxc[:, hs, :].unsqueeze(3).broadcast_to((P, 4, ST, NCMP)), ALU.mult))
                step(dve.memset(QC[64:128, 0, :], 0.0))
                step(dve.memset(QC[0:64, 1, :], 0.0))
                step(dve.memset(zpad[:, 0:2], 0.0))
                with lane.loop(4, 2 + 1 + 8 * (2 + 2) + 3) as t:
                    u0 = 8 * t + 32 * l
                    dve.wait_ge(s_done, PRIMED + u0)
                    lane.step(dve.tensor_copy(QC[0:64, 0, :], Q[0:64, bass.ds(t, 1), :].rearrange("p o n -> p (o n)")))
                    lane.step(dve.tensor_copy(Cc[:, :, :, :].rearrange("p r i n -> p r (i n)"),
                                              Pcm[:, bass.ds(2 * t, 2), :, :].rearrange("p r i n -> p r (i n)")))
                    dve.tensor_copy(QC[64:128, 1, :], Q[64:128, bass.ds(t, 1), :].rearrange("p o n -> p (o n)")) \
                       .then_inc(q_ready, 1)

                    def maxima(v):
                        w = (v // 2 + 1) * P
                        dve.wait_ge(s_done, PRIMED + u0 + v + 1)
                        for b in range(2):
                            lane.step(dve.tensor_reduce(mx[:, b:b + 1], bank[3 + b][:, 0:w], AX.X, ALU.max))
                        lane.settle()
                        dve.tensor_scalar(nb[:, v % 2, :], mx[:, :], -SCALE1, None, ALU.mult).then_inc(max_ready, 1)

                    def rest_out(i):
                        dve.wait_ge(oh_ready, 4 * t + 16 * l + i + 1)
                        dve.tensor_tensor(ML[:, bass.ds(t, 1), i * P:(i + 1) * P].rearrange("p o n -> p (o n)"),
                                          bank[7][:, P:2 * P],
                                          MH[:, bass.ds(t, 1), i * P:(i + 1) * P].rearrange("p o n -> p (o n)"),
                                          ALU.subtract).then_inc(ol_ready, 1)

                    def pair_out(v):
                        dve.wait_ge(pv_done, PRIMED + u0 + v + 1)
                        dve.tensor_copy(ot[:, :], bank[7][:, 0:P]).then_inc(comb_ready, 1)

                    maxima(0)
                    dve.wait_ge(tc_done, t + 4 * l + 1)
                    lane.step(dve.tensor_copy(PTc[:, 0:ST, :], bank[5][0:NCMP, :].rearrange("p (i q) -> p i q", q=P)))
                    dve.tensor_copy(PTc[:, ST:2 * ST, :], bank[6][0:NCMP, :].rearrange("p (i q) -> p i q", q=P)) \
                       .then_inc(tc_ready, 1)
                    for v in range(8):
                        i, r = v // 2, v % 2
                        w = (i + 1) * P
                        dve.wait_ge(exp_ready, PRIMED + 2 * (u0 + v + 1))
                        step(dve.reciprocal(rz[:, :], Z[:, r, :]))
                        step(dve.tensor_tensor(fac[:, :], rz[:, :],
                                               GA[:, i, 1:3, bass.ds(2 * t + r, 1)].rearrange("p b o -> p (b o)"),
                                               ALU.mult))
                        for b in range(2):
                            ins = dve.tensor_scalar(Psw[:, r, b, 0:w], Psw[:, r, b, 0:w], fac[:, b:b + 1], None,
                                                    ALU.mult)
                        ins.then_inc(ps_ready, 1)
                        if v < 7:
                            maxima(v + 1)
                        if v >= 3 and r == 1:
                            rest_out((v - 3) // 2)
                        dve.wait_ge(t_done, u0 + v + 1)
                        dve.wait_ge(pv_done, u0 + v - 1 + PRIMED)
                        dve.tensor_copy(PTsw[:, r, 1, 0:i + 1, :], bank[6][:, 0:(i + 1) * P]
                                        .rearrange("p (k q) -> p k q", q=P)).then_inc(ptw_ready, 1)
                        if r == 0 and v > 0:
                            pair_out(v - 1)
                        if v == 6:
                            convolve(t, l)
                    pair_out(7)
                    dve.wait_ge(tile_done, 3 * t + n0 + 3)
                    take(dve.tensor_tensor(cy[:, :], cy[:, :], bank[(n0 + 2) % RING][:, :], ALU.mult), n0 + 2)
                    rest_out(3)
                    dve.wait_ge(mixh_ready, 4 * l + t + 1)
                    dve.tensor_tensor(ML[:, bass.ds(t + 4, 1), :].rearrange("p o n -> p (o n)"), cy[:, :],
                                      MH[:, bass.ds(t + 4, 1), :].rearrange("p o n -> p (o n)"), ALU.subtract) \
                       .then_inc(mixl_ready, 1)

            def convolve(t, l):
                n0 = BASE_MIX[l] + 11
                dve.wait_ge(bank_free[n0 % RING], t + n0 // RING + 1)
                dve.wait_ge(tile_done, 3 * t + n0 + 2)
                take(dve.tensor_tensor(zpad[:, 2:2 + S], t_cg[:, :], bank[(n0 + 1) % RING][:, :], ALU.mult), n0 + 1)
                dve.wait_ge(bank_free[(n0 + 1) % RING], t + (n0 + 1) // RING + 1)
                w = [par[:, bass.ds(t + (WHERE["conv_w"] + 12 * l + 4 * i), 1)] for i in range(3)]
                step(dve.tensor_scalar(cy[:, :], zpad[:, 0:S], w[0], None, ALU.mult))
                for i in (1, 2):
                    step(dve.scalar_tensor_tensor(out=cy[:, :], in0=zpad[:, i:i + S], scalar=w[i],
                                                  in1=cy[:, :], op0=ALU.mult, op1=ALU.add))

            def router():
                dve.wait_ge(lg_done, 1)
                dve.tensor_copy(lgT[:, :], bank[5][0:EXPERTS, :]).then_inc(lg_ready, 1)
                dve.wait_ge(lg_done, 2)
                step(dve.tensor_copy(lg[:, :, :], bank[6][:, 0:ST * EXPERTS].rearrange("p (t e) -> p t e", e=EXPERTS)))
                step(dve.tensor_reduce(top[:, :], lg[:, :, :], AX.X, ALU.max))
                flat = lg[:, :, :].rearrange("p t e -> p (t e)")
                for t in range(ST):
                    rows = slice(t * EXPERTS, (t + 1) * EXPERTS)
                    other = lg[:, t, :].unsqueeze(1).broadcast_to((P, EXPERTS, EXPERTS))
                    own = lg[:, t, :].unsqueeze(2).broadcast_to((P, EXPERTS, EXPERTS))
                    step(dve.tensor_tensor(gt8[:, rows, :], other, own, ALU.is_gt))
                    step(dve.tensor_tensor(eq8[:, rows, :], other, own, ALU.is_equal))
                    step(dve.tensor_tensor(eq8[:, rows, :], eq8[:, rows, :],
                                           cst[:, K_PAIR:K_ALL].rearrange("p (e j) -> p e j", j=EXPERTS), ALU.mult))
                step(dve.tensor_tensor(gt8[:, :, :], gt8[:, :, :], eq8[:, :, :], ALU.add))
                step(dve.tensor_reduce(sel[:, :, :].rearrange("p t e -> p (t e)"), gt8[:, :, :], AX.X, ALU.add))
                step(dve.tensor_scalar(sel[:, :, :], sel[:, :, :], 2.0, None, ALU.is_lt))
                dve.tensor_tensor(lg[:, :, :], lg[:, :, :], top[:, :].unsqueeze(2).broadcast_to((P, ST, EXPERTS)),
                                  ALU.subtract).then_inc(lg_ready, 1)
                dve.wait_ge(router_exp, 1)
                step(dve.tensor_tensor(ex[:, :, :], ex[:, :, :], sel[:, :, :], ALU.mult))
                step(dve.tensor_reduce(top[:, :], ex[:, :, :], AX.X, ALU.add))
                step(dve.reciprocal(top[:, :], top[:, :]))
                dve.tensor_tensor(ex[:, :, :], ex[:, :, :], top[:, :].unsqueeze(2).broadcast_to((P, ST, EXPERTS)),
                                  ALU.mult).then_inc(lg_ready, 1)
                dve.wait_ge(lg_done, 3)
                dve.tensor_copy(lgT[:, :], bank[5][0:EXPERTS, :]).then_inc(lg_ready, 1)
                for e in range(EXPERTS):
                    dve.wait_ge(lg_done, 4 + e)
                    dve.tensor_copy(GB[:, e, :], bank[6 + e % 2][:, :]).then_inc(gate_ready, 1)

            def ffn(l):
                n0 = BASE_FFN[l]
                if l == 1:
                    router()
                dve.wait_ge(hl_ready, KT * (2 * l + 2))
                for k in range(KT):
                    lane.step(dve.tensor_scalar(H[:, k, :], H[:, k, :], ALPHA, None, ALU.mult))
                lane.settle()
                if l == 1:
                    dve.wait_ge(gate_ready, EXPERTS)
                with dve.Fori(0, PARTS[l]) as e:
                    turn = e * (N_PART // RING)

                    def taken_here(n):
                        dve.wait_ge(bank_free[n % RING], turn + n // RING + 1)

                    for j in range(PT):
                        n = n0 + 2 * j
                        q = PT * e + PT * DENSE_PARTS * l
                        taken_here(n)
                        dve.wait_ge(tile_done, e * N_PART + n + 2)
                        if j >= 2:
                            dve.wait_ge(ul_ready, q + j - 1)
                        take(dve.tensor_tensor(gu[:, j % 2, :], silu_g[:, j % 2, :], bank[(n + 1) % RING][:, :],
                                               ALU.mult), n + 1)
                        dve.wait_ge(uh_ready, q + j + 1)
                        dve.tensor_tensor(UL[:, j, :], gu[:, j % 2, :], UH[:, j, :], ALU.subtract) \
                           .then_inc(ul_ready, 1)
                    for k in range(KT):
                        n = n0 + 2 * PT + k
                        dve.wait_ge(tile_done, e * N_PART + n + 1)
                        if l == 0:
                            take(dve.tensor_tensor(H[:, k, :], H[:, k, :], bank[n % RING][:, :], ALU.add), n)
                        else:
                            if k < 2:
                                dve.wait_ge(ul_ready, q + PT)
                            dve.wait_ge(down_taken, PRIMED + e * KT + max(k - 1, 0))
                            take(dve.tensor_tensor(gu[:, k % 2, :], bank[n % RING][:, :],
                                                   GB[:, bass.ds(e, 1), :].rearrange("p o n -> p (o n)"), ALU.mult), n)
                            taken_here(n)
                            dve.tensor_tensor(H[:, k, :], H[:, k, :], gu[:, k % 2, :], ALU.add) \
                               .then_inc(down_taken, 1)

            for l in range(DEPTH):
                mixer(l)
                layer_norm(2 * l + 1)
                ffn(l)
                layer_norm(2 * l + 2, split_=(l == 0))

            dve.wait_ge(h_ready, 5 * KT)
            step(dve.scalar_tensor_tensor(out=modg[:, :], in0=mod[:, KT:2 * KT], scalar=1.0,
                                          in1=par[:, WHERE["g_norm_2"]:WHERE["g_norm_2"] + KT],
                                          op0=ALU.add, op1=ALU.mult))
            lam = par[:, WHERE["lam_2"]:WHERE["lam_2"] + KT]
            L8 = [lamc[:, j, :] for j in range(8)]
            step(dve.tensor_scalar(L8[2], lam, -1.0, None, ALU.mult))
            dve.tensor_tensor(L8[0], lam, L8[2], ALU.max).then_inc(lam_abs, 1)
            invert(5)
            for k in range(KT):
                if k >= 2:
                    dve.wait_ge(hh_ready, 4 * KT + k - 1)
                dve.tensor_tensor(t2[:, k % 2, :], H[:, k, :], rstd[:, :], ALU.mult).then_inc(xn_ready, 1)
                dve.wait_ge(xn_ready, 5 * KT + k + 1)
                step(dve.tensor_scalar(IX[:, k, :], t2[:, k % 2, :], modg[:, k:k + 1], mod[:, k:k + 1],
                                       ALU.mult, ALU.add))
                dve.wait_ge(hh_ready, 4 * KT + k + 1)
                dve.tensor_tensor(HL[:, k, :], IX[:, k, :], HH[:, k, :], ALU.subtract).then_inc(hl_ready, 1)
            dve.wait_ge(lam_exp, 1)
            step(dve.tensor_scalar(L8[3], L8[1], 2.0, None, ALU.add))
            step(dve.reciprocal(L8[3], L8[3]))
            step(dve.tensor_tensor(L8[4], L8[1], L8[3], ALU.mult))
            step(dve.tensor_tensor(L8[5], L8[4], L8[4], ALU.mult))
            step(dve.tensor_scalar(L8[6], L8[5], 1.0 / 17, None, ALU.mult))
            for odd in (15, 13, 11, 9, 7, 5, 3):
                step(dve.scalar_tensor_tensor(out=L8[6], in0=L8[6], scalar=1.0 / odd, in1=L8[5],
                                              op0=ALU.add, op1=ALU.mult))
            step(dve.scalar_tensor_tensor(out=L8[6], in0=L8[6], scalar=1.0, in1=L8[4], op0=ALU.add, op1=ALU.mult))
            step(dve.tensor_scalar(L8[2], L8[2], 0.0, None, ALU.max))
            step(dve.scalar_tensor_tensor(out=L8[7], in0=L8[6], scalar=2.0, in1=L8[2], op0=ALU.mult, op1=ALU.add))
            step(dve.tensor_scalar(L8[6], L8[7], -8.0, None, ALU.mult))
            step(dve.tensor_scalar(L8[7], L8[7], 8.0, None, ALU.mult))
            dve.wait_ge(b2_landed, 48)
            step(dve.tensor_scalar(keep[:, :], posi[:, :], 0, None, ALU.not_equal))
            step(dve.tensor_scalar(drop[:, :], posi[:, :], 0, None, ALU.is_equal))
            step(dve.tensor_scalar(ang[:, :], posi[0:ROT, :], cst[0:ROT, K_FREQ:K_FREQ + 1], None, ALU.mult))
            two_pi = [6.28125, 0.0019350051879882812, 2 * np.pi - 6.28125 - 0.0019350051879882812]
            for o, quarter in ((sinT, 0.0), (cosT, np.pi / 2)):
                step(dve.tensor_scalar(turns[:, :], ang[:, :], quarter, 1 / (2 * np.pi), ALU.add, ALU.mult))
                step(dve.tensor_copy(turnf[:, :], turns[:, :]))
                step(dve.scalar_tensor_tensor(out=o[:, :], in0=turnf[:, :], scalar=-two_pi[0], in1=ang[:, :],
                                              op0=ALU.mult, op1=ALU.add))
                for part in two_pi[1:]:
                    step(dve.scalar_tensor_tensor(out=o[:, :], in0=turnf[:, :], scalar=-part, in1=o[:, :],
                                                  op0=ALU.mult, op1=ALU.add))
                step(dve.tensor_scalar(o[:, :], o[:, :], quarter, None, ALU.add))
                dve.tensor_scalar(o[:, :], o[:, :], 3.1415925, -3.1415925, ALU.min, ALU.max).then_inc(ang_ready, 1)

            step(dve.memset(xpad[:, 0:3], 0.0))

            def gated(k):
                dve.wait_ge(ri_ready, 2 * k + 2)
                dve.tensor_tensor(IX[:, k, :], IX[:, k, :], XC[:, k, :], ALU.mult).then_inc(ix_ready, 1)

            for k in range(KT):
                taken(dve, B2_X + k)
                w = [col("conv_w_2", KT * i + k) for i in range(4)]
                step(dve.tensor_scalar(XC[:, k, :], xpad[:, 0:S], w[0], col("conv_b_2", k), ALU.mult, ALU.add))
                for i in (1, 2, 3):
                    ins = dve.scalar_tensor_tensor(out=XC[:, k, :], in0=xpad[:, i:i + S], scalar=w[i],
                                                   in1=XC[:, k, :], op0=ALU.mult, op1=ALU.add)
                    if i < 3:
                        step(ins)
                ins.then_inc(xc_ready, 1)
                if k >= 1:
                    gated(k - 1)
            gated(KT - 1)
            for k in range(KT):
                dve.wait_ge(decay_ready, 2 * k + 2)
                step(dve.tensor_tensor(la2[:, :], XC[:, k, :], XC[:, k, :], ALU.mult))
                dve.scalar_tensor_tensor(out=R[:, k, :], in0=la2[:, :], scalar=1.0, in1=lt[:, k % 2, :],
                                         op0=ALU.add, op1=ALU.mult).then_inc(lru_q, 1)
                dve.wait_ge(lru_q, k + 1)
                step(dve.tensor_tensor(XC[:, k, :], XC[:, k, :], keep[:, :], ALU.mult))

            def gated_state(k):
                taken(dve, B2_Z + k)
                if k >= 2:
                    dve.wait_ge(u2l_ready, k - 1)
                dve.tensor_tensor(t2[:, k % 2, :], R[:, k, :], XC[:, k, :], ALU.mult).then_inc(u2_ready, 1)
                dve.wait_ge(u2h_ready, k + 1)
                dve.tensor_tensor(RL[:, k, :], t2[:, k % 2, :], RH[:, k, :], ALU.subtract).then_inc(u2l_ready, 1)

            for k in range(KT):
                dve.wait_ge(root_ready, k + 1)
                step(dve.tensor_tensor(R[:, k, :], R[:, k, :], keep[:, :], ALU.mult))
                step(dve.tensor_tensor(R[:, k, :], R[:, k, :], drop[:, :], ALU.add))
                step(dve.tensor_tensor(IX[:, k, :], IX[:, k, :], R[:, k, :], ALU.mult))
                dve.tensor_tensor_scan(out=R[:, k, :], data0=XC[:, k, :], data1=IX[:, k, :], initial=0.0,
                                       op0=ALU.mult, op1=ALU.add).then_inc(hr_ready, 1)
                dve.wait_ge(hr_ready, k + 1)
                if k >= 1:
                    gated_state(k - 1)
            gated_state(KT - 1)
            for k in range(KT):
                n = B2_RNN + 2 * k
                taken(dve, n)
                dve.wait_ge(tile_done, n + 2)
                take(dve.tensor_tensor(M[:, k, :], t2[:, k % 2, :], bank[(n + 1) % RING][:, :], ALU.mult), n + 1)
            taken(dve, B2_RNN + 2 * KT - 1)
            with lane.loop(HEADS, 2 * 2 + 2 * ST) as h:
                for j, x in enumerate((qh, kh)):
                    dve.wait_ge(rot_done, 2 * h + j + 1)
                    lane.step(dve.tensor_tensor(t2[0:ROT, 0, :], bank[3 + j][0:ROT, :], sinT[:, :], ALU.mult))
                    lane.step(dve.tensor_tensor(t2[0:ROT, 1, :], x[0:ROT, :], cosT[:, :], ALU.mult))
                    lane.settle()
                    dve.tensor_tensor(x[0:ROT, :], t2[0:ROT, 0, :], t2[0:ROT, 1, :], ALU.add).then_inc(rope_ready, 1)
                    dve.wait_ge(rope_ready, 2 * h + j + 1)
                dve.wait_ge(v2_done, h + 1)
                dve.tensor_copy(V2[:, :, :], bank[5][:, :].rearrange("p (t n) -> p t n", n=P)).then_inc(v2_ready, 1)

                def maxima2(i):
                    w = (i + 1) * P
                    dve.wait_ge(s2_done, 4 * h + i + 1)
                    step(dve.tensor_reduce(m2[:, i % 2:i % 2 + 1], bank[6 + i % 2][:, 0:w], AX.X, ALU.max))
                    dve.tensor_scalar(n2[:, i % 2:i % 2 + 1], m2[:, i % 2:i % 2 + 1], -SCALE2, None, ALU.mult) \
                       .then_inc(m2_ready, 1)

                maxima2(0)
                for i in range(ST):
                    w = (i + 1) * P
                    if i < ST - 1:
                        maxima2(i + 1)
                    dve.wait_ge(e2_ready, 4 * h + i + 1)
                    step(dve.reciprocal(r2[:, i % 2:i % 2 + 1], z2[:, i % 2:i % 2 + 1]))
                    dve.tensor_scalar(P2[:, i % 2, 0:w], P2[:, i % 2, 0:w], r2[:, i % 2:i % 2 + 1], None, ALU.mult) \
                       .then_inc(p2_ready, 1)
                dve.wait_ge(pv2_done, PRIMED + 4 * h + ST)
                dve.wait_ge(u2l_ready, h + KT)
                dve.tensor_tensor(oz[:, :], bank[4][:, :], XC[:, bass.ds(h, 1), :].rearrange("p o n -> p (o n)"),
                                  ALU.mult).then_inc(u2_ready, 1)
                dve.wait_ge(u2h_ready, h + KT + 1)
                dve.tensor_tensor(RL[:, bass.ds(h, 1), :].rearrange("p o n -> p (o n)"), oz[:, :],
                                  RH[:, bass.ds(h, 1), :].rearrange("p o n -> p (o n)"), ALU.subtract) \
                   .then_inc(u2l_ready, 1)
            for k in range(KT):
                n = B2_ATT + 2 * k
                taken(dve, n)
                dve.wait_ge(tile_done, n + 2)
                if k >= 2:
                    dve.wait_ge(u2l_ready, 2 * KT + k - 1)
                take(dve.tensor_tensor(P2[:, k % 2, :], t2[:, k % 2, :], bank[(n + 1) % RING][:, :], ALU.mult), n + 1)
                taken(dve, n + 1)
                dve.tensor_tensor(P2[:, k % 2, :], P2[:, k % 2, :], M[:, k, :], ALU.add).then_inc(u2_ready, 1)
                dve.wait_ge(u2h_ready, 2 * KT + k + 1)
                dve.tensor_tensor(GL[:, k, :], P2[:, k % 2, :], GH[:, k, :], ALU.subtract).then_inc(u2l_ready, 1)
            for k in range(KT):
                n = B2_O + k
                dve.wait_ge(tile_done, n + 1)
                take(dve.scalar_tensor_tensor(out=H[:, k, :], in0=bank[n % RING][:, :],
                                              scalar=mod[:, 2 * KT + k:2 * KT + k + 1], in1=H[:, k, :],
                                              op0=ALU.mult, op1=ALU.add), n)
            invert(6)
            for k in range(KT):
                dve.scalar_tensor_tensor(out=H[:, k, :], in0=H[:, k, :], scalar=col("g_final_2", k), in1=rstd[:, :],
                                         op0=ALU.mult, op1=ALU.mult).then_inc(xn_ready, 1)


_INS = ["x", "ln_in_g", "ln_in_b", "w_in", "cmp_pos", "cmp_w1", "cmp_b1", "cmp_w2", "cmp_b2", "conv_w", "w_o",
        "ln1_g", "ln1_b", "ln2_g", "ln2_b", "ffn_wg", "ffn_wu", "ffn_wd", "moe_router", "moe_wg", "moe_wu",
        "moe_wd", "c_2", "positions_2", "g_norm_2", "w_mod_2", "b_mod_2", "w_in_2", "b_gate_2", "conv_w_2",
        "conv_b_2", "w_a_2", "b_a_2", "w_x_2", "b_x_2", "lam_2", "w_out_rnn_2", "w_out_attn_2", "w_o_2",
        "g_final_2"]


def kernel(**inputs):
    import concourse.bacc as _bacc
    from concourse.bass_utils import run_bass_kernel_spmd as _run

    nc = _bacc.Bacc("TRN2", target_bir_lowering=False, num_devices=1)
    arrays, args = {}, {}
    for name in _INS + ["consts"]:
        v = constant_table() if name == "consts" else np.ascontiguousarray(inputs[name])
        arrays[f"in_{name}_dram"] = v
        args[name] = nc.dram_tensor(f"in_{name}_dram", v.shape, mybir.dt.from_np(v.dtype),
                                    kind="ExternalInput").ap()
    out = nc.dram_tensor("out_0_dram", (1, S, D), F32, kind="ExternalOutput").ap()
    build(nc, args, out)
    r = _run(nc, [arrays], core_ids=[0])
    return r.results[0]["out_0_dram"]
```

```python
from contextlib import ExitStack, contextmanager

import numpy as np

import concourse.bass as bass
from concourse import mybir

F32 = mybir.dt.float32
F32R = mybir.dt.float32r
I32 = mybir.dt.int32
ALU = mybir.AluOpType
ACT = mybir.ActivationFunctionType
AX = mybir.AxisListType

P = 128
S = 512
D = 1024
KT = D // P
ST = S // P
DEPTH = 2
HEADS = 8
GROUPS = 2
HD = 64
ATTN_W = HEADS * HD
KV_W = GROUPS * HD
CONV_CH = D - ATTN_W
NCMP = S // 16 - 1
CMP_PAIRS = 16
ALPHA = float((2 * DEPTH) ** 0.25)
LN_EPS = 1e-5
RMS_EPS = 1e-6
NEG = -1e30
D_PART = 1408
PT = D_PART // P
DENSE_PARTS = 2
EXPERTS = 8
SCALE1 = HD ** -0.5
HD2 = 128
SCALE2 = HD2 ** -0.5
ROT = 32
RING = 3
PRIMED = 1

C_Q, C_KC, C_VC, C_KS, C_VS, C_KW, C_VW = 0, 512, 640, 768, 896, 1024, 1152
C_GATES = C_VW + KV_W
C_U = C_GATES + 3 * HEADS
C_BG = C_U + CONV_CH
C_CG = C_BG + CONV_CH

K_ID = 0
K_CAUSAL = K_ID + P
K_CMP = K_CAUSAL + P
K_VALID = K_CMP + ST * NCMP
K_DIL = K_VALID + 1
K_ROT = K_DIL + S
K_FREQ = K_ROT + P
K_PAIR = K_FREQ + 1
K_ALL = K_PAIR + EXPERTS * EXPERTS

VECTORS = [("ln_in_g", 8), ("ln_in_b", 8), ("ln1_g", 16), ("ln1_b", 16), ("ln2_g", 16), ("ln2_b", 16),
           ("cmp_b1", 8), ("conv_w", 24), ("b2dup", DEPTH),
           ("g_norm_2", 8), ("b_mod_2", 24), ("b_gate_2", 16), ("conv_w_2", 32),
           ("conv_b_2", 8), ("b_a_2", 8), ("b_x_2", 8), ("lam_2", 8), ("g_final_2", 8), ("c_2", 8),
           ("cmp_pos", 64)]
FIRST_OF = {"g_norm_2": 1, "cmp_pos": 2}


def vector_places():
    where, stage, row = {}, 0, 0
    for name, rows in VECTORS:
        if name in FIRST_OF:
            stage, row = FIRST_OF[name], 0
        where[name] = stage * P + row
        row += rows
        assert row <= P
    return where


def stage_rows():
    used = [0, 0, 0]
    for name, rows in VECTORS:
        used[WHERE[name] // P] = WHERE[name] % P + rows
    return used


def vector_sources(a, name):
    v = a[name]
    if name == "cmp_pos":
        return v.rearrange("l v (t q) d -> (l v t) (q d)", q=2)
    if name in ("b_a_2", "b_x_2"):
        return v.rearrange("l k p -> (l k) p")
    form = {1: "(k p) -> k p", 2: "l (k p) -> (l k) p", 3: "l v (k p) -> (l v k) p"}[len(v.shape)]
    return v.rearrange(form, p=P)


WHERE = vector_places()
STAGE_ROWS = stage_rows()
STAGED = len(VECTORS) - 1 + 2 * DEPTH

N_MOD = 24
N_MOD_1 = 9
N_PROJ = 7 + 4 + 12
N_MIX = N_PROJ + KT
N_PART = 2 * PT + KT
BASE_MIX = [N_MOD_1, N_MOD_1 + N_MIX + DENSE_PARTS * N_PART]
BASE_FFN = [b + N_MIX for b in BASE_MIX]
PARTS = [DENSE_PARTS, EXPERTS]
BASE_MOD = BASE_FFN[1] + EXPERTS * N_PART
BASE_2 = BASE_MOD + N_MOD - N_MOD_1
M_KEYS = [0, 1, 7, 8]
M_Q = 2
M_GATES = 6
M_V = 9
B2_X = BASE_2
B2_Z = B2_X + KT
B2_ZA = B2_Z + KT
B2_RNN = B2_ZA + KT
B2_HEAD = B2_RNN + 2 * KT
B2_ATT = B2_HEAD + 3 * HEADS
B2_O = B2_ATT + 2 * KT
N_ALL = B2_O + KT


def mod_place(i):
    return i if i < N_MOD_1 else BASE_MOD + i - N_MOD_1


def constant_table():
    t = np.zeros((P, K_ALL), np.float32)
    p = np.arange(P)[:, None]
    j = np.arange(P)[None, :]
    t[:, K_ID:K_ID + P] = (p == j)
    t[:, K_CAUSAL:K_CAUSAL + P] = np.where(j <= p, 0.0, NEG)
    for i in range(ST):
        ends = np.arange(NCMP)[None, :] * 16 + 31
        t[:, K_CMP + i * NCMP:K_CMP + (i + 1) * NCMP] = np.where(ends <= i * P + p, 0.0, NEG)
    t[:, K_VALID] = (p[:, 0] >= 31)
    dist = p + (S - P) - np.arange(S)[None, :]
    count = ((dist >= 0) & (dist <= 128)).astype(np.float64) + ((dist >= 0) & (dist % 4 == 0)) \
        + ((dist >= 0) & (dist % 16 == 0))
    t[:, K_DIL:K_DIL + S] = np.where(count > 0, np.log(np.maximum(count, 1)) / SCALE2, NEG)
    half = ROT // 2
    for i in range(half):
        t[i + half, K_ROT + i] = -1.0
        t[i, K_ROT + i + half] = 1.0
    freq = np.float32(500000.0) ** (-np.arange(0, ROT, 2, dtype=np.float32) / np.float32(ROT))
    t[:ROT, K_FREQ] = np.concatenate([freq, freq])
    e = np.arange(EXPERTS)
    t[:, K_PAIR:] = (e[None, :] < e[:, None]).astype(np.float32).reshape(1, -1)
    return t


class Lane:

    def __init__(self, eng, sem):
        self.eng, self.sem, self.n, self.turn = eng, sem, 0, 0

    def step(self, ins):
        ins.then_inc(self.sem, 1)
        self.n += 1

    def settle(self):
        self.eng.wait_ge(self.sem, self.turn + self.n)

    @contextmanager
    def loop(self, count, per):
        with self.eng.Fori(0, count) as i:
            before, outer = self.n, self.turn
            self.turn = outer + i * per
            yield i
            assert self.n == before + per, (self.n - before, per)
            self.turn = outer
        self.n = before + per * count


def build(nc, a, out):
    with ExitStack() as ctx:
        def sb(name, shape, dt=F32, stack=ctx):
            return stack.enter_context(nc.sbuf_tensor(name, shape, dt))

        def sem(name):
            return ctx.enter_context(nc.semaphore(name))

        bank = [ctx.enter_context(nc.psum_tensor(f"bank{b}", [P, 512], F32)) for b in range(8)]

        raw = [sb(f"raw{r}", [P, PT, P]) for r in range(RING)]
        head = [sb(f"head{r}", [P, PT, P], F32R) for r in range(RING)]
        rest = [sb(f"rest{r}", [P, PT, P], F32R) for r in range(RING)]
        cst = sb("cst", [P, K_ALL])
        par = sb("par", [P, 3 * P])
        H = sb("H", [P, KT, S])
        HH = sb("HH", [P, KT, S], F32R)
        HL = sb("HL", [P, KT, S], F32R)
        mean_w = sb("mean_w", [P, P])
        eps = sb("eps", [P, 2])
        sq = sb("sq", [P, 2, S])
        rstd = sb("rstd", [P, S])
        mod = sb("mod", [P, N_MOD])
        c_act = sb("c_act", [P, KT, 2])
        c_head = sb("c_head", [P, KT, 2], F32R)
        c_rest = sb("c_rest", [P, KT, 2], F32R)
        ident = cst[:, K_ID:K_ID + P]
        causal = cst[:, K_CAUSAL:K_CAUSAL + P]

        with ExitStack() as s:
            x_tok = sb("x_tok", [P, ST, D], stack=s)
            stage = sb("stage", [P, 3, P], stack=s)
        with ExitStack() as s:
            K4 = sb("K4", [P, 4, GROUPS, S], stack=s)
            V = sb("V", [P, 2, ST, P], stack=s)
            GA = sb("GA", [P, ST, 3, HEADS], stack=s)
            KC = sb("KC", [P, GROUPS, NCMP], stack=s)
            VC = sb("VC", [NCMP, GROUPS, HD], stack=s)
            Q = sb("Q", [P, 4, S], stack=s)
            with ExitStack() as s2:
                W1 = sb("W1", [P, 2, CMP_PAIRS, 256], stack=s2)
            with ExitStack() as s2:
                MH = sb("MH", [P, KT, S], F32R, stack=s2)
                ML = sb("ML", [P, KT, S], F32R, stack=s2)
            s.enter_context(nc.sbuf_tensor("mix_place", [P, 2 * KT, S], F32))
            with ExitStack() as s2:
                VT = sb("VT", [P, 2, S], stack=s2)
                GT = sb("GT", [3 * HEADS, S], stack=s2)
                A2 = sb("A2", [P, 2, 3, S // 2], stack=s2)
                W2 = sb("W2", [P, 2, 2, P], stack=s2)
                b2row = sb("b2row", [NCMP, HD], stack=s2)
                bsum = sb("bsum", [P, 4], stack=s2)
                HG = sb("HG", [P, 2, 2, GROUPS * NCMP], stack=s2)
            with ExitStack() as s2:
                QC = sb("QC", [P, 2, S], stack=s2)
                Cc = sb("Cc", [P, 2, ST, NCMP], stack=s2)
                Psw = sb("Psw", [P, 2, 2, S], stack=s2)
                PTsw = sb("PTsw", [P, 2, 2, ST, P], stack=s2)
                mxc = sb("mxc", [P, HEADS, ST], stack=s2)
                mx = sb("mx", [P, 2], stack=s2)
                nb = sb("nb", [P, 2, 2], stack=s2)
                Z = sb("Z", [P, 2, 2], stack=s2)
                rz = sb("rz", [P, 2], stack=s2)
                fac = sb("fac", [P, 2], stack=s2)
                ot = sb("ot", [P, P], stack=s2)
                t_cg = sb("t_cg", [P, S], stack=s2)
                zpad = sb("zpad", [P, 2 + S], stack=s2)
                cy = sb("cy", [P, S], stack=s2)
            Pcm = K4[:, 0, :, :].rearrange("p g n -> p (g n)")[:, 0:HEADS * ST * NCMP] \
                .rearrange("p (h i n) -> p h i n", h=HEADS, n=NCMP)
            PTc = K4[0:NCMP, 1, :, :].rearrange("p g (a q) -> p (g a) q", q=P)
        with ExitStack() as s:
            UH = sb("UH", [P, PT, S], F32R, stack=s)
            UL = sb("UL", [P, PT, S], F32R, stack=s)
            silu_g = sb("silu_g", [P, 2, S], stack=s)
            gu = sb("gu", [P, 2, S], stack=s)
            GB = sb("GB", [P, EXPERTS, S], stack=s)
            rw = sb("rw", [P, KT, EXPERTS], stack=s)
            lgT = sb("lgT", [EXPERTS, S], stack=s)
            lg = sb("lg", [P, ST, EXPERTS], stack=s)
            gt8 = sb("gt8", [P, ST * EXPERTS, EXPERTS], stack=s)
            eq8 = sb("eq8", [P, ST * EXPERTS, EXPERTS], stack=s)
            sel = sb("sel", [P, ST, EXPERTS], stack=s)
            top = sb("top", [P, ST], stack=s)
            ex = sb("ex", [P, ST, EXPERTS], stack=s)
        with ExitStack() as s:
            with ExitStack() as s2:
                XC = sb("XC", [P, KT, S], stack=s2)
                IX = sb("IX", [P, KT, S], stack=s2)
                R = sb("R", [P, KT, S], stack=s2)
                M = sb("M", [P, KT, S], stack=s2)
            with ExitStack() as s2:
                GH = sb("GH", [P, KT, S], F32R, stack=s2)
                RH = sb("RH", [P, KT, S], F32R, stack=s2)
                RL = sb("RL", [P, KT, S], F32R, stack=s2)
                GL = sb("GL", [P, KT, S], F32R, stack=s2)
            s.enter_context(nc.sbuf_tensor("three_places", [P, 3 * KT, S], F32))
            with ExitStack() as s2:
                with ExitStack() as s3:
                    WA = sb("WA", [P, 2, KT, P], stack=s3)
                    xpad = sb("xpad", [P, 3 + S], stack=s3)
                with ExitStack() as s3:
                    lt = sb("lt", [P, 2, S], stack=s3)
                    la2 = sb("la2", [P, S], stack=s3)
                s2.enter_context(nc.sbuf_tensor("wa_place", [P, 2 * KT * P + S + 4], F32))
                keep = sb("keep", [P, S], stack=s2)
                drop = sb("drop", [P, S], stack=s2)
            s.enter_context(nc.sbuf_tensor("m_place", [P, KT, S], F32))
            modg = sb("modg", [P, KT], stack=s)
            lamc = sb("lamc", [P, 8, KT], stack=s)
            t2 = sb("t2", [P, 2, S], stack=s)
            cosT = sb("cosT", [ROT, S], stack=s)
            sinT = sb("sinT", [ROT, S], stack=s)
            with ExitStack() as s2:
                posi = sb("posi", [P, S], I32, stack=s2)
                ang = sb("ang", [ROT, S], stack=s2)
                turns = sb("turns", [ROT, S], I32, stack=s2)
                turnf = sb("turnf", [ROT, S], stack=s2)
            with ExitStack() as s2:
                qh = sb("qh", [P, S], stack=s2)
                kh = sb("kh", [P, S], stack=s2)
                vh = sb("vh", [P, S], stack=s2)
                V2 = sb("V2", [P, ST, P], stack=s2)
                P2 = sb("P2", [P, 2, S], stack=s2)
                PT2 = sb("PT2", [P, ST, P], stack=s2)
                m2 = sb("m2", [P, 2], stack=s2)
                n2 = sb("n2", [P, 2], stack=s2)
                z2 = sb("z2", [P, 2], stack=s2)
                r2 = sb("r2", [P, 2], stack=s2)
                oz = sb("oz", [P, S], stack=s2)
            with ExitStack() as s2:
                ZS = sb("ZS", [P, KT, S], stack=s2)
        with ExitStack() as s:
            y_tok = sb("y_tok", [P, ST, D], stack=s)

        sem_cst = sem("constants_landed")
        sem_stage = sem("vectors_landed")
        sem_x = sem("x_landed")
        raw_landed = [sem(f"raw_landed{r}") for r in range(RING)]
        head_done = sem("head_done")
        weights_split = sem("weights_split")
        tile_done = sem("tile_done")
        bank_free = [sem(f"bank_free{b}") for b in range(RING)]
        vec_step = sem("vec_step")
        act_step = sem("act_step")
        setup_done = sem("setup_done")
        par_T = sem("par_transposed")
        par_ready = sem("par_ready")
        c_hi = sem("c_head_ready")
        c_lo = sem("c_rest_ready")
        x_T = sem("x_transposed")
        y_ready = sem("y_ready")
        sum_ready = sem("sum_ready")
        mean_done = sem("mean_done")
        d_ready = sem("d_ready")
        sq_ready = sem("sq_ready")
        sq_used = sem("sq_used")
        std_ready = sem("std_ready")
        rs_ready = sem("rs_ready")
        xn_ready = sem("xn_ready")
        h_ready = sem("h_ready")
        hh_ready = sem("hh_ready")
        hl_ready = sem("hl_ready")
        w1_landed = sem("w1_landed")
        dup_c = sem("dup_cmp")
        dup_s = sem("dup_sel_win")
        vg_T = sem("vg_transposed")
        vg_ready = sem("vg_ready")
        a2_ready = sem("a2_ready")
        hid_done = sem("hidden_done")
        bsum_ready = sem("bsum_ready")
        gelu_ready = sem("gelu_ready")
        kcvc_done = sem("kcvc_done")
        kcvc_ready = sem("kcvc_ready")
        mixh_ready = sem("mixh_ready")
        mixl_ready = sem("mixl_ready")
        q_ready = sem("q_ready")
        s_done = sem("scores_done")
        max_ready = sem("max_ready")
        exp_ready = sem("exp_ready")
        t_done = sem("probs_transposed")
        cs_done = sem("cmp_scores_done")
        cx_ready = sem("cmp_shifted_ready")
        ce_ready = sem("cmp_exp_ready")
        tc_done = sem("cmp_transposed")
        tc_ready = sem("cmp_transposed_taken")
        ps_ready = sem("probs_scaled")
        pts_ready = sem("pts_ready")
        ptw_ready = sem("ptw_ready")
        pv_done = sem("pv_done")
        comb_ready = sem("combined_ready")
        ot_done = sem("out_transposed")
        oh_ready = sem("att_head_ready")
        ol_ready = sem("att_rest_ready")
        silu_ready = sem("silu_ready")
        uh_ready = sem("uh_ready")
        ul_ready = sem("ul_ready")
        down_taken = sem("down_taken")
        rw_landed = sem("router_landed")
        lg_done = sem("logits_done")
        lg_ready = sem("logits_ready")
        gate_ready = sem("gate_ready")
        b2_landed = sem("block2_landed")
        xc_ready = sem("xc_ready")
        ri_done = sem("ri_done")
        ri_ready = sem("ri_ready")
        ix_ready = sem("ix_ready")
        decay_ready = sem("decay_ready")
        lam_abs = sem("lam_abs_ready")
        lam_exp = sem("lam_exp_ready")
        router_exp = sem("router_exp_ready")
        lru_q = sem("lru_q_ready")
        root_ready = sem("root_ready")
        hr_ready = sem("hr_ready")
        zs_ready = sem("zs_ready")
        u2_ready = sem("u2_ready")
        u2h_ready = sem("u2h_ready")
        u2l_ready = sem("u2l_ready")
        ang_ready = sem("angles_ready")
        tab_ready = sem("tables_ready")
        rot_done = sem("rotation_done")
        rope_ready = sem("rope_ready")
        v2_done = sem("v2_done")
        v2_ready = sem("v2_ready")
        s2_done = sem("scores2_done")
        m2_ready = sem("max2_ready")
        e2_ready = sem("exp2_ready")
        p2_ready = sem("p2_ready")
        t2_done = sem("t2_done")
        pt2_ready = sem("pt2_ready")
        pv2_done = sem("pv2_done")
        y_T = sem("y_transposed")
        y_ready2 = sem("y_tok_ready")
        y_out = sem("y_out")

        block = ctx.enter_context(nc.Block())

        def col(name, k):
            c = WHERE[name] + k
            return par[:, c:c + 1]

        def slab(w, c):
            return w[:, c:c + P].rearrange("(k p) n -> p k n", p=P)

        def taken(eng, n):
            eng.wait_ge(bank_free[n % RING], n // RING + 1)

        def take(ins, n):
            ins.then_inc(bank_free[n % RING], 1)

        @block.sync
        def _(sp):
            def load(n, src, kt=KT):
                if not isinstance(n, int) or n >= RING:
                    sp.wait_ge(weights_split, n - (RING - 1))
                sp.dma_start(raw[slot][:, 0:kt, :], src).then_inc(raw_landed[slot], 16)

            sp.dma_start(cst[:, :], a["consts"]).then_inc(sem_cst, 16)
            sp.dma_start(x_tok[:, :, :], a["x"].rearrange("b (t p) d -> p (b t) d", p=P)).then_inc(sem_x, 16)
            for n in range(N_MOD_1):
                slot = n % RING
                load(n, slab(a["w_mod_2"][0], n * P))
            for l in range(DEPTH):
                w = a["w_in"][l]
                order = [C_KC, C_VC] + [C_Q + P * t for t in range(4)] + [C_GATES, C_KS, C_KW, C_VS, C_VW]
                for t in range(4):
                    order += [C_CG + P * t, C_U + P * t, C_BG + P * t]
                for k, c in enumerate(order):
                    slot = (BASE_MIX[l] + k) % RING
                    load(BASE_MIX[l] + k, slab(w, c))
                for k in range(KT):
                    n = BASE_MIX[l] + N_PROJ + k
                    slot = n % RING
                    load(n, slab(a["w_o"][l], k * P))
                with sp.Fori(0, PARTS[l]) as e:
                    for j in range(N_PART):
                        n = BASE_FFN[l] + e * N_PART + j
                        slot = (BASE_FFN[l] + j) % RING
                        if j < 2 * PT:
                            m = j // 2
                            if l == 0:
                                w = a["ffn_wg" if j % 2 == 0 else "ffn_wu"]
                                src = w[0].rearrange("(k p) n -> p k n", p=P)[:, :, bass.ds(e * D_PART + m * P, P)]
                            else:
                                w = a["moe_wg" if j % 2 == 0 else "moe_wu"]
                                src = w[0, bass.ds(e, 1), :, m * P:(m + 1) * P] \
                                    .rearrange("o (k p) n -> p (o k) n", p=P)
                            load(n, src)
                        else:
                            m = j - 2 * PT
                            if l == 0:
                                src = a["ffn_wd"][0].rearrange("(e k p) n -> e p k n", p=P, k=PT)[
                                    bass.ds(e, 1), :, :, m * P:(m + 1) * P].rearrange("o p k n -> (o p) k n")
                            else:
                                src = a["moe_wd"][0, bass.ds(e, 1), :, m * P:(m + 1) * P] \
                                    .rearrange("o (k p) n -> p (o k) n", p=P)
                            load(n, src, PT)
            for i in range(N_MOD_1, N_MOD):
                slot = mod_place(i) % RING
                load(mod_place(i), slab(a["w_mod_2"][0], i * P))
            w2 = a["w_in_2"][0]
            order = [(w2, k * P) for k in range(2 * KT)]
            order += [(w2, 5 * D + k * P) for k in range(KT)]
            for k in range(KT):
                order += [(w2, 6 * D + k * P), (a["w_out_rnn_2"][0], k * P)]
            for h in range(HEADS):
                order += [(w2, 2 * D + h * P), (w2, 3 * D + h * P), (w2, 4 * D + h * P)]
            for k in range(KT):
                order += [(w2, 7 * D + k * P), (a["w_out_attn_2"][0], k * P)]
            order += [(a["w_o_2"][0], k * P) for k in range(KT)]
            assert len(order) == N_ALL - BASE_2
            for k, (w, c) in enumerate(order):
                slot = (BASE_2 + k) % RING
                load(BASE_2 + k, slab(w, c))
            for t in range(ST):
                sp.wait_ge(y_ready2, 2 * (t + 1))
                sp.dma_start(out[0, t * P:(t + 1) * P, :], y_tok[:, t, :]).then_inc(y_out, 16)
            sp.wait_ge(y_out, 16 * ST)

        @block.gpsimd
        def _(pool):
            def split(n, slot, kt):
                pool.wait_ge(head_done, n + 1)
                pool.tensor_tensor(rest[slot][:, 0:kt, :], raw[slot][:, 0:kt, :], head[slot][:, 0:kt, :],
                                   ALU.subtract).then_inc(weights_split, 1)

            def run(n0, count, kt=KT):
                turns_, left = count // RING, count % RING
                first = 0
                if n0 == 0:
                    for j in range(RING):
                        split(j, j, kt)
                    first = RING
                    turns_ -= 1
                if turns_ > 0:
                    with pool.Fori(0, turns_) as i:
                        for j in range(RING):
                            n = n0 + first + j
                            slot = n % RING
                            split(i * RING + n, slot, kt)
                for j in range(left):
                    n = n0 + first + turns_ * RING + j
                    split(n, n % RING, kt)

            run(0, BASE_FFN[0])
            for l in range(DEPTH):
                with pool.Fori(0, PARTS[l]) as e:
                    for j in range(N_PART):
                        n = BASE_FFN[l] + j
                        slot = n % RING
                        split(e * N_PART + n, slot, KT if j < 2 * PT else PT)
                if l == 0:
                    run(BASE_MIX[1], N_MIX)
            run(BASE_MOD, N_ALL - BASE_MOD)

        @block.tensor
        def _(pe):
            def tile(n, hi, lo, kt=KT, cols=S, use=None, ready=None):
                static = n if isinstance(n, int) else use[0]
                slot = static % RING
                pe.wait_ge(weights_split, n + 1)
                if static >= RING:
                    pe.wait_ge(bank_free[slot], static // RING if isinstance(n, int) else use[1])
                last = None
                for k in range(kt):
                    if ready:
                        ready(k)
                    for w, act, first, final in ((head, hi, True, False), (head, lo, False, False),
                                                 (rest, hi, False, True)):
                        last = pe.matmul(bank[slot][:, 0:cols], w[slot][:, k, :], act[:, k, 0:cols],
                                         start=(k == 0 and first), stop=(k == kt - 1 and final))
                last.then_inc(tile_done, 1)

            def together(n0, hi, lo, ready):
                pe.wait_ge(weights_split, n0 + 2)
                for n in range(n0, n0 + 2):
                    if n >= RING:
                        pe.wait_ge(bank_free[n % RING], n // RING)
                for k in range(KT):
                    ready(k)
                    for n in range(n0, n0 + 2):
                        slot = n % RING
                        for w, act, first, final in ((head, hi, True, False), (head, lo, False, False),
                                                     (rest, hi, False, True)):
                            last = pe.matmul(bank[slot][:, :], w[slot][:, k, :], act[:, k, :],
                                             start=(k == 0 and first), stop=(k == KT - 1 and final))
                        if k == KT - 1:
                            last.then_inc(tile_done, 1)

            def tiles(n0, count, hi, lo, ready=None):
                done = 0
                if ready:
                    together(n0, hi, lo, ready)
                    done = 2
                turns_ = (count - done) // RING
                if turns_ > 1:
                    with pe.Fori(0, turns_) as i:
                        for j in range(RING):
                            n = n0 + done + j
                            tile(i * RING + n, hi, lo, use=(n, i + n // RING))
                    done += turns_ * RING
                for j in range(done, count):
                    tile(n0 + j, hi, lo)

            def mean(L, ready):
                for k in range(KT):
                    ready(k)
                    last = pe.matmul(bank[3][:, :], mean_w[:, :], H[:, k, :], start=(k == 0), stop=(k == KT - 1))
                last.then_inc(mean_done, 1)

            def mean_of_sum(L):
                pe.wait_ge(sum_ready, L)
                pe.matmul(bank[3][:, :], mean_w[:, :], rstd[:, :], start=True, stop=True).then_inc(mean_done, 1)

            def var(L):
                for k in range(KT):
                    pe.wait_ge(sq_ready, KT * L + k + 1)
                    pe.matmul(bank[4][:, :], mean_w[:, :], sq[:, k % 2, :], start=(k == 0),
                              stop=(k == KT - 1)).then_inc(sq_used, 1)

            def mod_tiles(lo, hi):
                for i in range(lo, hi):
                    tile(mod_place(i), c_head, c_rest, cols=2)

            for primed in (s_done, pv_done, pv2_done):
                pe.sem_inc(primed, PRIMED)
            pe.wait_ge(sem_cst, 16)
            pe.wait_ge(sem_stage, 16 * STAGED)
            pe.wait_ge(setup_done, 3)
            for r, rows in enumerate(STAGE_ROWS):
                last = pe.transpose(bank[7][:, r * P:r * P + rows], stage[0:rows, r, :], cst[0:rows, K_ID:K_ID + rows])
            last.then_inc(par_T, 1)
            pe.wait_ge(sem_x, 16)
            for k in range(KT):
                if k >= 2:
                    pe.wait_ge(y_ready, k - 1)
                for t in range(ST):
                    last = pe.transpose(bank[5 + k % 2][:, t * P:(t + 1) * P], x_tok[:, t, k * P:(k + 1) * P], ident)
                last.then_inc(x_T, 1)
            mean(0, lambda k: pe.wait_ge(y_ready, k + 1))
            pe.wait_ge(c_lo, 1)
            mod_tiles(0, N_MOD_1)
            var(0)

            def mixer(l):
                n0 = BASE_MIX[l]
                tiles(n0, M_GATES, HH, HL, ready=lambda k: pe.wait_ge(hl_ready, KT * 2 * l + k + 1))
                pe.wait_ge(w1_landed, 16 * 7 * (l + 1))
                pe.wait_ge(a2_ready, l + 1)
                for kv in range(2):
                    for m in range(2):
                        b = bank[3 + 2 * kv + m]
                        for tp in range(CMP_PAIRS):
                            last = pe.matmul(b[:, 0:3 * NCMP].rearrange("p (g n) -> p g n", g=3),
                                             W1[:, kv, tp, m * P:(m + 1) * P],
                                             A2[:, kv, :, tp:tp + 8 * (NCMP - 1) + 1:8],
                                             start=(tp == 0), stop=(tp == CMP_PAIRS - 1))
                        last.then_inc(hid_done, 1)
                tiles(n0 + M_GATES, 2, HH, HL)
                taken(pe, n0 + M_GATES)
                for t in range(ST):
                    last = pe.transpose(bank[7][:, t * 24:(t + 1) * 24], GT[:, t * P:(t + 1) * P],
                                        cst[0:24, K_ID:K_ID + 24])
                last.then_inc(vg_T, 1)
                pe.wait_ge(vg_ready, 3 * l + 1)
                pe.wait_ge(gelu_ready, 4 * (l + 1))
                for m in range(2):
                    pe.matmul(bank[7][:, 0:2 * NCMP], W2[:, 0, m, :], HG[:, 0, m, :], start=(m == 0), stop=(m == 1))
                for g in range(GROUPS):
                    for m in range(2):
                        last = pe.matmul(bank[7][0:NCMP, 64 + g * HD:64 + (g + 1) * HD],
                                         HG[:, 1, m, g * NCMP:(g + 1) * NCMP], W2[:, 1, m, 0:HD],
                                         start=(m == 0), stop=(m == 1))
                last.then_inc(kcvc_done, 1)
                tiles(n0 + M_KEYS[3], 1, HH, HL)
                compressed_scores(l)
                tiles(n0 + M_V, 2, HH, HL)
                for b in range(2):
                    taken(pe, n0 + M_V + b)
                    for t in range(ST):
                        last = pe.transpose(bank[5 + b][:, t * P:(t + 1) * P], VT[:, b, t * P:(t + 1) * P], ident)
                    last.then_inc(vg_T, 1)
                attention(l)
                pe.wait_ge(mixl_ready, 4 * (l + 1))
                pe.wait_ge(ol_ready, PRIMED + 16 * (l + 1))
                tiles(n0 + N_PROJ, KT, MH, ML)
                mean_of_sum(2 * l + 1)
                var(2 * l + 1)

            def compressed_scores(l):
                pe.wait_ge(kcvc_ready, 2 * (l + 1))
                for t in range(4):
                    taken(pe, BASE_MIX[l] + M_Q + t)
                for h in [0, 2, 4, 6, 1, 3, 5, 7]:
                    rows = slice(HD * (h % 2), HD * (h % 2) + HD)
                    for i in range(ST):
                        c = ((h // 2) * ST + i) * NCMP
                        last = pe.matmul(bank[3 + h % 2][:, c:c + NCMP], Q[rows, h // 2, i * P:(i + 1) * P],
                                         KC[rows, h // 4, :], start=True, stop=True)
                last.then_inc(cs_done, 1)

            def attention(l):
                n0 = BASE_MIX[l] + 11
                pe.wait_ge(vg_ready, 3 * (l + 1))
                pe.wait_ge(cx_ready, 2 * (l + 1))
                pe.wait_ge(dup_s, 64 * (l + 1))

                with pe.Fori(0, 4) as t:
                    g = t // 2
                    u0 = 8 * t + 32 * l

                    def scores(v):
                        i = v // 2
                        w = (i + 1) * P
                        if v == 0:
                            pe.wait_ge(q_ready, t + 4 * l + 1)
                        pe.wait_ge(exp_ready, PRIMED + 2 * (u0 + v))
                        lhs = QC[:, v % 2, i * P:(i + 1) * P]
                        for b, kind in ((3, 2), (4, 3)):
                            pe.matmul(bank[b][:, 0:w], lhs,
                                      K4[:, kind, bass.ds(g, 1), 0:w].rearrange("p o n -> p (o n)"),
                                      start=True, stop=False)
                            last = pe.matmul(bank[b][:, i * P:w], ident, causal, start=False, stop=True)
                        last.then_inc(s_done, 1)

                    def compressed_turn():
                        for r in range(2):
                            for i in range(ST):
                                last = pe.transpose(bank[5 + r][0:NCMP, i * P:(i + 1) * P], Cc[:, r, i, :], ident)
                        last.then_inc(tc_done, 1)

                    def piece(v):
                        for z in range(3 * v, 3 * v + 3):
                            j, k = z // KT, z % KT
                            slot = (n0 + j) % RING
                            if k == 0:
                                pe.wait_ge(weights_split, 3 * t + n0 + j + 1)
                                pe.wait_ge(bank_free[slot], t + (n0 + j) // RING)
                            for w, x in ((head, HH), (head, HL), (rest, HH)):
                                last = pe.matmul(bank[slot][:, :], w[slot][:, k, :], x[:, k, :],
                                                 start=(k == 0 and w is head and x is HH),
                                                 stop=(k == KT - 1 and w is rest))
                            if k == KT - 1:
                                last.then_inc(tile_done, 1)

                    def turn(v):
                        i = v // 2
                        pe.wait_ge(ps_ready, u0 + v + 1)
                        if v == 0:
                            pe.wait_ge(tc_ready, t + 4 * l + 1)
                        else:
                            pe.wait_ge(pts_ready, PRIMED + u0 + v)
                            pe.wait_ge(ptw_ready, u0 + v)
                        for b in range(2):
                            for k in range(i + 1):
                                last = pe.transpose(bank[5 + b][:, k * P:(k + 1) * P],
                                                    Psw[:, v % 2, b, k * P:(k + 1) * P], ident)
                        last.then_inc(t_done, 1)

                    def values(v):
                        i, r = v // 2, v % 2
                        pe.wait_ge(ptw_ready, u0 + v + 1)
                        pe.wait_ge(pts_ready, PRIMED + u0 + v + 1)
                        if v == 0:
                            pe.wait_ge(tc_ready, t + 4 * l + 1)
                        if r == 0:
                            pe.wait_ge(ol_ready, PRIMED + 4 * t + 16 * l + i)
                        o = bank[7][:, r * HD:(r + 1) * HD]
                        for b in range(2):
                            for k in range(i + 1):
                                pe.matmul(o, PTsw[:, v % 2, b, k, :], V[:, b, k, bass.ds(g * HD, HD)],
                                          start=(b == 0 and k == 0), stop=False)
                        pe.matmul(o, PTc[:, ST * r + i, :], VC[:, bass.ds(g, 1), :].rearrange("p o n -> p (o n)"),
                                  start=False, stop=True).then_inc(pv_done, 1)

                    def out_turn(i):
                        pe.wait_ge(comb_ready, 4 * t + 16 * l + i + 1)
                        pe.transpose(bank[7][:, P:2 * P], ot[:, :], ident).then_inc(ot_done, 1)

                    scores(0)
                    compressed_turn()
                    for v in range(8):
                        if v < 7:
                            scores(v + 1)
                        if v >= 3 and v % 2 == 1:
                            out_turn((v - 3) // 2)
                        piece(v)
                        turn(v)
                        if v > 0:
                            values(v - 1)
                    values(7)
                    out_turn(3)

            def ffn(l):
                n0 = BASE_FFN[l]
                L = 2 * l + 1

                def ready(k):
                    pe.wait_ge(hl_ready, KT * L + k + 1)

                if l == 0:
                    tiles(n0, 2 * PT, HH, HL, ready=ready)
                else:
                    tiles(n0, 3, HH, HL, ready=ready)
                    router_logits()
                    tiles(n0 + 3, 2, HH, HL)
                    router_turn()
                    tiles(n0 + 5, 6, HH, HL)
                    router_gates()
                    for j in range(EXPERTS // 2):
                        tiles(n0 + 11 + j, 1, HH, HL)
                        router_broadcast(2 * j)
                        router_broadcast(2 * j + 1)
                    tiles(n0 + 11 + EXPERTS // 2, 2 * PT - 11 - EXPERTS // 2, HH, HL)

                def down(e):
                    for j in range(KT):
                        n = n0 + 2 * PT + j

                        def u_ready(k, j=j):
                            if j == 0:
                                pe.wait_ge(ul_ready, PT * e + PT * l * DENSE_PARTS + k + 1)
                        tile(e * N_PART + n, UH, UL, kt=PT, use=(n, e * (N_PART // RING) + n // RING), ready=u_ready)

                with pe.Fori(0, PARTS[l] - 1) as e:
                    down(e)
                    for j in range(2 * PT):
                        n = n0 + N_PART + j
                        tile(e * N_PART + n, HH, HL, use=(n, e * (N_PART // RING) + n // RING))
                down(PARTS[l] - 1)
                mean_of_sum(L + 1)
                if l == 1:
                    mod_tiles(9, 12)
                var(L + 1)
                if l == 1:
                    mod_tiles(12, 15)

            def router_logits():
                pe.wait_ge(rw_landed, 16)
                for k in range(KT):
                    last = pe.matmul(bank[5][0:EXPERTS, :], rw[:, k, :], H[:, k, :], start=(k == 0), stop=(k == KT - 1))
                last.then_inc(lg_done, 1)

            def router_turn():
                pe.wait_ge(lg_ready, 1)
                for t in range(ST):
                    last = pe.transpose(bank[6][:, t * EXPERTS:(t + 1) * EXPERTS], lgT[:, t * P:(t + 1) * P],
                                        cst[0:EXPERTS, 0:EXPERTS])
                last.then_inc(lg_done, 1)

            def router_gates():
                pe.wait_ge(lg_ready, 3)
                for t in range(ST):
                    last = pe.transpose(bank[5][0:EXPERTS, t * P:(t + 1) * P], ex[:, t, :], ident)
                last.then_inc(lg_done, 1)

            def router_broadcast(e):
                pe.wait_ge(lg_ready, 4)
                if e >= 2:
                    pe.wait_ge(gate_ready, e - 1)
                pe.matmul(bank[6 + e % 2][:, :], cst[0:EXPERTS, e:e + 1].broadcast_to((EXPERTS, P)), lgT[:, :],
                          start=True, stop=True).then_inc(lg_done, 1)

            for l in range(DEPTH):
                mixer(l)
                ffn(l)

            var(5)
            mod_tiles(15, N_MOD)
            pe.wait_ge(b2_landed, 48)

            def lru_gates(k):
                pe.wait_ge(xc_ready, k + 1)
                for b in range(2):
                    if k >= 1:
                        pe.wait_ge(ri_ready, 2 * (k - 1) + b + 1)
                    pe.matmul(bank[5 + b][:, :], WA[:, b, k, :], XC[:, k, :], start=True, stop=True) \
                      .then_inc(ri_done, 1)

            together(B2_X, HH, HL, lambda k: pe.wait_ge(hl_ready, 4 * KT + k + 1))
            lru_gates(0)
            for k in range(2, KT):
                tile(B2_X + k, HH, HL)
                lru_gates(k - 1)
            lru_gates(KT - 1)
            tiles(B2_Z, 2 * KT, HH, HL)
            for k in range(KT):
                tile(B2_RNN + 2 * k, HH, HL)
                pe.wait_ge(u2l_ready, KT)
                tile(B2_RNN + 2 * k + 1, RH, RL)

            def attend(h, last=False):
                def piece(v):
                    for z in range(3 * v, 3 * v + 3) if not last else ():
                        j, k = z // KT, z % KT
                        n = B2_HEAD + 3 + j
                        slot = n % RING
                        if k == 0:
                            pe.wait_ge(weights_split, 3 * h + n + 1)
                            pe.wait_ge(bank_free[slot], h + n // RING)
                        for w, x in ((head, HH), (head, HL), (rest, HH)):
                            ins = pe.matmul(bank[slot][:, :], w[slot][:, k, :], x[:, k, :],
                                            start=(k == 0 and w is head and x is HH),
                                            stop=(k == KT - 1 and w is rest))
                        if k == KT - 1:
                            ins.then_inc(tile_done, 1)

                for j, src in ((0, qh), (1, kh)):
                    pe.wait_ge(bank_free[(B2_HEAD + j) % RING], h + (B2_HEAD + j) // RING + 1)
                    if j == 1:
                        pe.wait_ge(u2_ready, KT + h)
                    pe.matmul(bank[3 + j][:, :], cst[:, K_ROT:K_ROT + P], src[:, :], start=True,
                              stop=True).then_inc(rot_done, 1)
                pe.wait_ge(bank_free[(B2_HEAD + 2) % RING], h + (B2_HEAD + 2) // RING + 1)
                for t in range(ST):
                    ins = pe.transpose(bank[5][:, t * P:(t + 1) * P], vh[:, t * P:(t + 1) * P], ident)
                ins.then_inc(v2_done, 1)
                piece(0)
                pe.wait_ge(rope_ready, 2 * h + 2)

                def scores2(i):
                    w = (i + 1) * P
                    if i >= 2:
                        pe.wait_ge(e2_ready, 4 * h + i - 1)
                    pe.matmul(bank[6 + i % 2][:, 0:w], qh[:, i * P:w], kh[:, 0:w], start=True, stop=False)
                    pe.matmul(bank[6 + i % 2][:, 0:w], ident, cst[:, K_DIL + (3 - i) * P:K_DIL + S], start=False,
                              stop=True).then_inc(s2_done, 1)

                scores2(0)
                pe.wait_ge(v2_ready, h + 1)
                for i in range(ST):
                    if i < ST - 1:
                        scores2(i + 1)
                        piece(2 * i + 1)
                    pe.wait_ge(p2_ready, 4 * h + i + 1)
                    if i >= 1:
                        pe.wait_ge(pt2_ready, 4 * h + i)
                    for k in range(i + 1):
                        ins = pe.transpose(bank[5][:, k * P:(k + 1) * P], P2[:, i % 2, k * P:(k + 1) * P], ident)
                    ins.then_inc(t2_done, 1)
                    piece(min(2 * i + 2, 7))
                    pe.wait_ge(pt2_ready, 4 * h + i + 1)
                    for k in range(i + 1):
                        ins = pe.matmul(bank[4][:, i * P:(i + 1) * P], V2[:, k, :], PT2[:, k, :],
                                        start=(k == 0), stop=(k == i))
                    ins.then_inc(pv2_done, 1)

            tiles(B2_HEAD, 3, HH, HL)
            with pe.Fori(0, HEADS - 1) as h:
                attend(h)
            attend(HEADS - 1, last=True)
            for k in range(KT):
                tile(B2_ATT + 2 * k, HH, HL)
                pe.wait_ge(u2l_ready, 2 * KT)
                tile(B2_ATT + 2 * k + 1, RH, RL)
            pe.wait_ge(u2l_ready, 3 * KT)
            tiles(B2_O, KT, GH, GL)
            var(6)
            for t in range(ST):
                for b in range(2):
                    q = 2 * t + b
                    pe.wait_ge(xn_ready, 7 * KT)
                    if q >= 2:
                        pe.wait_ge(y_ready2, q - 1)
                    for k in range(4):
                        last = pe.transpose(bank[5 + b][:, k * P:(k + 1) * P],
                                            H[:, 4 * b + k, t * P:(t + 1) * P], ident)
                    last.then_inc(y_T, 1)

        @block.scalar
        def _(act):
            lane = Lane(act, act_step)
            for primed in (exp_ready, pts_ready):
                act.sem_inc(primed, PRIMED)
            for name, rows in VECTORS:
                st, row = WHERE[name] // P, WHERE[name] % P
                if name == "b2dup":
                    for l in range(DEPTH):
                        for d in range(2):
                            act.dma_start(stage[row + l:row + l + 1, st, d * HD:(d + 1) * HD],
                                          a["cmp_b2"][l, 0:1, :]).then_inc(sem_stage, 16)
                else:
                    act.dma_start(stage[row:row + rows, st, :], vector_sources(a, name)).then_inc(sem_stage, 16)

            def compression_weights(l):
                for kv in range(2):
                    act.dma_start(W1[:, kv, :, :], a["cmp_w1"][l, kv].rearrange("(k p) n -> p k n", p=P)) \
                       .then_inc(w1_landed, 16)
                    for d in range(2):
                        act.dma_start(W2[:, kv, :, d * HD:(d + 1) * HD],
                                      a["cmp_w2"][l, kv].rearrange("(k p) n -> p k n", p=P)).then_inc(w1_landed, 16)
                act.dma_start(b2row[:, :], a["cmp_b2"][l, 1:2, :].broadcast_to((NCMP, HD))).then_inc(w1_landed, 16)

            def make_head(n, kt=KT, use=None):
                static = n if use is None else use[0]
                slot = static % RING
                landed = 16 * (static // RING + 1) if use is None else use[1]
                act.wait_ge(raw_landed[slot], landed)
                if static >= RING:
                    act.wait_ge(tile_done, n - (RING - 1))
                act.activation(head[slot][:, 0:kt, :], raw[slot][:, 0:kt, :], ACT.Copy).then_inc(head_done, 1)

            def heads_ahead(first, count):
                for n in range(first + 2, first + count + 2):
                    if n < N_ALL:
                        make_head(n)

            def squares(L, ready):
                for k in range(KT):
                    ready(k)
                    if KT * L + k >= 2:
                        act.wait_ge(sq_used, KT * L + k - 1)
                    act.activation(sq[:, k % 2, :], H[:, k, :], ACT.Square).then_inc(sq_ready, 1)

            def root(L, e):
                act.wait_ge(sq_used, KT * (L + 1))
                act.activation(rstd[:, :], bank[4][:, :], ACT.Sqrt, bias=eps[:, e:e + 1]).then_inc(std_ready, 1)

            def layer_norm(L, g, b, row, split_=True, after_centre=None, after_root=None):
                if after_centre:
                    after_centre()
                squares(L, lambda k: act.wait_ge(d_ready, KT * L + k + 1))
                root(L, 0)
                if after_root:
                    after_root()
                for k in range(KT):
                    act.wait_ge(xn_ready, KT * L + k + 1)
                    act.activation(H[:, k, :], H[:, k, :], ACT.Identity, bias=col(b, row + k),
                                   scale=col(g, row + k)).then_inc(h_ready, 1)
                    if split_:
                        act.wait_ge(h_ready, KT * L + k + 1)
                        act.activation(HH[:, k, :], H[:, k, :], ACT.Copy).then_inc(hh_ready, 1)

            make_head(0)
            make_head(1)
            act.wait_ge(par_ready, 3)
            act.wait_ge(setup_done, 3)
            for d in range(2):
                lane.step(act.activation(c_act[:, :, d], par[:, WHERE["c_2"]:WHERE["c_2"] + KT], ACT.Silu))
            lane.settle()
            act.activation(c_head[:, :, :], c_act[:, :, :], ACT.Copy).then_inc(c_hi, 1)
            layer_norm(0, "ln_in_g", "ln_in_b", 0, after_centre=lambda: heads_ahead(0, N_MOD_1))
            for l in range(DEPTH):
                n0 = BASE_MIX[l]
                if l == 1:
                    act.wait_ge(tile_done, BASE_MIX[1])
                compression_weights(l)
                def keys(kind):
                    n = n0 + M_KEYS[kind]
                    heads_ahead(n, 1)
                    act.wait_ge(tile_done, n + 1)
                    lane.step(act.activation(K4[0:64, kind, 0, :], bank[n % RING][0:64, :], ACT.Copy))
                    take(act.activation(K4[64:128, kind, 1, :], bank[n % RING][64:128, :], ACT.Copy), n)
                    lane.settle()
                    taken(act, n)
                    for g in range(GROUPS):
                        rows, other = slice(64 * g, 64 * g + 64), slice(64 - 64 * g, 128 - 64 * g)
                        act.dma_start(K4[other, kind, g, :], K4[rows, kind, g, :]) \
                           .then_inc(dup_c if kind < 2 else dup_s, 16)

                def values(b):
                    n = n0 + M_V + b
                    heads_ahead(n, 1)
                    act.wait_ge(tile_done, n + 1)
                    take(act.activation(VT[:, b, :], bank[n % RING][:, :], ACT.Copy), n)

                keys(0)
                keys(1)
                heads_ahead(n0 + M_Q, 5)
                for kv in range(2):
                    for m in range(2):
                        j = 2 * kv + m
                        act.wait_ge(bsum_ready, 4 * l + j + 1)
                        act.activation(HG[:, kv, m, :], bank[3 + j][:, 0:2 * NCMP], ACT.Gelu_apprx_tanh,
                                       bias=bsum[:, j:j + 1]).then_inc(gelu_ready, 1)
                n = n0 + M_GATES
                act.wait_ge(tile_done, n + 1)
                take(act.activation(GT[:, :], bank[n % RING][0:3 * HEADS, :], ACT.Sigmoid), n)
                keys(2)
                keys(3)
                values(0)
                for b in range(2):
                    act.wait_ge(cx_ready, 2 * l + 2)
                    x = Pcm[:, 4 * b:4 * b + 4, :, :].rearrange("p h i n -> p (h i n)")
                    act.activation(x, x, ACT.Exp, scale=SCALE1).then_inc(ce_ready, 1)
                values(1)
                n0 = BASE_MIX[l] + 11
                with act.Fori(0, 4) as t:
                    u0 = 8 * t + 32 * l

                    def exps(v):
                        w = (v // 2 + 1) * P
                        act.wait_ge(max_ready, u0 + v + 1)
                        if v >= 2:
                            act.wait_ge(t_done, u0 + v - 1)
                        for b in range(2):
                            act.activation(Psw[:, v % 2, b, 0:w], bank[3 + b][:, 0:w], ACT.Exp,
                                           bias=nb[:, v % 2, b:b + 1], scale=SCALE1,
                                           accum_out=Z[:, v % 2, b:b + 1]).then_inc(exp_ready, 1)

                    def head_out(i):
                        act.wait_ge(ot_done, 4 * t + 16 * l + i + 1)
                        act.activation(MH[:, bass.ds(t, 1), i * P:(i + 1) * P].rearrange("p o n -> p (o n)"),
                                       bank[7][:, P:2 * P], ACT.Copy).then_inc(oh_ready, 1)

                    def head_of(j):
                        m = n0 + 2 + j
                        make_head(3 * t + m, use=(m, 16 * t + 16 * (m // RING + 1)))

                    exps(0)
                    for v in range(8):
                        i = v // 2
                        if v < 7:
                            exps(v + 1)
                        if v in (0, 3, 6):
                            head_of(v // 3)
                        if v == 3:
                            act.wait_ge(tile_done, 3 * t + n0 + 1)
                            take(act.activation(t_cg[:, :], bank[n0 % RING][:, :], ACT.Copy), n0)
                        if v >= 3 and v % 2 == 1:
                            head_out((v - 3) // 2)
                        act.wait_ge(t_done, u0 + v + 1)
                        act.wait_ge(pv_done, u0 + v - 1 + PRIMED)
                        act.activation(PTsw[:, v % 2, 0, 0:i + 1, :], bank[5][:, 0:(i + 1) * P]
                                       .rearrange("p (k q) -> p k q", q=P), ACT.Copy).then_inc(pts_ready, 1)
                    head_out(3)
                    act.wait_ge(bank_free[(n0 + 2) % RING], t + (n0 + 2) // RING + 1)
                    act.activation(MH[:, bass.ds(t + 4, 1), :].rearrange("p o n -> p (o n)"), cy[:, :],
                                   ACT.Copy).then_inc(mixh_ready, 1)
                heads_ahead(BASE_MIX[l] + N_PROJ, KT)
                layer_norm(2 * l + 1, "ln1_g", "ln1_b", KT * l)
                if l == 1:
                    act.dma_start(rw[:, :, :], a["moe_router"][0].rearrange("(k p) e -> p k e", p=P)) \
                       .then_inc(rw_landed, 16)
                n0 = BASE_FFN[l]

                def ahead(e, j):
                    m = n0 + j + 2
                    make_head(e * N_PART + m, PT if 2 * PT <= j + 2 < N_PART else KT,
                              use=(m, 16 * (N_PART // RING) * e + 16 * (m // RING + 1)))

                def gate_up(e, after=None):
                    for j in range(PT):
                        n = n0 + 2 * j
                        ahead(e, 2 * j)
                        act.wait_ge(tile_done, e * N_PART + n + 1)
                        take(act.activation(silu_g[:, j % 2, :], bank[n % RING][:, :], ACT.Silu), n)
                        ahead(e, 2 * j + 1)
                        act.wait_ge(bank_free[(n + 1) % RING], e * (N_PART // RING) + (n + 1) // RING + 1)
                        act.activation(UH[:, j, :], gu[:, j % 2, :], ACT.Copy).then_inc(uh_ready, 1)
                        if after:
                            after(j)

                def router_softmax(j):
                    if j == 4:
                        act.wait_ge(lg_ready, 2)
                        act.activation(ex[:, :, :], lg[:, :, :], ACT.Exp).then_inc(router_exp, 1)

                gate_up(0, router_softmax if l == 1 else None)
                with act.Fori(0, PARTS[l] - 1) as e:
                    for j in range(2 * PT, N_PART):
                        ahead(e, j)
                    gate_up(e + 1)
                for j in range(2 * PT, N_PART):
                    ahead(PARTS[l] - 1, j)
                if l == 0:
                    layer_norm(2, "ln2_g", "ln2_b", 0)
                else:
                    layer_norm(4, "ln2_g", "ln2_b", KT, split_=False, after_centre=lambda: heads_ahead(BASE_MOD, 3),
                               after_root=lambda: heads_ahead(BASE_MOD + 3, 3))

            squares(5, lambda k: act.wait_ge(h_ready, KT * 4 + k + 1))
            act.dma_start(WA[:, 0, :, :], a["w_a_2"][0].rearrange("k p n -> p k n")).then_inc(b2_landed, 16)
            act.dma_start(WA[:, 1, :, :], a["w_x_2"][0].rearrange("k p n -> p k n")).then_inc(b2_landed, 16)
            act.dma_start(posi[:, :], a["positions_2"].broadcast_to((P, S))).then_inc(b2_landed, 16)
            heads_ahead(BASE_MOD + 6, 1)
            root(5, 1)
            heads_ahead(BASE_MOD + 7, 2)
            for k in range(KT):
                act.wait_ge(xn_ready, 5 * KT + k + 1)
                act.activation(HH[:, k, :], t2[:, k % 2, :], ACT.Identity, bias=mod[:, k:k + 1],
                               scale=modg[:, k:k + 1]).then_inc(hh_ready, 1)
            heads_ahead(BASE_MOD + 9, 6)
            act.wait_ge(lam_abs, 1)
            act.activation(lamc[:, 1, :], lamc[:, 0, :], ACT.Exp, scale=-1.0).then_inc(lam_exp, 1)
            for j, o in enumerate((sinT, cosT)):
                act.wait_ge(ang_ready, j + 1)
                act.activation(o[:, :], o[:, :], ACT.Sin).then_inc(tab_ready, 1)

            def conv_in(k):
                n = B2_X + k
                heads_ahead(n, 1)
                act.wait_ge(tile_done, n + 1)
                if k >= 1:
                    act.wait_ge(xc_ready, k)
                take(act.activation(xpad[:, 3:3 + S], bank[n % RING][:, :], ACT.Copy), n)

            conv_in(0)
            for k in range(KT):
                if k + 1 < KT:
                    conv_in(k + 1)
                for b, (o, bias) in enumerate(((R, "b_a_2"), (IX, "b_x_2"))):
                    act.wait_ge(ri_done, 2 * k + b + 1)
                    act.activation(o[:, k, :], bank[5 + b][:, :], ACT.Sigmoid, bias=col(bias, k)) \
                       .then_inc(ri_ready, 1)
            def silu_z(k):
                n = B2_Z + k
                heads_ahead(n, 1)
                act.wait_ge(tile_done, n + 1)
                take(act.activation(ZS[:, k, :], bank[n % RING][:, :], ACT.Silu), n)

            for k in range(KT):
                act.wait_ge(ix_ready, k + 1)
                act.activation(XC[:, k, :], R[:, k, :], ACT.Exp, scale=lamc[:, 6, k:k + 1]).then_inc(decay_ready, 1)
                if k >= 2:
                    act.wait_ge(lru_q, k - 1)
                act.activation(lt[:, k % 2, :], R[:, k, :], ACT.Tanh, scale=lamc[:, 7, k:k + 1]) \
                   .then_inc(decay_ready, 1)
            for k in range(KT // 2):
                silu_z(k)
            for k in range(KT):
                act.wait_ge(lru_q, k + 1)
                act.activation(R[:, k, :], R[:, k, :], ACT.Sqrt).then_inc(root_ready, 1)
            for k in range(KT // 2, KT):
                silu_z(k)
            for k in range(KT):
                n = B2_ZA + k
                heads_ahead(n, 1)
                act.wait_ge(tile_done, n + 1)
                act.wait_ge(hr_ready, k + 1)
                take(act.activation(XC[:, k, :], bank[n % RING][:, :], ACT.Silu), n)
                act.wait_ge(u2_ready, k + 1)
                act.activation(RH[:, k, :], t2[:, k % 2, :], ACT.Copy).then_inc(u2h_ready, 1)
            act.wait_ge(u2l_ready, KT)
            for k in range(KT):
                n = B2_RNN + 2 * k
                heads_ahead(n, 1)
                act.wait_ge(tile_done, n + 1)
                if k >= 2:
                    taken(act, n + 1 - 4)
                take(act.activation(t2[:, k % 2, :], bank[n % RING][:, :], ACT.Sigmoid, bias=col("b_gate_2", k)), n)
                heads_ahead(n + 1, 1)
            make_head(B2_HEAD + 2)

            def attend(h, last=False):
                for j, o in enumerate((qh, kh, vh)):
                    n = B2_HEAD + j
                    act.wait_ge(tile_done, h * 3 + n + 1)
                    take(act.activation(o[:, :], bank[n % RING][:, :], ACT.Copy), n)
                for j in range(2 if last else 3):
                    n = B2_HEAD + 3 + j
                    make_head(h * 3 + n, use=(n, 16 * h + 16 * (n // RING + 1)))

                def turned(i):
                    act.wait_ge(t2_done, 4 * h + i + 1)
                    act.wait_ge(pv2_done, PRIMED + 4 * h + i)
                    act.activation(PT2[:, 0:i + 1, :], bank[5][:, 0:(i + 1) * P].rearrange("p (k q) -> p k q", q=P),
                                   ACT.Copy).then_inc(pt2_ready, 1)

                for i in range(ST):
                    w = (i + 1) * P
                    act.wait_ge(m2_ready, 4 * h + i + 1)
                    if i >= 2:
                        act.wait_ge(t2_done, 4 * h + i - 1)
                    act.activation(P2[:, i % 2, 0:w], bank[6 + i % 2][:, 0:w], ACT.Exp, bias=n2[:, i % 2:i % 2 + 1],
                                   scale=SCALE2, accum_out=z2[:, i % 2:i % 2 + 1]).then_inc(e2_ready, 1)
                    if i >= 1:
                        turned(i - 1)
                turned(ST - 1)
                act.wait_ge(u2_ready, h + KT + 1)
                act.activation(RH[:, bass.ds(h, 1), :].rearrange("p o n -> p (o n)"), oz[:, :], ACT.Copy) \
                   .then_inc(u2h_ready, 1)

            with act.Fori(0, HEADS - 1) as h:
                attend(h)
            attend(HEADS - 1, last=True)
            for k in range(KT):
                n = B2_ATT + 2 * k
                heads_ahead(n, 1)
                act.wait_ge(tile_done, n + 1)
                if k >= 2:
                    taken(act, n + 1 - 4)
                take(act.activation(t2[:, k % 2, :], bank[n % RING][:, :], ACT.Sigmoid, bias=col("b_gate_2", KT + k)),
                     n)
                heads_ahead(n + 1, 1)
                act.wait_ge(u2_ready, 2 * KT + k + 1)
                act.activation(GH[:, k, :], P2[:, k % 2, :], ACT.Copy).then_inc(u2h_ready, 1)
            heads_ahead(B2_O, KT)
            squares(6, lambda k: taken(act, B2_O + k))
            root(6, 1)
            for q in range(2 * ST):
                t, b = q // 2, q % 2
                act.wait_ge(y_T, q + 1)
                act.activation(y_tok[:, t, b * S:(b + 1) * S], bank[5 + b][:, :], ACT.Copy).then_inc(y_ready2, 1)

        @block.vector
        def _(dve):
            lane = Lane(dve, vec_step)

            def step(ins):
                lane.step(ins)
                lane.settle()

            for primed in (ol_ready, down_taken):
                dve.sem_inc(primed, PRIMED)
            dve.memset(mean_w[:, :], 1.0 / D).then_inc(setup_done, 1)
            dve.memset(eps[:, 0:1], LN_EPS).then_inc(setup_done, 1)
            dve.memset(eps[:, 1:2], RMS_EPS).then_inc(setup_done, 1)
            dve.wait_ge(par_T, 1)
            for r, rows in enumerate(STAGE_ROWS):
                dve.tensor_copy(par[:, r * P:r * P + rows], bank[7][:, r * P:r * P + rows]).then_inc(par_ready, 1)
            dve.wait_ge(c_hi, 1)
            dve.tensor_tensor(c_rest[:, :, :], c_act[:, :, :], c_head[:, :, :], ALU.subtract).then_inc(c_lo, 1)
            for k in range(KT):
                dve.wait_ge(x_T, k + 1)
                dve.tensor_copy(H[:, k, :], bank[5 + k % 2][:, :]).then_inc(y_ready, 1)

            def summed(k):
                if k == 0:
                    return
                ins = dve.tensor_tensor(rstd[:, :], H[:, 0, :] if k == 1 else rstd[:, :], H[:, k, :], ALU.add)
                if k == KT - 1:
                    ins.then_inc(sum_ready, 1)
                else:
                    step(ins)

            def mod_taken(lo, hi):
                for i in range(lo, hi):
                    n = mod_place(i)
                    dve.wait_ge(tile_done, n + 1)
                    take(dve.tensor_tensor(mod[:, i:i + 1], bank[n % RING][:, 0:1], col("b_mod_2", i), ALU.add), n)

            def centre(L):
                dve.wait_ge(mean_done, L + 1)
                for k in range(KT):
                    dve.tensor_tensor(H[:, k, :], H[:, k, :], bank[3][:, :], ALU.subtract).then_inc(d_ready, 1)

            def invert(L):
                dve.wait_ge(std_ready, L + 1)
                dve.reciprocal(rstd[:, :], rstd[:, :]).then_inc(rs_ready, 1)
                dve.wait_ge(rs_ready, L + 1)

            def layer_norm(L, split_=True, between=None):
                centre(L)
                if between:
                    between()
                invert(L)
                for k in range(KT + 2):
                    if k < KT:
                        dve.tensor_tensor(H[:, k, :], H[:, k, :], rstd[:, :], ALU.mult).then_inc(xn_ready, 1)
                    if split_ and k >= 2:
                        dve.wait_ge(hh_ready, KT * L + k - 1)
                        dve.tensor_tensor(HL[:, k - 2, :], H[:, k - 2, :], HH[:, k - 2, :], ALU.subtract) \
                           .then_inc(hl_ready, 1)

            layer_norm(0, between=lambda: mod_taken(0, N_MOD_1))

            def mixer(l):
                n0 = BASE_MIX[l]
                if l == 1:
                    dve.wait_ge(tile_done, BASE_MIX[1])
                step(dve.memset(A2[:, :, 2, :], 0.0))
                for kv in range(2):
                    c = WHERE["cmp_pos"] + (2 * l + kv) * CMP_PAIRS
                    step(dve.tensor_copy(A2[:, kv, 2, 0:CMP_PAIRS], par[:, c:c + CMP_PAIRS]))
                dve.wait_ge(dup_c, 64 * (l + 1))
                for kv in range(2):
                    for q in range(2):
                        rows = slice(64 * q, 64 * q + 64)
                        ins = dve.tensor_copy(A2[rows, kv, 0:2, :], K4[rows, kv, :, q:S:2])
                        if kv == 1 and q == 1:
                            ins.then_inc(a2_ready, 1)
                        else:
                            step(ins)
                for t in range(4):
                    n = n0 + M_Q + t
                    dve.wait_ge(tile_done, n + 1)
                    take(dve.tensor_copy(Q[:, t, :], bank[n % RING][:, :]), n)
                for j in range(4):
                    dve.wait_ge(hid_done, 4 * l + j + 1)
                    dve.tensor_tensor(bsum[:, j:j + 1], bank[3 + j][:, 2 * NCMP:2 * NCMP + 1],
                                      col("cmp_b1", 4 * l + j), ALU.add).then_inc(bsum_ready, 1)
                dve.wait_ge(vg_T, 3 * l + 1)
                dve.tensor_copy(GA[:, :, :, :], bank[7][:, 0:ST * 24].rearrange("p (t b h) -> p t b h", b=3, h=HEADS)) \
                   .then_inc(vg_ready, 1)
                dve.wait_ge(vg_ready, 3 * l + 1)
                step(dve.tensor_scalar(GA[:, 0, 0, :], GA[:, 0, 0, :], cst[:, K_VALID:K_VALID + 1], None, ALU.mult))
                dve.wait_ge(kcvc_done, l + 1)
                dve.tensor_scalar(KC[:, :, :], bank[7][:, 0:2 * NCMP].rearrange("p (g n) -> p g n", g=2),
                                  col("b2dup", l), None, ALU.add).then_inc(kcvc_ready, 1)
                dve.tensor_tensor(VC[:, :, :], bank[7][0:NCMP, 64:64 + 2 * HD].rearrange("p (g d) -> p g d", g=2),
                                  b2row[:, :].unsqueeze(1).broadcast_to((NCMP, 2, HD)), ALU.add) \
                   .then_inc(kcvc_ready, 1)
                dve.wait_ge(gelu_ready, 4 * (l + 1))
                dve.wait_ge(kcvc_ready, 2 * (l + 1))
                attention(l)
                for k in range(KT):
                    n = n0 + N_PROJ + k
                    dve.wait_ge(tile_done, n + 1)
                    take(dve.scalar_tensor_tensor(out=H[:, k, :], in0=H[:, k, :], scalar=ALPHA,
                                                  in1=bank[n % RING][:, :], op0=ALU.mult, op1=ALU.add), n)
                    if k >= 1:
                        taken(dve, n - 1)
                        summed(k - 1)
                taken(dve, n0 + N_PROJ + KT - 1)
                summed(KT - 1)

            def attention(l):
                n0 = BASE_MIX[l] + 11
                dve.wait_ge(cs_done, l + 1)
                mask = cst[:, K_CMP:K_CMP + ST * NCMP].rearrange("p (i n) -> p i n", n=NCMP)
                for b in range(2):
                    hs = slice(b, HEADS, 2)
                    step(dve.tensor_tensor(Pcm[:, hs, :, :], bank[3 + b][:, 0:4 * ST * NCMP]
                                           .rearrange("p (h i n) -> p h i n", h=4, n=NCMP),
                                           mask.unsqueeze(1).broadcast_to((P, 4, ST, NCMP)), ALU.add))
                    step(dve.tensor_reduce(mxc[:, hs, :], Pcm[:, hs, :, :], AX.X, ALU.max))
                    dve.tensor_tensor(Pcm[:, hs, :, :], Pcm[:, hs, :, :],
                                      mxc[:, hs, :].unsqueeze(3).broadcast_to((P, 4, ST, NCMP)), ALU.subtract) \
                       .then_inc(cx_ready, 1)
                for b in range(2):
                    hs = slice(4 * b, 4 * b + 4)
                    dve.wait_ge(ce_ready, 2 * l + b + 1)
                    step(dve.tensor_reduce(mxc[:, hs, :], Pcm[:, hs, :, :], AX.X, ALU.add))
                    step(dve.reciprocal(mxc[:, hs, :], mxc[:, hs, :]))
                    step(dve.tensor_tensor(mxc[:, hs, :], mxc[:, hs, :],
                                           GA[:, :, 0, hs].rearrange("p i h -> p h i"), ALU.mult))
                    step(dve.tensor_tensor(Pcm[:, hs, :, :], Pcm[:, hs, :, :],
                                           mxc[:, hs, :].unsqueeze(3).broadcast_to((P, 4, ST, NCMP)), ALU.mult))
                for b in range(2):
                    dve.wait_ge(vg_T, 3 * l + b + 2)
                    dve.tensor_copy(V[:, b, :, :], bank[5 + b][:, :].rearrange("p (t n) -> p t n", n=P)) \
                       .then_inc(vg_ready, 1)
                step(dve.memset(QC[64:128, 0, :], 0.0))
                step(dve.memset(QC[0:64, 1, :], 0.0))
                step(dve.memset(zpad[:, 0:2], 0.0))
                with lane.loop(4, 2 + 1 + 8 * (2 + 2) + 3) as t:
                    u0 = 8 * t + 32 * l
                    dve.wait_ge(s_done, PRIMED + u0)
                    lane.step(dve.tensor_copy(QC[0:64, 0, :], Q[0:64, bass.ds(t, 1), :].rearrange("p o n -> p (o n)")))
                    lane.step(dve.tensor_copy(Cc[:, :, :, :].rearrange("p r i n -> p r (i n)"),
                                              Pcm[:, bass.ds(2 * t, 2), :, :].rearrange("p r i n -> p r (i n)")))
                    dve.tensor_copy(QC[64:128, 1, :], Q[64:128, bass.ds(t, 1), :].rearrange("p o n -> p (o n)")) \
                       .then_inc(q_ready, 1)

                    def maxima(v):
                        w = (v // 2 + 1) * P
                        dve.wait_ge(s_done, PRIMED + u0 + v + 1)
                        for b in range(2):
                            lane.step(dve.tensor_reduce(mx[:, b:b + 1], bank[3 + b][:, 0:w], AX.X, ALU.max))
                        lane.settle()
                        dve.tensor_scalar(nb[:, v % 2, :], mx[:, :], -SCALE1, None, ALU.mult).then_inc(max_ready, 1)

                    def rest_out(i):
                        dve.wait_ge(oh_ready, 4 * t + 16 * l + i + 1)
                        dve.tensor_tensor(ML[:, bass.ds(t, 1), i * P:(i + 1) * P].rearrange("p o n -> p (o n)"),
                                          bank[7][:, P:2 * P],
                                          MH[:, bass.ds(t, 1), i * P:(i + 1) * P].rearrange("p o n -> p (o n)"),
                                          ALU.subtract).then_inc(ol_ready, 1)

                    def pair_out(v):
                        dve.wait_ge(pv_done, PRIMED + u0 + v + 1)
                        dve.tensor_copy(ot[:, :], bank[7][:, 0:P]).then_inc(comb_ready, 1)

                    maxima(0)
                    dve.wait_ge(tc_done, t + 4 * l + 1)
                    lane.step(dve.tensor_copy(PTc[:, 0:ST, :], bank[5][0:NCMP, :].rearrange("p (i q) -> p i q", q=P)))
                    dve.tensor_copy(PTc[:, ST:2 * ST, :], bank[6][0:NCMP, :].rearrange("p (i q) -> p i q", q=P)) \
                       .then_inc(tc_ready, 1)
                    for v in range(8):
                        i, r = v // 2, v % 2
                        w = (i + 1) * P
                        dve.wait_ge(exp_ready, PRIMED + 2 * (u0 + v + 1))
                        step(dve.reciprocal(rz[:, :], Z[:, r, :]))
                        step(dve.tensor_tensor(fac[:, :], rz[:, :],
                                               GA[:, i, 1:3, bass.ds(2 * t + r, 1)].rearrange("p b o -> p (b o)"),
                                               ALU.mult))
                        for b in range(2):
                            ins = dve.tensor_scalar(Psw[:, r, b, 0:w], Psw[:, r, b, 0:w], fac[:, b:b + 1], None,
                                                    ALU.mult)
                        ins.then_inc(ps_ready, 1)
                        if v < 7:
                            maxima(v + 1)
                        if v >= 3 and r == 1:
                            rest_out((v - 3) // 2)
                        dve.wait_ge(t_done, u0 + v + 1)
                        dve.wait_ge(pv_done, u0 + v - 1 + PRIMED)
                        dve.tensor_copy(PTsw[:, r, 1, 0:i + 1, :], bank[6][:, 0:(i + 1) * P]
                                        .rearrange("p (k q) -> p k q", q=P)).then_inc(ptw_ready, 1)
                        if r == 0 and v > 0:
                            pair_out(v - 1)
                        if v == 6:
                            convolve(t, l)
                    pair_out(7)
                    dve.wait_ge(tile_done, 3 * t + n0 + 3)
                    take(dve.tensor_tensor(cy[:, :], cy[:, :], bank[(n0 + 2) % RING][:, :], ALU.mult), n0 + 2)
                    rest_out(3)
                    dve.wait_ge(mixh_ready, 4 * l + t + 1)
                    dve.tensor_tensor(ML[:, bass.ds(t + 4, 1), :].rearrange("p o n -> p (o n)"), cy[:, :],
                                      MH[:, bass.ds(t + 4, 1), :].rearrange("p o n -> p (o n)"), ALU.subtract) \
                       .then_inc(mixl_ready, 1)

            def convolve(t, l):
                n0 = BASE_MIX[l] + 11
                dve.wait_ge(bank_free[n0 % RING], t + n0 // RING + 1)
                dve.wait_ge(tile_done, 3 * t + n0 + 2)
                take(dve.tensor_tensor(zpad[:, 2:2 + S], t_cg[:, :], bank[(n0 + 1) % RING][:, :], ALU.mult), n0 + 1)
                dve.wait_ge(bank_free[(n0 + 1) % RING], t + (n0 + 1) // RING + 1)
                w = [par[:, bass.ds(t + (WHERE["conv_w"] + 12 * l + 4 * i), 1)] for i in range(3)]
                step(dve.tensor_scalar(cy[:, :], zpad[:, 0:S], w[0], None, ALU.mult))
                for i in (1, 2):
                    step(dve.scalar_tensor_tensor(out=cy[:, :], in0=zpad[:, i:i + S], scalar=w[i],
                                                  in1=cy[:, :], op0=ALU.mult, op1=ALU.add))

            def router_compare(t):
                rows = slice(t * EXPERTS, (t + 1) * EXPERTS)
                other = lg[:, t, :].unsqueeze(1).broadcast_to((P, EXPERTS, EXPERTS))
                own = lg[:, t, :].unsqueeze(2).broadcast_to((P, EXPERTS, EXPERTS))
                step(dve.tensor_tensor(gt8[:, rows, :], other, own, ALU.is_gt))
                step(dve.tensor_tensor(eq8[:, rows, :], other, own, ALU.is_equal))
                step(dve.tensor_tensor(eq8[:, rows, :], eq8[:, rows, :],
                                       cst[:, K_PAIR:K_ALL].rearrange("p (e j) -> p e j", j=EXPERTS), ALU.mult))

            def router(j):
                if j == 0:
                    dve.wait_ge(lg_done, 1)
                    dve.tensor_copy(lgT[:, :], bank[5][0:EXPERTS, :]).then_inc(lg_ready, 1)
                elif j == 1:
                    dve.wait_ge(lg_done, 2)
                    step(dve.tensor_copy(lg[:, :, :], bank[6][:, 0:ST * EXPERTS]
                                         .rearrange("p (t e) -> p t e", e=EXPERTS)))
                    step(dve.tensor_reduce(top[:, :], lg[:, :, :], AX.X, ALU.max))
                    router_compare(0)
                elif j == 2:
                    router_compare(1)
                    router_compare(2)
                elif j == 3:
                    router_compare(3)
                    step(dve.tensor_tensor(gt8[:, :, :], gt8[:, :, :], eq8[:, :, :], ALU.add))
                    step(dve.tensor_reduce(sel[:, :, :].rearrange("p t e -> p (t e)"), gt8[:, :, :], AX.X, ALU.add))
                    step(dve.tensor_scalar(sel[:, :, :], sel[:, :, :], 2.0, None, ALU.is_lt))
                    dve.tensor_tensor(lg[:, :, :], lg[:, :, :], top[:, :].unsqueeze(2).broadcast_to((P, ST, EXPERTS)),
                                      ALU.subtract).then_inc(lg_ready, 1)
                elif j == 4:
                    dve.wait_ge(router_exp, 1)
                    step(dve.tensor_tensor(ex[:, :, :], ex[:, :, :], sel[:, :, :], ALU.mult))
                    step(dve.tensor_reduce(top[:, :], ex[:, :, :], AX.X, ALU.add))
                    step(dve.reciprocal(top[:, :], top[:, :]))
                    dve.tensor_tensor(ex[:, :, :], ex[:, :, :], top[:, :].unsqueeze(2).broadcast_to((P, ST, EXPERTS)),
                                      ALU.mult).then_inc(lg_ready, 1)
                elif j == 5:
                    dve.wait_ge(lg_done, 3)
                    dve.tensor_copy(lgT[:, :], bank[5][0:EXPERTS, :]).then_inc(lg_ready, 1)
                gates = {5: (0, 1), 6: (2, 3, 4, 5), 7: (6, 7)}
                for e in gates.get(j, ()):
                    dve.wait_ge(lg_done, 4 + e)
                    dve.tensor_copy(GB[:, e, :], bank[6 + e % 2][:, :]).then_inc(gate_ready, 1)

            def ffn(l):
                n0 = BASE_FFN[l]
                q0 = PT * DENSE_PARTS * l

                def gate_up(e, after=None):
                    for j in range(PT):
                        n = n0 + 2 * j
                        q = PT * e + q0
                        dve.wait_ge(bank_free[n % RING], e * (N_PART // RING) + n // RING + 1)
                        dve.wait_ge(tile_done, e * N_PART + n + 2)
                        if j >= 2:
                            dve.wait_ge(ul_ready, q + j - 1)
                        take(dve.tensor_tensor(gu[:, j % 2, :], silu_g[:, j % 2, :], bank[(n + 1) % RING][:, :],
                                               ALU.mult), n + 1)
                        dve.wait_ge(uh_ready, q + j + 1)
                        dve.tensor_tensor(UL[:, j, :], gu[:, j % 2, :], UH[:, j, :], ALU.subtract) \
                           .then_inc(ul_ready, 1)
                        if after:
                            after(j)

                def down(e, last=False):
                    for k in range(KT):
                        n = n0 + 2 * PT + k
                        turn = e * (N_PART // RING)
                        dve.wait_ge(tile_done, e * N_PART + n + 1)
                        if l == 0:
                            take(dve.tensor_tensor(H[:, k, :], H[:, k, :], bank[n % RING][:, :], ALU.add), n)
                            if last and k >= 1:
                                taken(dve, BASE_MIX[1] - KT + k - 1)
                                summed(k - 1)
                        else:
                            if k < 2:
                                dve.wait_ge(ul_ready, PT * e + q0 + PT)
                            dve.wait_ge(down_taken, PRIMED + e * KT + max(k - 1, 0))
                            gate = GB[:, e, :] if last else GB[:, bass.ds(e, 1), :].rearrange("p o n -> p (o n)")
                            take(dve.tensor_tensor(gu[:, k % 2, :], bank[n % RING][:, :], gate, ALU.mult), n)
                            dve.wait_ge(bank_free[n % RING], turn + n // RING + 1)
                            dve.tensor_tensor(H[:, k, :], H[:, k, :], gu[:, k % 2, :], ALU.add) \
                               .then_inc(down_taken, 1)
                            if last and k >= 1:
                                dve.wait_ge(down_taken, PRIMED + e * KT + k)
                                summed(k - 1)
                    if last:
                        if l == 0:
                            taken(dve, BASE_MIX[1] - 1)
                        else:
                            dve.wait_ge(down_taken, PRIMED + EXPERTS * KT)
                        summed(KT - 1)

                def first_part(j):
                    if l == 1:
                        router(j)
                    if j == 1:
                        for k in range(KT):
                            lane.step(dve.tensor_scalar(H[:, k, :], H[:, k, :], ALPHA, None, ALU.mult))
                        lane.settle()

                gate_up(0, first_part)
                with dve.Fori(0, PARTS[l] - 1) as e:
                    down(e)
                    gate_up(e + 1)
                down(PARTS[l] - 1, last=True)

            for l in range(DEPTH):
                mixer(l)
                layer_norm(2 * l + 1)
                ffn(l)
                layer_norm(2 * l + 2, split_=(l == 0), between=(lambda: mod_taken(9, 12)) if l == 1 else None)

            lam = par[:, WHERE["lam_2"]:WHERE["lam_2"] + KT]
            L8 = [lamc[:, j, :] for j in range(8)]
            step(dve.tensor_scalar(L8[2], lam, -1.0, None, ALU.mult))
            dve.tensor_tensor(L8[0], lam, L8[2], ALU.max).then_inc(lam_abs, 1)
            mod_taken(12, 15)
            invert(5)
            mod_taken(15, 18)
            dve.wait_ge(h_ready, 5 * KT)
            for i in range(2 * KT - RING, 2 * KT):
                taken(dve, mod_place(i))
            step(dve.scalar_tensor_tensor(out=modg[:, :], in0=mod[:, KT:2 * KT], scalar=1.0,
                                          in1=par[:, WHERE["g_norm_2"]:WHERE["g_norm_2"] + KT],
                                          op0=ALU.add, op1=ALU.mult))
            for k in range(KT):
                if k >= 2:
                    dve.wait_ge(hh_ready, 4 * KT + k - 1)
                dve.tensor_tensor(t2[:, k % 2, :], H[:, k, :], rstd[:, :], ALU.mult).then_inc(xn_ready, 1)
                dve.wait_ge(xn_ready, 5 * KT + k + 1)
                step(dve.tensor_scalar(IX[:, k, :], t2[:, k % 2, :], modg[:, k:k + 1], mod[:, k:k + 1],
                                       ALU.mult, ALU.add))
                dve.wait_ge(hh_ready, 4 * KT + k + 1)
                dve.tensor_tensor(HL[:, k, :], IX[:, k, :], HH[:, k, :], ALU.subtract).then_inc(hl_ready, 1)
            mod_taken(18, N_MOD)
            dve.wait_ge(lam_exp, 1)
            step(dve.tensor_scalar(L8[3], L8[1], 2.0, None, ALU.add))
            step(dve.reciprocal(L8[3], L8[3]))
            step(dve.tensor_tensor(L8[4], L8[1], L8[3], ALU.mult))
            step(dve.tensor_tensor(L8[5], L8[4], L8[4], ALU.mult))
            step(dve.tensor_scalar(L8[6], L8[5], 1.0 / 17, None, ALU.mult))
            for odd in (15, 13, 11, 9, 7, 5, 3):
                step(dve.scalar_tensor_tensor(out=L8[6], in0=L8[6], scalar=1.0 / odd, in1=L8[5],
                                              op0=ALU.add, op1=ALU.mult))
            step(dve.scalar_tensor_tensor(out=L8[6], in0=L8[6], scalar=1.0, in1=L8[4], op0=ALU.add, op1=ALU.mult))
            step(dve.tensor_scalar(L8[2], L8[2], 0.0, None, ALU.max))
            step(dve.scalar_tensor_tensor(out=L8[7], in0=L8[6], scalar=2.0, in1=L8[2], op0=ALU.mult, op1=ALU.add))
            step(dve.tensor_scalar(L8[6], L8[7], -8.0, None, ALU.mult))
            step(dve.tensor_scalar(L8[7], L8[7], 8.0, None, ALU.mult))
            dve.wait_ge(b2_landed, 48)
            step(dve.tensor_scalar(keep[:, :], posi[:, :], 0, None, ALU.not_equal))
            step(dve.tensor_scalar(drop[:, :], posi[:, :], 0, None, ALU.is_equal))
            step(dve.tensor_scalar(ang[:, :], posi[0:ROT, :], cst[0:ROT, K_FREQ:K_FREQ + 1], None, ALU.mult))
            two_pi = [6.28125, 0.0019350051879882812, 2 * np.pi - 6.28125 - 0.0019350051879882812]
            for o, quarter in ((sinT, 0.0), (cosT, np.pi / 2)):
                step(dve.tensor_scalar(turns[:, :], ang[:, :], quarter, 1 / (2 * np.pi), ALU.add, ALU.mult))
                step(dve.tensor_copy(turnf[:, :], turns[:, :]))
                step(dve.scalar_tensor_tensor(out=o[:, :], in0=turnf[:, :], scalar=-two_pi[0], in1=ang[:, :],
                                              op0=ALU.mult, op1=ALU.add))
                for part in two_pi[1:]:
                    step(dve.scalar_tensor_tensor(out=o[:, :], in0=turnf[:, :], scalar=-part, in1=o[:, :],
                                                  op0=ALU.mult, op1=ALU.add))
                step(dve.tensor_scalar(o[:, :], o[:, :], quarter, None, ALU.add))
                dve.tensor_scalar(o[:, :], o[:, :], 3.1415925, -3.1415925, ALU.min, ALU.max).then_inc(ang_ready, 1)

            step(dve.memset(xpad[:, 0:3], 0.0))

            def gated(k):
                dve.wait_ge(ri_ready, 2 * k + 2)
                dve.tensor_tensor(IX[:, k, :], IX[:, k, :], XC[:, k, :], ALU.mult).then_inc(ix_ready, 1)

            for k in range(KT):
                taken(dve, B2_X + k)
                w = [col("conv_w_2", KT * i + k) for i in range(4)]
                step(dve.tensor_scalar(XC[:, k, :], xpad[:, 0:S], w[0], col("conv_b_2", k), ALU.mult, ALU.add))
                for i in (1, 2, 3):
                    ins = dve.scalar_tensor_tensor(out=XC[:, k, :], in0=xpad[:, i:i + S], scalar=w[i],
                                                   in1=XC[:, k, :], op0=ALU.mult, op1=ALU.add)
                    if i < 3:
                        step(ins)
                ins.then_inc(xc_ready, 1)
                if k >= 1:
                    gated(k - 1)
            gated(KT - 1)
            for k in range(KT):
                dve.wait_ge(decay_ready, 2 * k + 2)
                step(dve.tensor_tensor(la2[:, :], XC[:, k, :], XC[:, k, :], ALU.mult))
                dve.scalar_tensor_tensor(out=R[:, k, :], in0=la2[:, :], scalar=1.0, in1=lt[:, k % 2, :],
                                         op0=ALU.add, op1=ALU.mult).then_inc(lru_q, 1)
                dve.wait_ge(lru_q, k + 1)
                step(dve.tensor_tensor(XC[:, k, :], XC[:, k, :], keep[:, :], ALU.mult))

            def gated_state(k):
                taken(dve, B2_Z + k)
                if k >= 2:
                    dve.wait_ge(u2l_ready, k - 1)
                dve.tensor_tensor(t2[:, k % 2, :], R[:, k, :], ZS[:, k, :], ALU.mult).then_inc(u2_ready, 1)
                dve.wait_ge(u2h_ready, k + 1)
                dve.tensor_tensor(RL[:, k, :], t2[:, k % 2, :], RH[:, k, :], ALU.subtract).then_inc(u2l_ready, 1)

            for k in range(KT):
                dve.wait_ge(root_ready, k + 1)
                step(dve.tensor_tensor(R[:, k, :], R[:, k, :], keep[:, :], ALU.mult))
                step(dve.tensor_tensor(R[:, k, :], R[:, k, :], drop[:, :], ALU.add))
                step(dve.tensor_tensor(IX[:, k, :], IX[:, k, :], R[:, k, :], ALU.mult))
                dve.tensor_tensor_scan(out=R[:, k, :], data0=XC[:, k, :], data1=IX[:, k, :], initial=0.0,
                                       op0=ALU.mult, op1=ALU.add).then_inc(hr_ready, 1)
                dve.wait_ge(hr_ready, k + 1)
                if k >= 1:
                    gated_state(k - 1)
            gated_state(KT - 1)
            for k in range(KT):
                n = B2_RNN + 2 * k
                taken(dve, n)
                dve.wait_ge(tile_done, n + 2)
                take(dve.tensor_tensor(M[:, k, :], t2[:, k % 2, :], bank[(n + 1) % RING][:, :], ALU.mult), n + 1)
            taken(dve, B2_RNN + 2 * KT - 1)
            with lane.loop(HEADS, 2 * 2 + 2 * ST) as h:
                for j, x in enumerate((qh, kh)):
                    dve.wait_ge(rot_done, 2 * h + j + 1)
                    lane.step(dve.tensor_tensor(t2[0:ROT, 0, :], bank[3 + j][0:ROT, :], sinT[:, :], ALU.mult))
                    lane.step(dve.tensor_tensor(t2[0:ROT, 1, :], x[0:ROT, :], cosT[:, :], ALU.mult))
                    lane.settle()
                    dve.tensor_tensor(x[0:ROT, :], t2[0:ROT, 0, :], t2[0:ROT, 1, :], ALU.add).then_inc(rope_ready, 1)
                    dve.wait_ge(rope_ready, 2 * h + j + 1)
                dve.wait_ge(v2_done, h + 1)
                dve.tensor_copy(V2[:, :, :], bank[5][:, :].rearrange("p (t n) -> p t n", n=P)).then_inc(v2_ready, 1)

                def maxima2(i):
                    w = (i + 1) * P
                    dve.wait_ge(s2_done, 4 * h + i + 1)
                    step(dve.tensor_reduce(m2[:, i % 2:i % 2 + 1], bank[6 + i % 2][:, 0:w], AX.X, ALU.max))
                    dve.tensor_scalar(n2[:, i % 2:i % 2 + 1], m2[:, i % 2:i % 2 + 1], -SCALE2, None, ALU.mult) \
                       .then_inc(m2_ready, 1)

                maxima2(0)
                for i in range(ST):
                    w = (i + 1) * P
                    if i < ST - 1:
                        maxima2(i + 1)
                    dve.wait_ge(e2_ready, 4 * h + i + 1)
                    step(dve.reciprocal(r2[:, i % 2:i % 2 + 1], z2[:, i % 2:i % 2 + 1]))
                    dve.tensor_scalar(P2[:, i % 2, 0:w], P2[:, i % 2, 0:w], r2[:, i % 2:i % 2 + 1], None, ALU.mult) \
                       .then_inc(p2_ready, 1)
                dve.wait_ge(pv2_done, PRIMED + 4 * h + ST)
                dve.wait_ge(u2l_ready, h + KT)
                dve.tensor_tensor(oz[:, :], bank[4][:, :], XC[:, bass.ds(h, 1), :].rearrange("p o n -> p (o n)"),
                                  ALU.mult).then_inc(u2_ready, 1)
                dve.wait_ge(u2h_ready, h + KT + 1)
                dve.tensor_tensor(RL[:, bass.ds(h, 1), :].rearrange("p o n -> p (o n)"), oz[:, :],
                                  RH[:, bass.ds(h, 1), :].rearrange("p o n -> p (o n)"), ALU.subtract) \
                   .then_inc(u2l_ready, 1)
            for k in range(KT):
                n = B2_ATT + 2 * k
                taken(dve, n)
                dve.wait_ge(tile_done, n + 2)
                if k >= 2:
                    dve.wait_ge(u2l_ready, 2 * KT + k - 1)
                take(dve.tensor_tensor(P2[:, k % 2, :], t2[:, k % 2, :], bank[(n + 1) % RING][:, :], ALU.mult), n + 1)
                taken(dve, n + 1)
                dve.tensor_tensor(P2[:, k % 2, :], P2[:, k % 2, :], M[:, k, :], ALU.add).then_inc(u2_ready, 1)
                dve.wait_ge(u2h_ready, 2 * KT + k + 1)
                dve.tensor_tensor(GL[:, k, :], P2[:, k % 2, :], GH[:, k, :], ALU.subtract).then_inc(u2l_ready, 1)
            for k in range(KT):
                n = B2_O + k
                dve.wait_ge(tile_done, n + 1)
                take(dve.scalar_tensor_tensor(out=H[:, k, :], in0=bank[n % RING][:, :],
                                              scalar=mod[:, 2 * KT + k:2 * KT + k + 1], in1=H[:, k, :],
                                              op0=ALU.mult, op1=ALU.add), n)
            invert(6)
            for k in range(KT):
                dve.scalar_tensor_tensor(out=H[:, k, :], in0=H[:, k, :], scalar=col("g_final_2", k), in1=rstd[:, :],
                                         op0=ALU.mult, op1=ALU.mult).then_inc(xn_ready, 1)


_INS = ["x", "ln_in_g", "ln_in_b", "w_in", "cmp_pos", "cmp_w1", "cmp_b1", "cmp_w2", "cmp_b2", "conv_w", "w_o",
        "ln1_g", "ln1_b", "ln2_g", "ln2_b", "ffn_wg", "ffn_wu", "ffn_wd", "moe_router", "moe_wg", "moe_wu",
        "moe_wd", "c_2", "positions_2", "g_norm_2", "w_mod_2", "b_mod_2", "w_in_2", "b_gate_2", "conv_w_2",
        "conv_b_2", "w_a_2", "b_a_2", "w_x_2", "b_x_2", "lam_2", "w_out_rnn_2", "w_out_attn_2", "w_o_2",
        "g_final_2"]


def kernel(**inputs):
    import concourse.bacc as _bacc
    from concourse.bass_utils import run_bass_kernel_spmd as _run

    nc = _bacc.Bacc("TRN2", target_bir_lowering=False, num_devices=1)
    arrays, args = {}, {}
    for name in _INS + ["consts"]:
        v = constant_table() if name == "consts" else np.ascontiguousarray(inputs[name])
        arrays[f"in_{name}_dram"] = v
        args[name] = nc.dram_tensor(f"in_{name}_dram", v.shape, mybir.dt.from_np(v.dtype),
                                    kind="ExternalInput").ap()
    out = nc.dram_tensor("out_0_dram", (1, S, D), F32, kind="ExternalOutput").ap()
    build(nc, args, out)
    r = _run(nc, [arrays], core_ids=[0])
    return r.results[0]["out_0_dram"]
```
